# Optimizing a Trainium2 kernel written in Bass

```python
import math
import jax, jax.numpy as jnp
from jax import lax
import numpy as np

D_MODEL = 2048
BATCH = 1
SEQ = 256
DEPTH = 2

HEAD_DIM = 128
N_HEADS_A = D_MODEL // HEAD_DIM
N_KV_A = 4
ROT_DIM = HEAD_DIM // 4
IDX_HEADS = 16
IDX_DIM = 64
IDX_ROT = IDX_DIM // 4
TOPK_MAX = 256
N_HEADS_B = D_MODEL // HEAD_DIM
N_KV_B = 4
BLOCK_Q = 128
PLE_DIM = 256
ROPE_THETA = 500000.0
LN_EPS = 1e-5
N_A_LAYERS = DEPTH // 2
N_B_LAYERS = DEPTH - N_A_LAYERS
ALPHA = (2.0 * DEPTH) ** 0.25
BETA = (8.0 * DEPTH) ** -0.25

WIDTH_A = N_HEADS_A * HEAD_DIM
KVW_A = N_KV_A * HEAD_DIM
SPLITS_A = tuple(int(c) for c in np.cumsum([WIDTH_A, KVW_A, KVW_A, WIDTH_A, IDX_HEADS * IDX_DIM, IDX_DIM]))
COLS_A = WIDTH_A + 2 * KVW_A + WIDTH_A + IDX_HEADS * IDX_DIM + IDX_DIM + IDX_HEADS
WIDTH_B = N_HEADS_B * HEAD_DIM
KVW_B = N_KV_B * HEAD_DIM


def layer_norm(x, g, b):
    xf = x.astype(jnp.float32)
    mu = jnp.mean(xf, axis=-1, keepdims=True)
    var = jnp.mean(jnp.square(xf - mu), axis=-1, keepdims=True)
    y = (xf - mu) * lax.rsqrt(var + LN_EPS) * g.astype(jnp.float32) + b.astype(jnp.float32)
    return y.astype(x.dtype)

def partial_rope(x, positions, rot_dim):
    half = rot_dim // 2
    inv = 1.0 / (ROPE_THETA ** (jnp.arange(half, dtype=jnp.float32) / half))
    ang = positions.astype(jnp.float32)[..., None] * inv
    cos = jnp.cos(ang)[:, :, None, :]
    sin = jnp.sin(ang)[:, :, None, :]
    xr = x[..., :rot_dim].astype(jnp.float32)
    x1, x2 = xr[..., :half], xr[..., half:]
    rot = jnp.concatenate([x1 * cos - x2 * sin, x1 * sin + x2 * cos], axis=-1)
    return jnp.concatenate([rot.astype(x.dtype), x[..., rot_dim:]], axis=-1)

def to_blocks(a):
    b, s = a.shape[0], a.shape[1]
    return jnp.swapaxes(a.reshape((b, s // BLOCK_Q, BLOCK_Q) + a.shape[2:]), 0, 1)

def from_blocks(a):
    a = jnp.swapaxes(a, 0, 1)
    return a.reshape((a.shape[0], a.shape[1] * a.shape[2]) + a.shape[3:])

def mixer_a(x, w_in, w_o, positions):
    b, s, _ = x.shape
    proj = x @ w_in
    q, k, v, gate, iq, ik, iw = jnp.split(proj, SPLITS_A, axis=-1)
    q = partial_rope(q.reshape(b, s, N_HEADS_A, HEAD_DIM), positions, ROT_DIM)
    k = partial_rope(k.reshape(b, s, N_KV_A, HEAD_DIM), positions, ROT_DIM)
    v = v.reshape(b, s, N_KV_A, HEAD_DIM)
    iq = partial_rope(iq.reshape(b, s, IDX_HEADS, IDX_DIM), positions, IDX_ROT)
    ik = partial_rope(ik.reshape(b, s, 1, IDX_DIM), positions, IDX_ROT)[:, :, 0, :]
    n_sel = min(TOPK_MAX, s // 4)
    groups = N_HEADS_A // N_KV_A
    key_pos = jnp.arange(s, dtype=jnp.int32)
    idx_scale = (IDX_DIM ** -0.5) * (IDX_HEADS ** -0.5)
    starts = jnp.arange(s // BLOCK_Q, dtype=jnp.int32) * BLOCK_Q

    def block_fn(args):
        qb, iqb, iwb, start = args
        t = start + jnp.arange(BLOCK_Q, dtype=jnp.int32)
        dots = jnp.einsum('bqhd,bsd->bqhs', iqb, ik).astype(jnp.float32)
        iscore = jnp.einsum('bqhs,bqh->bqs', jax.nn.relu(dots), iwb.astype(jnp.float32)) * idx_scale
        causal = key_pos[None, :] <= t[:, None]
        iscore = jnp.where(causal[None], iscore, -jnp.inf)
        _, idx = lax.top_k(iscore, n_sel)
        ksel = jax.vmap(lambda kk, ii: kk[ii])(k, idx)
        vsel = jax.vmap(lambda vv, ii: vv[ii])(v, idx)
        qg = qb.reshape(b, BLOCK_Q, N_KV_A, groups, HEAD_DIM)
        logits = jnp.einsum('bqngd,bqknd->bqngk', qg, ksel).astype(jnp.float32) * (HEAD_DIM ** -0.5)
        valid = idx <= t[None, :, None]
        logits = jnp.where(valid[:, :, None, None, :], logits, -jnp.inf)
        wts = jax.nn.softmax(logits, axis=-1).astype(v.dtype)
        o = jnp.einsum('bqngk,bqknd->bqngd', wts, vsel)
        return o.reshape(b, BLOCK_Q, WIDTH_A)

    o = from_blocks(lax.map(block_fn, (to_blocks(q), to_blocks(iq), to_blocks(iw), starts)))
    return (o * jax.nn.silu(gate)) @ w_o

def shared_kv(x, w_kv):
    b, s, _ = x.shape
    k, v = jnp.split(x @ w_kv, [KVW_B], axis=-1)
    return k.reshape(b, s, N_KV_B, HEAD_DIM), v.reshape(b, s, N_KV_B, HEAD_DIM)

def mixer_b(x, w_in, w_o, k, v):
    b, s, _ = x.shape
    q, gate = jnp.split(x @ w_in, [WIDTH_B], axis=-1)
    q = q.reshape(b, s, N_HEADS_B, HEAD_DIM)
    groups = N_HEADS_B // N_KV_B
    key_pos = jnp.arange(s, dtype=jnp.int32)
    starts = jnp.arange(s // BLOCK_Q, dtype=jnp.int32) * BLOCK_Q

    def block_fn(args):
        qb, start = args
        t = start + jnp.arange(BLOCK_Q, dtype=jnp.int32)
        qg = qb.reshape(b, BLOCK_Q, N_KV_B, groups, HEAD_DIM)
        z = jnp.einsum('bqngd,bsnd->bngqs', qg, k).astype(jnp.float32) * (HEAD_DIM ** -0.5)
        strict = key_pos[None, :] < t[:, None]
        log_om = jnp.where(strict, -jax.nn.softplus(z), 0.0)
        suffix = lax.cumsum(log_om, axis=log_om.ndim - 1, reverse=True) - log_om
        a = jnp.where(strict, jnp.exp(jax.nn.log_sigmoid(z) + suffix), 0.0)
        o = jnp.einsum('bngqs,bsnd->bqngd', a.astype(v.dtype), v)
        return o.reshape(b, BLOCK_Q, WIDTH_B)

    o = from_blocks(lax.map(block_fn, (to_blocks(q), starts)))
    return (o * jax.nn.silu(gate)) @ w_o

def per_layer_embed(x, p_i, w_p, w_g):
    return (p_i @ w_p) * jax.nn.sigmoid(x @ w_g)

def first_inputs(seed: int = 0) -> dict:
    key = jax.random.key(seed)
    ks = jax.random.split(key, 12)
    nrm = jax.random.normal
    x = nrm(ks[0], (BATCH, SEQ, D_MODEL), jnp.float32)
    p = nrm(ks[1], (DEPTH, BATCH, SEQ, PLE_DIM), jnp.float32)
    positions = jnp.broadcast_to(jnp.arange(SEQ, dtype=jnp.int32)[None, :], (BATCH, SEQ))
    w_in_a = nrm(ks[2], (N_A_LAYERS, D_MODEL, COLS_A), jnp.float32) * D_MODEL ** -0.5
    w_o_a = nrm(ks[3], (N_A_LAYERS, WIDTH_A, D_MODEL), jnp.float32) * (WIDTH_A ** -0.5 * BETA)
    w_kv_b = nrm(ks[4], (D_MODEL, 2 * KVW_B), jnp.float32) * D_MODEL ** -0.5
    w_in_b = nrm(ks[5], (N_B_LAYERS, D_MODEL, 2 * WIDTH_B), jnp.float32) * D_MODEL ** -0.5
    w_o_b = nrm(ks[6], (N_B_LAYERS, WIDTH_B, D_MODEL), jnp.float32) * (WIDTH_B ** -0.5 * BETA)
    ln_g = 1.0 + 0.02 * nrm(ks[7], (DEPTH, D_MODEL), jnp.float32)
    ln_b = 0.02 * nrm(ks[8], (DEPTH, D_MODEL), jnp.float32)
    w_ple = nrm(ks[9], (DEPTH, PLE_DIM, D_MODEL), jnp.float32) * PLE_DIM ** -0.5
    w_ple_gate = nrm(ks[10], (DEPTH, D_MODEL, D_MODEL), jnp.float32) * D_MODEL ** -0.5
    return {"x": x, "p": p, "positions": positions, "w_in_a": w_in_a, "w_o_a": w_o_a,
            "w_kv_b": w_kv_b, "w_in_b": w_in_b, "w_o_b": w_o_b, "ln_g": ln_g, "ln_b": ln_b,
            "w_ple": w_ple, "w_ple_gate": w_ple_gate}

def first_block(x, p, positions, w_in_a, w_o_a, w_kv_b, w_in_b, w_o_b, ln_g, ln_b, w_ple, w_ple_gate):
    k_sh, v_sh = None, None
    for i in range(DEPTH):
        if i < N_A_LAYERS:
            h = mixer_a(x, w_in_a[i], w_o_a[i], positions)
        else:
            if i == N_A_LAYERS:
                k_sh, v_sh = shared_kv(x, w_kv_b)
            j = i - N_A_LAYERS
            h = mixer_b(x, w_in_b[j], w_o_b[j], k_sh, v_sh)
        x = layer_norm(ALPHA * x + h, ln_g[i], ln_b[i])
        x = x + per_layer_embed(x, p[i], w_ple[i], w_ple_gate[i])
    return x


DEPTH_2 = 1

MIX_WIDTH = D_MODEL
MLA_WIDTH = D_MODEL // 2
HGRN_WIDTH = MIX_WIDTH - MLA_WIDTH
MLA_HEADS = 8
MLA_V_DIM = MLA_WIDTH // MLA_HEADS
MLA_NOPE_DIM = 128
MLA_ROPE_DIM = 64
MLA_Q_RANK = D_MODEL // 4
MLA_KV_RANK = D_MODEL // 8
ROPE_BASE = 10000.0
Q_BLOCK = 128
HGRN_HEADS = 8
HGRN_KEY_DIM = 128
HGRN_VAL_DIM = HGRN_WIDTH // HGRN_HEADS
HGRN_QK_WIDTH = HGRN_HEADS * HGRN_KEY_DIM
HGRN_CHUNK = 64
D_FF = 4 * D_MODEL
NORM_EPS = 1e-6
N_MOD = 6
IN_WIDTH = MLA_Q_RANK + MLA_KV_RANK + MLA_ROPE_DIM + 3 * HGRN_QK_WIDTH + 2 * HGRN_WIDTH


def _in_proj_offsets():
    widths = (MLA_Q_RANK, MLA_KV_RANK, MLA_ROPE_DIM, HGRN_QK_WIDTH, HGRN_QK_WIDTH,
              HGRN_QK_WIDTH, HGRN_WIDTH, HGRN_WIDTH)
    return [int(o) for o in np.cumsum(widths)[:-1]]

def _rmsnorm(x, g):
    xf = x.astype(jnp.float32)
    y = xf * lax.rsqrt(jnp.mean(xf * xf, axis=-1, keepdims=True) + NORM_EPS)
    return (y * g.astype(jnp.float32)).astype(x.dtype)

def _rope_angles(positions):
    half = MLA_ROPE_DIM // 2
    inv_freq = ROPE_BASE ** (-jnp.arange(half, dtype=jnp.float32) / half)
    ang = positions.astype(jnp.float32)[..., None] * inv_freq
    return jnp.cos(ang), jnp.sin(ang)

def _apply_rope(x, cos, sin):
    x1, x2 = jnp.split(x.astype(jnp.float32), 2, axis=-1)
    return jnp.concatenate([x1 * cos - x2 * sin, x1 * sin + x2 * cos], axis=-1).astype(x.dtype)

def _mla(q_lat, kv_lat, k_rope, cos, sin, q_norm_g, kv_norm_g, w_uq, w_ukv):
    B, S, _ = q_lat.shape
    H = MLA_HEADS
    q = (_rmsnorm(q_lat, q_norm_g) @ w_uq).reshape(B, S, H, MLA_NOPE_DIM + MLA_ROPE_DIM)
    q_nope = q[..., :MLA_NOPE_DIM]
    q_rope = _apply_rope(q[..., MLA_NOPE_DIM:], cos[:, :, None, :], sin[:, :, None, :])
    kv = (_rmsnorm(kv_lat, kv_norm_g) @ w_ukv).reshape(B, S, H, MLA_NOPE_DIM + MLA_V_DIM)
    k_nope, v = kv[..., :MLA_NOPE_DIM], kv[..., MLA_NOPE_DIM:]
    k_rope = _apply_rope(k_rope, cos, sin)
    scale = (MLA_NOPE_DIM + MLA_ROPE_DIM) ** -0.5
    nb = S // Q_BLOCK

    def to_blocks(t):
        return t.reshape(B, nb, Q_BLOCK, *t.shape[2:]).swapaxes(0, 1)

    def attend(blk):
        qn, qr = blk
        s = (jnp.einsum('bqhd,bkhd->bhqk', qn, k_nope)
             + jnp.einsum('bqhr,bkr->bhqk', qr, k_rope))
        p = jax.nn.softmax(s.astype(jnp.float32) * scale, axis=-1).astype(v.dtype)
        return jnp.einsum('bhqk,bkhd->bqhd', p, v)

    o = lax.map(attend, (to_blocks(q_nope), to_blocks(q_rope)))
    return o.swapaxes(0, 1).reshape(B, S, H * MLA_V_DIM)

def _gla_chunkwise(q, k, v, log_f):
    B, S, H, Dk = q.shape
    Dv = v.shape[-1]
    n = S // HGRN_CHUNK

    def to_chunks(t):
        return t.reshape(B, n, HGRN_CHUNK, H, t.shape[-1]).transpose(1, 0, 3, 2, 4)

    qc, kc, vc = to_chunks(q), to_chunks(k), to_chunks(v)
    bc = jnp.cumsum(to_chunks(log_f), axis=3)
    mask = jnp.tril(jnp.ones((HGRN_CHUNK, HGRN_CHUNK), dtype=bool))[None, None, :, :, None]

    def step(state, inp):
        q_, k_, v_, b_ = inp
        rel = jnp.where(mask, b_[:, :, :, None, :] - b_[:, :, None, :, :], -jnp.inf)
        a = jnp.einsum('bhtd,bhsd,bhtsd->bhts', q_, k_, jnp.exp(rel))
        o = (jnp.einsum('bhts,bhse->bhte', a, v_)
             + jnp.einsum('bhtd,bhde->bhte', q_ * jnp.exp(b_), state))
        b_last = b_[:, :, -1:, :]
        state = (state * jnp.exp(b_last)[:, :, 0, :, None]
                 + jnp.einsum('bhsd,bhse->bhde', k_ * jnp.exp(b_last - b_), v_))
        return state, o

    state0 = jnp.zeros((B, H, Dk, Dv), jnp.float32)
    _, o = lax.scan(step, state0, (qc, kc, vc, bc))
    return o.transpose(1, 0, 3, 2, 4).reshape(B, S, H, Dv)

def _hgrn2_direction(q, f_logit, v, lb):
    f = lb + (1.0 - lb) * jax.nn.sigmoid(f_logit.astype(jnp.float32))
    return _gla_chunkwise(q.astype(jnp.float32), 1.0 - f, v.astype(jnp.float32), jnp.log(f))

def _lower_bound(lb_logits, layer):
    p = jax.nn.softmax(lb_logits.astype(jnp.float32), axis=0)
    return jnp.cumsum(p, axis=0)[layer].reshape(HGRN_HEADS, HGRN_KEY_DIM)

def _hgrn2_bidir(hq, f_fwd, f_bwd, hi, hg, lb_fwd, lb_bwd, norm_g):
    B, S, _ = hq.shape
    q = hq.reshape(B, S, HGRN_HEADS, HGRN_KEY_DIM)
    ff = f_fwd.reshape(B, S, HGRN_HEADS, HGRN_KEY_DIM)
    fb = f_bwd.reshape(B, S, HGRN_HEADS, HGRN_KEY_DIM)
    v = hi.reshape(B, S, HGRN_HEADS, HGRN_VAL_DIM)
    o_fwd = _hgrn2_direction(q, ff, v, lb_fwd)
    o_bwd = jnp.flip(_hgrn2_direction(jnp.flip(q, 1), jnp.flip(fb, 1), jnp.flip(v, 1), lb_bwd), 1)
    o = _rmsnorm(o_fwd + o_bwd, norm_g).reshape(B, S, HGRN_WIDTH)
    return (o * jax.nn.silu(hg.astype(jnp.float32))).astype(hq.dtype)

def second_inputs(seed: int = 0) -> dict:
    key = jax.random.key(seed)
    ks = jax.random.split(key, 24)
    f32 = jnp.float32

    def nrm(k, shape, fan_in, s=1.0):
        return jax.random.normal(k, shape, f32) * (s * fan_in ** -0.5)

    def gain(k, shape):
        return 1.0 + 0.05 * jax.random.normal(k, shape, f32)

    offs = jax.random.randint(ks[2], (BATCH, 1), 0, 1024, dtype=jnp.int32)
    positions = (jnp.arange(SEQ, dtype=jnp.int32)[None, :] + offs).astype(jnp.int32)
    return {
        "x": jax.random.normal(ks[0], (BATCH, SEQ, D_MODEL), f32),
        "c": jax.random.normal(ks[1], (BATCH, D_MODEL), f32),
        "positions": positions,
        "w_mod": nrm(ks[3], (DEPTH_2, D_MODEL, N_MOD * D_MODEL), D_MODEL, 0.5),
        "b_mod": 0.01 * jax.random.normal(ks[4], (DEPTH_2, N_MOD * D_MODEL), f32),
        "pre_mix_g": gain(ks[5], (DEPTH_2, D_MODEL)),
        "post_mix_g": gain(ks[6], (DEPTH_2, D_MODEL)),
        "pre_mlp_g": gain(ks[7], (DEPTH_2, D_MODEL)),
        "post_mlp_g": gain(ks[8], (DEPTH_2, D_MODEL)),
        "w_in": nrm(ks[9], (DEPTH_2, D_MODEL, IN_WIDTH), D_MODEL),
        "q_norm_g": gain(ks[10], (DEPTH_2, MLA_Q_RANK)),
        "kv_norm_g": gain(ks[11], (DEPTH_2, MLA_KV_RANK)),
        "w_uq": nrm(ks[12], (DEPTH_2, MLA_Q_RANK, MLA_HEADS * (MLA_NOPE_DIM + MLA_ROPE_DIM)), MLA_Q_RANK),
        "w_ukv": nrm(ks[13], (DEPTH_2, MLA_KV_RANK, MLA_HEADS * (MLA_NOPE_DIM + MLA_V_DIM)), MLA_KV_RANK),
        "hgrn_norm_g": gain(ks[14], (DEPTH_2, HGRN_VAL_DIM)),
        "hgrn_lb_logits_fwd": 0.1 * jax.random.normal(ks[15], (DEPTH_2 + 1, HGRN_QK_WIDTH), f32),
        "hgrn_lb_logits_bwd": 0.1 * jax.random.normal(ks[16], (DEPTH_2 + 1, HGRN_QK_WIDTH), f32),
        "w_out": nrm(ks[17], (DEPTH_2, MIX_WIDTH, D_MODEL), MIX_WIDTH),
        "w_up": nrm(ks[18], (DEPTH_2, D_MODEL, D_FF), D_MODEL),
        "w_down": nrm(ks[19], (DEPTH_2, D_FF, D_MODEL), D_FF),
    }

def second_block(x, c, positions, w_mod, b_mod, pre_mix_g, post_mix_g, pre_mlp_g, post_mlp_g,
              w_in, q_norm_g, kv_norm_g, w_uq, w_ukv, hgrn_norm_g, hgrn_lb_logits_fwd,
              hgrn_lb_logits_bwd, w_out, w_up, w_down):
    cos, sin = _rope_angles(positions)
    cond = jax.nn.silu(c)
    offsets = _in_proj_offsets()
    for layer in range(DEPTH_2):
        mod = (cond @ w_mod[layer] + b_mod[layer]).astype(x.dtype)
        shift_a, scale_a, gate_a, shift_m, scale_m, gate_m = [
            m[:, None, :] for m in jnp.split(mod, N_MOD, axis=-1)]

        h = _rmsnorm(x, pre_mix_g[layer]) * (1.0 + scale_a) + shift_a
        proj = h @ w_in[layer]
        q_lat, kv_lat, k_rope, hq, f_fwd, f_bwd, hi, hg = jnp.split(proj, offsets, axis=-1)
        attn_out = _mla(q_lat, kv_lat, k_rope, cos, sin, q_norm_g[layer], kv_norm_g[layer],
                        w_uq[layer], w_ukv[layer])
        rec_out = _hgrn2_bidir(hq, f_fwd, f_bwd, hi, hg,
                               _lower_bound(hgrn_lb_logits_fwd, layer),
                               _lower_bound(hgrn_lb_logits_bwd, layer), hgrn_norm_g[layer])
        mix = jnp.concatenate([attn_out, rec_out], axis=-1) @ w_out[layer]
        x = x + gate_a * _rmsnorm(mix, post_mix_g[layer])

        h = _rmsnorm(x, pre_mlp_g[layer]) * (1.0 + scale_m) + shift_m
        y = jnp.square(jax.nn.relu(h @ w_up[layer])) @ w_down[layer]
        x = x + gate_m * _rmsnorm(y, post_mlp_g[layer])
    return x


def setup_inputs(seed=0):
    out = dict(first_inputs(seed))
    for name, value in second_inputs(seed + 1).items():
        if name != "x":
            out[name + "_2"] = value
    return out


def reference(
    x, p, positions, w_in_a, w_o_a, w_kv_b, w_in_b, w_o_b, ln_g, ln_b, w_ple, w_ple_gate, c_2,
    positions_2, w_mod_2, b_mod_2, pre_mix_g_2, post_mix_g_2, pre_mlp_g_2, post_mlp_g_2, w_in_2,
    q_norm_g_2, kv_norm_g_2, w_uq_2, w_ukv_2, hgrn_norm_g_2, hgrn_lb_logits_fwd_2,
    hgrn_lb_logits_bwd_2, w_out_2, w_up_2, w_down_2,
):
    x = first_block(
        x, p, positions, w_in_a, w_o_a, w_kv_b, w_in_b, w_o_b, ln_g, ln_b, w_ple, w_ple_gate,
    )
    return second_block(
        x, c_2, positions_2, w_mod_2, b_mod_2, pre_mix_g_2, post_mix_g_2, pre_mlp_g_2,
        post_mlp_g_2, w_in_2, q_norm_g_2, kv_norm_g_2, w_uq_2, w_ukv_2, hgrn_norm_g_2,
        hgrn_lb_logits_fwd_2, hgrn_lb_logits_bwd_2, w_out_2, w_up_2, w_down_2,
    )


_drawn_inputs = setup_inputs


def setup_inputs(seed=0):
    import zlib

    import numpy as np

    out = dict(_drawn_inputs(seed))
    spreads = {}
    factors = {'b_mod_2': 3.718,
     'post_mix_g_2': 4.153,
     'pre_mlp_g_2': 4.052,
     'post_mlp_g_2': 4.531,
     'q_norm_g_2': 8.0,
     'kv_norm_g_2': 8.0,
     'hgrn_norm_g_2': 18.612,
     'hgrn_lb_logits_fwd_2': 4.75,
     'hgrn_lb_logits_bwd_2': 4.359}
    for name, (base, spread) in spreads.items():
        noise = np.random.default_rng([zlib.crc32(name.encode()), seed]).standard_normal(out[name].shape)
        drawn = base * np.exp(spread * noise) if base else spread * noise
        out[name] = __import__('jax').numpy.asarray(drawn.astype(out[name].dtype))
    for name, factor in factors.items():
        out[name] = (out[name] * factor).astype(out[name].dtype)
    return out
```

```python
from collections import defaultdict, namedtuple
from contextlib import ExitStack

import concourse.bass as bass
from concourse import mybir

F32 = mybir.dt.float32
F32R = mybir.dt.float32r
I32 = mybir.dt.int32
ACT = mybir.ActivationFunctionType
ALU = mybir.AluOpType
AXX = mybir.AxisListType.X

P = 128
RB = 2
T = RB * P
D = 2048
KT = D // P
HD = 128
NH = 16
NKV = 4
GROUP = NH // NKV
N_SEL = T // 4
IDX_H, IDX_D = 16, 64
ROT_A, ROT_I, ROT_M = 16, 8, 32
NROT = ROT_A + ROT_I + ROT_M
ALPHA = 4.0 ** 0.25
LN_EPS, RMS_EPS = 1e-5, 1e-6
NEG = -1e30
TAKEN = -3e38
MH, NOPE, ROPE, VD = 8, 128, 64, 128
QRANK, KVRANK = 512, 256
HH = 8
LEVELS = 8
WORDS = 18432
TWO_PI_HI, TWO_PI_MID, TWO_PI_LO = 6.28125, 1.9350051879882812e-03, 3.0199159819545e-07
ROUND = 12582912.0

C_IDENT, C_ONES, C_TRI, C_LT, C_GT, C_ROT = 0, 128, 256, 384, 512, 640
NCONST = C_ROT

STAGES = [
    ("a_qkv", 6, True, 4, 512), ("a_gate", 4, True, 4, 512), ("a_idx", 4, True, 4, 276),
    ("a_out", 4, True, 4, 512), ("ple0", 4, False, 4, 512),
    ("b_kvq", 6, True, 4, 512), ("b_gate", 4, True, 4, 512), ("b_out", 4, True, 4, 512), ("ple1", 4, False, 4, 512),
    ("c_hq", 2, True, 4, 512), ("c_f", 4, True, 4, 512), ("c_hi", 2, True, 4, 512), ("c_hg", 2, True, 4, 512),
    ("c_mla", 2, True, 4, 416), ("uq", 1, False, 4, 384), ("ukv", 1, False, 2, 512),
    ("c_out", 4, True, 4, 512), ("mlp", 32, False, 4, 512),
]


Stage = namedtuple("Stage", "name units mods kq width v0 g0 s0 m0 next per")


class Names:
    pass


def plan():
    out, v, g, s, m = {}, 0, 0, 0, 0
    for n, (name, units, mods, kq, width) in enumerate(STAGES):
        nxt = STAGES[n + 1][0] if n + 1 < len(STAGES) else None
        out[name] = Stage(name=name, units=units, mods=mods, kq=kq, width=width, v0=v, g0=g, s0=s, m0=m,
                                    next=nxt, per=3 if mods else 2)
        v += units + (units // 2 if mods else 0)
        m += units // 2 if mods else 0
        g += units
        s += 4 if units == 1 else units
    return out


PLAN = plan()


def v_of(st, i, k):
    if k == 0:
        return st.v0 if isinstance(i, int) and i == 0 else st.v0 + st.per * i
    return st.v0 + st.per * i + (k if k == 1 else st.per)


def v_mod(st, i):
    return st.v0 + st.per * i + 2


class Lane:

    def __init__(self, eng, step):
        self.eng, self.step = eng, step
        self.base, self.n = {}, defaultdict(int)

    def at(self, key="step"):
        return self.base.get(key, 0) + self.n[key]

    def did(self, ins):
        ins.then_inc(self.step, 1)
        self.n["step"] += 1

    def sync(self):
        self.eng.wait_ge(self.step, self.at())

    def link(self, ins):
        self.did(ins)
        self.sync()

    def loop(self, count, per, body):
        if count == 1:
            body(0)
            return
        if count <= 0:
            return
        start = {k: self.at(k) for k in set(per) | set(self.n)}
        with self.eng.Fori(0, count) as i:
            self.base = {k: start[k] + i * per[k] if per.get(k) else start[k] for k in start}
            self.n = defaultdict(int)
            body(i)
            got = {k: n for k, n in self.n.items() if n}
            assert got == {k: n for k, n in per.items() if n}, f"a turn counts {got}"
        self.base = {}
        self.n = defaultdict(int, {k: start[k] + count * per.get(k, 0) for k in start})


def heads_in_turn(lane, per, turn, count=4, unroll=4):
    turn((0, 0), None)

    def body(i):
        for k in range(unroll):
            turn((i, k + 1) if k + 1 < unroll else (i + 1, 0), (i, k))

    lane.loop(count - 1, per, body)
    last = count - 1
    for k in range(unroll):
        turn((last, k + 1) if k + 1 < unroll else None, (last, k))


def build(nc, d, out):
    ctx = ExitStack()
    with ctx:
        m = memory(nc, ctx, d, out)
        block = ctx.enter_context(nc.Block())

        @block.sync
        def _(eng):
            sync_program(nc, eng, m, d, out)

        @block.gpsimd
        def _(eng):
            pool_program(nc, eng, m, d)

        @block.scalar
        def _(eng):
            scalar_program(nc, eng, m, d)

        @block.vector
        def _(eng):
            vector_program(nc, eng, m, d)

        @block.tensor
        def _(eng):
            tensor_program(nc, eng, m, d)


def memory(nc, ctx, d, out):
    m = Names()

    def sb(name, shape, dt=F32):
        return ctx.enter_context(nc.sbuf_tensor(name, shape, dt))

    def ps(name, shape):
        return ctx.enter_context(nc.psum_tensor(name, shape, F32))

    def sem(name):
        return ctx.enter_context(nc.semaphore(name))

    arena = nc.alloc_sbuf_tensor("arena", [P, WORDS], F32)
    base = nc.lookup_mloc(arena).addr

    def at(name, word, shape, dt=F32):
        n = 1
        for x in shape[1:]:
            n *= x
        assert word + n <= WORDS, (name, word + n)
        return nc.alloc_sbuf_tensor_at(name, shape, dt, offset=base + 4 * word)

    raw_words = 4 * 4 * 512
    raw_arena = nc.alloc_sbuf_tensor("raw", [P, 4, 4, 512], F32)
    raw_base = nc.lookup_mloc(raw_arena).addr
    m.raw = raw_arena

    def at_raw(name, word, shape, dt=F32):
        n = 1
        for x in shape[1:]:
            n *= x
        assert word + n <= raw_words, (name, word + n)
        return nc.alloc_sbuf_tensor_at(name, shape, dt, offset=raw_base + 4 * word)

    m.hi, m.lo = sb("w_high", [P, 4, 4, 512], F32R), sb("w_low", [P, 4, 4, 512], F32R)
    m.xh, m.xl = sb("x_high", [P, KT, T], F32R), sb("x_low", [P, KT, T], F32R)
    m.const = sb("const", [P, NCONST])
    m.ident, m.ones = m.const[:, C_IDENT:C_IDENT + P], m.const[:, C_ONES:C_ONES + P]
    m.tri, m.lt, m.gt = (m.const[:, c:c + P] for c in (C_TRI, C_LT, C_GT))
    m.acc = sb("mod_sum", [P, 512])
    m.ct = sb("cond_columns", [P, KT])
    m.cs = sb("cos_sin", [P, 2, RB, NROT])
    m.st = sb("stats", [P, RB, 4, 6])
    m.mv = sb("mean_var", [P, 2 * RB, 2])
    m.rstd = sb("rstd", [P, 2 * RB])
    m.msq = sb("mean_square", [P, 2 * RB])
    m.brow = sb("mod_bias", [1, 512])
    m.dummy = sb("credit_word", [P, 1])

    m.res = at("residual", 0, [P, RB, D])
    m.posi = at("positions_i", 4096, [P, 2 * RB], I32)
    m.posf = at("positions_f", 4104, [P, 2 * RB])
    m.ang = at("angles", 4112, [P, RB, NROT])
    m.turns = at("angle_turns", 4112 + 2 * NROT, [P, RB, NROT])
    m.crow = at("cond_rows", 4112 + 4 * NROT, [KT, P])
    m.rot = at("rotary_rates", 4112 + 4 * NROT + P, [P, NROT])
    m.pa = at("proj_a", 4096, [P, RB, 6224])
    m.a_kt = at("a_keys_t", 0, [P, NKV, T])
    m.a_ikt = at("a_index_keys_t", 1024, [P, T])
    m.a_ikd = at("a_index_keys_twice", 1280, [P, RB, 2, IDX_D])
    m.a_bias0 = at("a_causal_bias", 1536, [P, 384])
    m.a_bias = at("a_bias", 1920, [P, 384])
    m.a_score = at("a_index_score", 2304, [P, 384])
    m.a_top = at("a_top8", 2688, [P, 2, 8])
    m.a_rope = at("a_rope", 2704, [P, 2, 20 * 2 * ROT_A])
    m.a_iqs = at("a_index_q", 2704, [P, 2, RB, P])
    m.a_iws = at("a_index_w", 16544, [P, 2, RB, 2])
    m.a_iqt = at("a_index_q_t", 3216, [P, 2, T])
    m.a_rl = at("a_index_relu", 16552, [P, 2, 2, 384])
    m.a_qs = at("a_q", 2704, [P, 2, RB, P])
    m.a_qt = at("a_q_t", 3216, [P, 2, T])
    m.a_lg = at("a_logits", 16544, [P, 2, 384])
    m.a_pt = at("a_probs_t", 17312, [P, 2, 384])
    m.a_og = at("a_out_gated", 2304, [P, RB, P])
    m.a_nm = at("a_neg_max", 2560, [P, 2, RB])
    m.a_sum = at("a_sum", 2568, [P, 2, RB])
    m.a_rs = at("a_inverse_sum", 2576, [P, 2, RB])
    m.row_g = at("row_g", 4096, [P, D])
    m.row_b = at("row_b", 6144, [P, D])
    m.ple_w = at("ple_w", 8192, [P, 2, D])
    m.ple_p = at("ple_p", 12288, [P, RB, 256])
    m.ple_pt = at("ple_p_t", 12800, [P, 2, T])
    m.ple_s = at("ple_gate", 13312, [P, 2, RB, 512])
    m.pb = at("proj_b", 4096, [P, RB, 5120])
    m.b_kt = at("b_keys_t", 14336, [P, NKV, T])
    m.b_qs = at("b_q", 15360, [P, 2, RB, P])
    m.b_qt = at("b_q_t", 15872, [P, 1, T])
    m.b_mask = at("b_mask", 16128, [P, 384])
    m.b_e = at("b_exp", 16512, [P, 384])
    m.b_sp = at("b_softplus", 16896, [P, 384])
    m.b_lom = at("b_log_one_minus", 17280, [P, 384])
    m.b_a = at("b_weights", 17664, [P, 1, 384])
    m.b_og = at("b_out_gated", 18048, [P, RB, P])
    m.c_g1 = at("c_row_gain", 4096, [P, D])
    m.c_sc = at("c_row_scale", 6144, [P, D])
    m.c_sh = at("c_row_shift", 15360, [P, D])
    m.c_h = at("c_normed", 10240, [P, RB, D])
    m.pc = at("proj_c", 0, [P, RB, 5120])
    m.pm = at("proj_mla", 10240, [P, RB, 832])
    m.m_rg = at("m_norm_rows", 11904, [P, QRANK + KVRANK])
    m.m_rope = at("m_rope", 12672, [P, 2, 512])
    m.m_krd = m.acc[:, 0:RB * P].rearrange("p (r e) -> p r e", r=RB)
    m.mq = at("mla_q", 11264, [P, RB, 1536])
    m.mkv = at("mla_kv", 14336, [P, RB, 2048])
    m.m_rope2 = at_raw("m_rope2", 0, [P, 2, 512])
    m.m_qs = at_raw("m_q", 1024, [P, 2, RB, 256])
    m.m_ks = at_raw("m_k", 2048, [P, 2, RB, P])
    m.m_qt = at_raw("m_q_t", 2560, [P, 2, 2, T])
    m.m_ktt = at_raw("m_k_t", 3584, [P, 2, T])
    m.m_krt = at_raw("m_k_rope_t", 4096, [P, T])
    m.m_lg = at_raw("m_logits", 4352, [P, 2, RB, T])
    m.m_pt = at_raw("m_probs_t", 5376, [P, 2, RB, T])
    m.m_og = at_raw("m_out", 6400, [P, RB, P])
    m.m_nm = at_raw("m_neg_max", 6656, [P, 2, RB])
    m.m_sum = at_raw("m_sum", 6664, [P, 2, RB])
    m.m_rs = at_raw("m_inverse_sum", 6672, [P, 2, RB])
    m.h_l0 = at("h_lb_logits", 10240, [P, 2, 2, 1024])
    m.h_t = at("h_one_minus", 14336, [P, RB, 2048])
    m.h_md = at("h_spans", 10240, [P, 2, 9, P])
    m.h_mask = at("h_level_masks", 12544, [P, LEVELS, P])
    m.h_tm = at("h_masked", 13568, [P, 2, LEVELS, P])
    m.h_lf = at("h_log_f", 15616, [P, 2, RB, P])
    m.h_fs = at("h_f", 16128, [P, 2, RB, P])
    m.h_qs = at("h_q", 16640, [P, RB, P])
    m.h_qt = at("h_q_t", 16896, [P, T])
    m.h_kt = at("h_k_t", 17152, [P, 2, T])
    m.h_ks = at("h_k_sum", 17664, [P, T])
    m.h_at = at("h_weights_t", 17920, [P, 4, P])
    m.h_e = at_raw("h_decay", 0, [P, 2, 4, T])
    m.h_kq = at_raw("h_keys_queries", 2048, [P, 2, 4, T])
    m.h_sq = at_raw("h_squares", 4096, [P, RB, 1024])
    m.h_ng = at_raw("h_norm_g", 6144, [P, P])
    m.h_ms = at_raw("h_mean_sq", 6272, [P, RB, HH])
    m.h_r = at_raw("h_rstd", 6288, [P, RB, HH])
    m.mix = at("mix", 4096, [P, RB, D])
    m.x_ga = at("x_row_gate", 8192, [P, D])
    m.x_pg = at("x_row_post", 10240, [P, D])
    m.x_g1 = at("x_row_gain", 12288, [P, D])
    m.x_sc = at("x_row_scale", 14336, [P, D])
    m.x_sh = at("x_row_shift", 16384, [P, D])
    m.y = at("mlp_sum", 4096, [P, RB, D])
    m.uh = at("u_high", 8192, [P, KT, T], F32R)
    m.ul = at("u_low", 12288, [P, KT, T], F32R)
    m.ur = at("u_rows", 16384, [P, 2, RB, 512])
    m.z_gm = at_raw("z_row_gate", 0, [P, D])
    m.z_pg = at_raw("z_row_post", 2048, [P, D])

    m.g = ps("products", [P, 4, 512])
    m.t = ps("transposed", [P, 2, 512])
    m.u = ps("aside", [P, 2, 512])

    m.mod_d = nc.dram_tensor("mod_row", (6 * D,), F32).ap()
    m.res_d = nc.dram_tensor("residual_kept", (T, D), F32).ap()

    m.s_landed = [sem(f"quarter_landed_{j}") for j in range(4)]
    m.s_raw_used = sem("raw_used")
    m.s_w_high = sem("w_high")
    m.s_w_used = sem("w_used")
    m.s_x_high_ready = sem("x_high_ready")
    m.s_y_ready = sem("y_ready")
    m.s_const_landed = sem("const_landed")
    m.s_x_landed = sem("x_landed")
    m.s_pos_landed = sem("pos_landed")
    m.s_rows_landed = sem("rows_landed")
    m.s_rows2_landed = sem("rows2_landed")
    m.s_ple_landed = sem("ple_landed")
    m.s_res_stored = sem("res_stored")
    m.s_out_stored = sem("out_stored")
    m.s_mod_summed = sem("mod_summed")
    m.s_mod_row = sem("mod_row")
    m.s_brow_landed = sem("brow_landed")
    m.s_mod_stored = sem("mod_stored")
    m.s_pool_step = sem("pool_step")
    m.s_act_step = sem("act_step")
    m.s_dve_step = sem("dve_step")
    m.s_pe_step = sem("pe_step")
    m.s_angles_ready = sem("angles_ready")
    m.s_sin_ready = sem("sin_ready")
    m.s_var_ready = sem("var_ready")
    m.s_std_ready = sem("std_ready")
    m.s_ple_full = sem("ple_full")
    m.s_ple_free = sem("ple_free")
    m.s_x4_ready = sem("x4_ready")
    m.s_mlp_done = sem("mlp_done")
    m.s_res2_landed = sem("res2_landed")
    m.s_a_ready = sem("a_ready")
    m.s_a_k_t = sem("a_k_t")
    m.s_a_ktp = sem("a_ktp")
    m.s_a_k_copied = sem("a_k_copied")
    m.s_a_iq = sem("a_iq")
    m.s_a_iqt = sem("a_iqt")
    m.s_a_iqc = sem("a_iqc")
    m.s_a_dots = sem("a_dots")
    m.s_a_relu = sem("a_relu")
    m.s_a_idx_done = sem("a_idx_done")
    m.s_a_biased = sem("a_biased")
    m.s_a_q = sem("a_q")
    m.s_a_qtp = sem("a_qtp")
    m.s_a_qtc = sem("a_qtc")
    m.s_a_s = sem("a_s")
    m.s_a_nmax = sem("a_nmax")
    m.s_a_p = sem("a_p")
    m.s_a_ptp = sem("a_ptp")
    m.s_a_ptc = sem("a_ptc")
    m.s_a_o = sem("a_o")
    m.s_a_ogr = sem("a_ogr")
    m.s_a_ogt = sem("a_ogt")
    m.s_a_xh = sem("a_xh")
    m.s_a_done = sem("a_done")
    m.s_b_ready = sem("b_ready")
    m.s_b_k_t = sem("b_k_t")
    m.s_b_k_copied = sem("b_k_copied")
    m.s_b_q = sem("b_q")
    m.s_b_qtp = sem("b_qtp")
    m.s_b_qtc = sem("b_qtc")
    m.s_b_z = sem("b_z")
    m.s_b_abs = sem("b_abs")
    m.s_b_l = sem("b_l")
    m.s_b_lomr = sem("b_lomr")
    m.s_b_sfx = sem("b_sfx")
    m.s_b_a1 = sem("b_a1")
    m.s_b_ex = sem("b_ex")
    m.s_b_w = sem("b_w")
    m.s_b_o = sem("b_o")
    m.s_b_ogr = sem("b_ogr")
    m.s_b_ogt = sem("b_ogt")
    m.s_b_xh = sem("b_xh")
    m.s_b_done = sem("b_done")
    m.s_m_ready = sem("m_ready")
    m.s_m_krt_t = sem("m_krt_t")
    m.s_m_krt_c = sem("m_krt_c")
    m.s_m_q = sem("m_q")
    m.s_m_qtp = sem("m_qtp")
    m.s_m_qtc = sem("m_qtc")
    m.s_m_s = sem("m_s")
    m.s_m_nmax = sem("m_nmax")
    m.s_m_p = sem("m_p")
    m.s_m_ptp = sem("m_ptp")
    m.s_m_ptc = sem("m_ptc")
    m.s_m_o = sem("m_o")
    m.s_m_ogr = sem("m_ogr")
    m.s_m_ogt = sem("m_ogt")
    m.s_m_xh = sem("m_xh")
    m.s_m_done = sem("m_done")
    m.s_m_qkv = sem("m_qkv")
    m.s_h_lb = sem("h_lb")
    m.s_h_lbs = sem("h_lbs")
    m.s_h_fr = sem("h_fr")
    m.s_h_rows = sem("h_rows")
    m.s_h_consts = sem("h_consts")
    m.s_h_q = sem("h_q")
    m.s_h_logf = sem("h_logf")
    m.s_h_tr = sem("h_tr")
    m.s_h_qc = sem("h_qc")
    m.s_h_kc = sem("h_kc")
    m.s_h_d = sem("h_d")
    m.s_h_ex = sem("h_ex")
    m.s_h_mul = sem("h_mul")
    m.s_h_am = sem("h_am")
    m.s_h_msk = sem("h_msk")
    m.s_h_off = sem("h_off")
    m.s_h_red = sem("h_red")
    m.s_h_o = sem("h_o")
    m.s_h_oc = sem("h_oc")
    m.s_h_ms1 = sem("h_ms1")
    m.s_h_std = sem("h_std")
    m.s_g_free = [sem(f"product_free_{b}") for b in range(2)]
    m.s_t_full = [sem(f"transposed_full_{b}") for b in range(2)]
    m.s_t_free = [sem(f"transposed_free_{b}") for b in range(2)]
    return m


def gemm_turns(lane, st, per, turn, tail):
    n = st.units // 2
    lane.loop(n - 1, per, turn)
    tail(n - 1)


def rows(ap, n):
    return ap.rearrange("(o n) -> o n", o=1).broadcast_to((P, n))


def sync_program(nc, sp, m, d, out):
    lane = Lane(sp, m.s_pe_step)

    def load(st, v, src):
        for j in range(4):
            sp.wait_ge(m.s_raw_used, 4 * v + j + 1)
            sp.dma_start(m.raw[:, j, 0:st.kq, 0:st.width], src(j)).then_inc(m.s_landed[j], 16)

    def tiles(w, j, col, width, row=0):
        return w.rearrange("(k p) n -> p k n", p=P)[:, row + 4 * j:row + 4 * j + 4, bass.ds(col, width)]

    def source(name, u):
        col = {"a_qkv": 0, "a_gate": 3072, "a_idx": 5120, "b_gate": 2048, "c_hq": 832, "c_f": 1856,
               "c_hi": 3904, "c_hg": 4928}.get(name, 0)
        width = PLAN[name].width
        if name == "b_kvq":
            w, c = (d.w_kv_b, 512 * u) if isinstance(u, int) and u < 2 else (d.w_in_b, 512 * (u - 2))
        elif name == "uq":
            return lambda j: d.w_uq.rearrange("(k p) n -> p k n", p=P)[:, :, 384 * j:384 * j + 384]
        elif name == "ukv":
            return lambda j: d.w_ukv.rearrange("(k p) n -> p k n", p=P)[:, :, 512 * j:512 * j + 512]
        else:
            w = {"a": d.w_in_a, "b": d.w_in_b, "c": d.w_in_c}.get(name[0])
            w = {"a_out": d.w_o_a, "b_out": d.w_o_b, "c_out": d.w_out, "ple0": d.w_g0, "ple1": d.w_g1}.get(name, w)
            c = col + width * u
        c = sp.snap(c) if not isinstance(c, int) else c
        return lambda j: tiles(w, j, c, width)

    def load_unit(name, i, k):
        st = PLAN[name]
        load(st, v_of(st, i, k), source(name, 2 * i + k))

    def load_mod(name, i):
        st = PLAN[name]
        c = 512 * (st.m0 + i)
        c = sp.snap(c) if not isinstance(c, int) else c
        load(PLAN["a_qkv"], v_mod(st, i), lambda j: tiles(d.w_mod, j, c, 512))

    def gemm(name, before_next=None, next_too=True, peel=0):
        st = PLAN[name]

        def turn(i):
            load_unit(name, i, 1)
            if st.mods:
                load_mod(name, i)
            load_unit(name, i, 2)

        def tail(i):
            load_unit(name, i, 1)
            if st.mods:
                load_mod(name, i)
            if before_next:
                before_next()
            if next_too:
                load_unit(st.next, 0, 0)

        n = st.units // 2
        if name == "b_kvq":
            for i in range(n - 1):
                turn(i)
        else:
            lane.loop(n - 1, {}, turn)
        tail(n - 1)

    def bring(tile, src, s):
        sp.dma_start(tile, src).then_inc(s, 16)

    tokens = "(r p) n -> p r n"
    bring(m.const[:], d.consts, m.s_const_landed)
    bring(m.crow[:], d.c.rearrange("o (k p) -> (o k) p", p=P), m.s_const_landed)
    bring(m.res[:], d.x.rearrange(tokens, p=P), m.s_x_landed)
    with nc.allow_non_contiguous_dma(reason="512 positions"):
        bring(m.posi[:, 0:RB], d.positions.rearrange("o (r p) -> p (o r)", p=P), m.s_pos_landed)
        bring(m.posi[:, RB:2 * RB], d.positions_2.rearrange("o (r p) -> p (o r)", p=P), m.s_pos_landed)
    bring(m.rot[:], d.rates, m.s_pos_landed)
    load_unit("a_qkv", 0, 0)
    for name in ("a_qkv", "a_gate", "a_idx"):
        gemm(name)

    def norm_rows(layer):
        def go():
            bring(m.row_g[:], rows(d.ln_g[layer], D), m.s_rows_landed)
            bring(m.row_b[:], rows(d.ln_b[layer], D), m.s_rows_landed)
            bring(m.ple_w[:], d.w_ple[layer].rearrange("(k p) n -> p k n", p=P), m.s_ple_landed)
            bring(m.ple_p[:], d.p[layer].rearrange(tokens, p=P), m.s_ple_landed)
        return go

    sp.wait_ge(m.s_a_done, NH + 2)
    bring(m.res[:], d.x.rearrange(tokens, p=P), m.s_x_landed)
    gemm("a_out", norm_rows(0))
    gemm("ple0")
    gemm("b_kvq")
    gemm("b_gate")
    sp.wait_ge(m.s_b_done, NH + 2)
    gemm("b_out", norm_rows(1))

    def c_rows():
        sp.wait_ge(m.s_y_ready, 20)
        bring(m.c_g1[:], rows(d.pre_mix_g, D), m.s_rows2_landed)
        sp.wait_ge(m.s_mod_stored, 16 * 9)
        bring(m.c_sh[:], rows(m.mod_d[0:D], D), m.s_rows2_landed)
        bring(m.c_sc[:], rows(m.mod_d[D:2 * D], D), m.s_rows2_landed)

    gemm("ple1", c_rows)
    sp.wait_ge(m.s_x4_ready, 4)
    bring(m.res_d.rearrange(tokens, p=P), m.res[:], m.s_res_stored)
    for name in ("c_hq", "c_f", "c_hi", "c_hg"):
        gemm(name)
    sp.wait_ge(m.s_w_used, 4 * PLAN["c_f"].g0 + 4)
    bring(m.m_rg[:, 0:QRANK], rows(d.q_norm_g, QRANK), m.s_rows2_landed)
    bring(m.m_rg[:, QRANK:], rows(d.kv_norm_g, KVRANK), m.s_rows2_landed)
    gemm("c_mla")
    load_unit("ukv", 0, 0)
    sp.wait_ge(m.s_m_done, MH + 2)
    for s in range(2):
        for dr, lb in enumerate((d.lb_f, d.lb_b)):
            bring(m.h_l0[:, s, dr, :], rows(lb[s], 1024), m.s_h_rows)
    bring(m.h_ng[:], rows(d.hgrn_g, P), m.s_h_rows)
    sp.wait_ge(m.s_h_fr, 2)
    bring(m.h_md[:], d.spans.rearrange("p (a b c) -> p a b c", a=2, b=9), m.s_h_consts)
    bring(m.h_mask[:], d.level_masks.rearrange("p (a b) -> p a b", a=LEVELS), m.s_h_consts)
    for b in range(2):
        sp.wait_ge(m.s_t_free[b], 26)
    load_unit("c_out", 0, 0)
    sp.wait_ge(m.s_res_stored, 16)
    bring(m.res[:], m.res_d.rearrange(tokens, p=P), m.s_res2_landed)

    def x_rows():
        sp.wait_ge(m.s_mod_stored, 16 * 21)
        bring(m.x_ga[:], rows(m.mod_d[2 * D:3 * D], D), m.s_rows2_landed)
        bring(m.x_pg[:], rows(d.post_mix_g, D), m.s_rows2_landed)
        bring(m.x_g1[:], rows(d.pre_mlp_g, D), m.s_rows2_landed)
        bring(m.x_sc[:], rows(m.mod_d[4 * D:5 * D], D), m.s_rows2_landed)
        bring(m.x_sh[:], rows(m.mod_d[3 * D:4 * D], D), m.s_rows2_landed)

    gemm("c_out", x_rows, next_too=False)
    mlp = PLAN["mlp"]

    def mlp_load(q, k):
        if k < 4:
            c = 2048 * q + 512 * k
            c = sp.snap(c) if not isinstance(c, int) else c
            load(mlp, mlp.v0 + 8 * q + k, lambda j: tiles(d.w_up, j, c, 512))
        else:
            if isinstance(q, int):
                load(mlp, mlp.v0 + 8 * q + k,
                     lambda j: tiles(d.w_down, j, 512 * (k - 4), 512, row=KT * q))
            else:
                off = sp.snap(2048 * q)
                w = d.w_down[bass.ds(off, 2048), :]
                load(mlp, mlp.v0 + 8 * q + k, lambda j: tiles(w, j, 512 * (k - 4), 512))

    lane.loop(4, {}, lambda q: [mlp_load(q, k) for k in range(8)])
    sp.wait_ge(m.s_raw_used, 4 * (mlp.v0 + 32) + 4)
    sp.wait_ge(m.s_mod_stored, 16 * 25)
    bring(m.z_gm[:], rows(m.mod_d[5 * D:6 * D], D), m.s_rows2_landed)
    bring(m.z_pg[:], rows(d.post_mlp_g, D), m.s_rows2_landed)
    for c in range(4):
        sp.wait_ge(m.s_mlp_done, c + 1)
        bring(out.rearrange(tokens, p=P)[:, :, 512 * c:512 * c + 512], m.res[:, :, 512 * c:512 * c + 512], m.s_out_stored)
    sp.wait_ge(m.s_out_stored, 64)


def pool_program(nc, pool, m, d):
    lane = Lane(pool, m.s_pool_step)
    credits = [(m.s_raw_used, 4), (m.s_w_used, 4), (m.s_mod_summed, 1), (m.s_mod_stored, 16), (m.s_h_oc, 1),
               (m.s_a_done, 2), (m.s_b_done, 2), (m.s_m_done, 2), (m.s_a_idx_done, 2), (m.s_ple_free, 1)]
    credits += [(s, 1) for s in m.s_g_free + m.s_t_free]
    for n, (s, k) in enumerate(credits):
        if n:
            pool.wait_ge(credits[n - 1][0], 1)
        nc.gpsimd.memset(m.dummy[:], 0.0).then_inc(s, k)

    pool.wait_ge(m.s_a_ready, 1)
    nc.gpsimd.tensor_copy(m.a_ikd[:, :, 0, :], m.pa[:, :, 6144:6208]).then_inc(m.s_a_k_t, 1)
    nc.gpsimd.tensor_copy(m.a_ikd[:, :, 1, :], m.pa[:, :, 6144:6208]).then_inc(m.s_a_k_t, 1)

    def index_pair(i):
        for k in range(2):
            t = 2 * i + k
            pool.wait_ge(m.s_a_idx_done, t + 1)
            nc.gpsimd.tensor_copy(m.a_iws[:, k], m.pa[:, :, bass.ds(6208 + 2 * t, 2)]).then_inc(m.s_a_iq, 1)
            nc.gpsimd.tensor_copy(m.a_iqs[:, k], m.pa[:, :, bass.ds(5120 + P * t, P)]).then_inc(m.s_a_iq, 1)

    lane.loop(4, {}, index_pair)

    pool.wait_ge(m.s_a_biased, 1)

    def a_heads(i):
        for k in range(GROUP):
            pool.wait_ge(m.s_a_done, 4 * i + k + 1)
            nc.gpsimd.tensor_copy(m.a_qs[:, k % 2], m.pa[:, :, bass.ds(HD * (4 * k + i), HD)]).then_inc(m.s_a_q, 1)

    lane.loop(GROUP, {}, a_heads)
    pool.wait_ge(m.s_b_ready, 1)

    def b_heads(i):
        for k in range(GROUP):
            pool.wait_ge(m.s_b_done, 4 * i + k + 1)
            nc.gpsimd.tensor_copy(m.b_qs[:, k % 2], m.pb[:, :, bass.ds(1024 + HD * (4 * k + i), HD)]).then_inc(m.s_b_q, 1)

    lane.loop(GROUP, {}, b_heads)
    pool.wait_ge(m.s_m_ready, 1)
    nc.gpsimd.memset(m.m_qs[:], 0.0).then_inc(m.s_m_qkv, 1)
    pool.wait_ge(m.s_m_qkv, 1)

    def m_heads(i):
        for k in range(2):
            t = 2 * i + k
            pool.wait_ge(m.s_m_done, t + 1)
            nc.gpsimd.tensor_copy(m.m_qs[:, k, :, 0:NOPE + ROPE], m.mq[:, :, bass.ds((NOPE + ROPE) * t, NOPE + ROPE)]).then_inc(m.s_m_q, 1)
            nc.gpsimd.tensor_copy(m.m_ks[:, k], m.mkv[:, :, bass.ds((NOPE + VD) * t, NOPE)]).then_inc(m.s_m_q, 1)

    lane.loop(MH // 2, {}, m_heads)
    pool.wait_ge(m.s_h_fr, 2)

    def h_heads(t):
        pool.wait_ge(m.s_h_oc, t + 1)
        nc.gpsimd.tensor_copy(m.h_qs[:], m.pc[:, :, bass.ds(HD * t, HD)]).then_inc(m.s_h_q, 1)
        for dr in range(2):
            nc.gpsimd.tensor_copy(m.h_fs[:, dr], m.pc[:, :, bass.ds(1024 * (dr + 1) + HD * t, HD)]).then_inc(m.s_h_q, 1)

    lane.loop(HH, {}, h_heads)


def scalar_program(nc, act, m, d):
    lane = Lane(act, m.s_act_step)

    def high(st, v, g, js=range(4)):
        for j in js:
            act.wait_ge(m.s_landed[j], 16 * v + 16)
            act.wait_ge(m.s_w_used, 4 * g + j + 1)
            act.activation(m.hi[:, j, 0:st.kq, 0:st.width], m.raw[:, j, 0:st.kq, 0:st.width], ACT.Copy).then_inc(m.s_w_high, 1)

    def high_unit(name, i, k):
        st = PLAN[name]
        high(st, v_of(st, i, k), st.g0 + 2 * i + k)

    def product(st, i, k):
        act.wait_ge(m.s_w_used, 4 * (st.g0 + 2 * i + k) + 8)
        return m.g[:, 2 * k:2 * k + 2, 0:st.width]

    def mod_io(st, i):
        n = st.m0 + i
        act.wait_ge(m.s_mod_row, n + 1)
        act.dma_start(m.mod_d[bass.ds(512 * n, 512)].rearrange("(o n) -> o n", o=1), m.acc[0:1, :]).then_inc(m.s_mod_stored, 16)
        if not (isinstance(n, int) and n == 23):
            act.dma_start(m.brow[:], d.b_mod[bass.ds(512 * n + 512, 512)].rearrange("(o n) -> o n", o=1)).then_inc(m.s_brow_landed, 16)

    def gemm(name, take, next_too=True, per={}):
        st = PLAN[name]

        def turn(i):
            high_unit(name, i, 1)
            take(st, i, 0)
            high_unit(name, i, 2)
            take(st, i, 1)
            if st.mods:
                mod_io(st, i)

        def tail(i):
            high_unit(name, i, 1)
            take(st, i, 0)
            if next_too:
                high_unit(st.next, 0, 0)
            take(st, i, 1)
            if st.mods:
                mod_io(st, i)

        gemm_turns(lane, st, per, turn, tail)

    def keep(tile, col, func=ACT.Copy):
        def take(st, i, k):
            src = product(st, i, k)
            act.activation(tile[:, :, bass.ds(col + st.width * (2 * i + k), st.width)], src, func).then_inc(m.s_g_free[k], 1)
        return take

    def nothing(st, i, k):
        pass

    def high_columns(k0, uses):
        for q in range(uses):
            n = lane.n["T"]
            act.wait_ge(m.s_t_full[n % 2], n // 2 + 1)
            act.activation(m.xh[:, k0 + 2 * q:k0 + 2 * q + 2, :], m.t[:, n % 2, :].rearrange("p (k t) -> p k t", k=2), ACT.Copy)\
               .then_inc(m.s_x_high_ready, 1)
            lane.n["T"] += 1

    def std(n, columns=RB):
        act.wait_ge(m.s_var_ready, n)
        act.activation(m.rstd[:, 0:columns], m.msq[:, 0:columns], ACT.Sqrt).then_inc(m.s_std_ready, 1)

    act.dma_start(m.brow[:], d.b_mod[0:512].rearrange("(o n) -> o n", o=1)).then_inc(m.s_brow_landed, 16)
    act.wait_ge(m.s_t_full[0], 1)
    act.activation(m.ct[:], m.t[:, 0, 0:KT], ACT.Silu).then_inc(m.s_t_free[0], 1)
    lane.n["T"] += 1
    act.wait_ge(m.s_angles_ready, 1)
    act.activation(m.cs[:, 0], m.turns[:], ACT.Sin).then_inc(m.s_sin_ready, 1)
    act.activation(m.cs[:, 1], m.ang[:], ACT.Sin).then_inc(m.s_sin_ready, 1)
    high_unit("a_qkv", 0, 0)
    high_columns(0, 8)
    gemm("a_qkv", keep(m.pa, 0))
    gemm("a_gate", keep(m.pa, 3072, ACT.Silu))
    gemm("a_idx", keep(m.pa, 5120))

    act.wait_ge(m.s_a_ktp, 2)
    act.activation(m.a_kt[:].rearrange("p (a k) t -> p a (k t)", a=2), m.g[:, 2:4, :], ACT.Copy).then_inc(m.s_a_k_copied, 1)
    act.activation(m.a_ikt[:], m.g[:, 0, 0:T], ACT.Copy).then_inc(m.s_a_k_copied, 1)
    banks = [m.g[:, 2:4, 0:384], m.u[:, 0:2, 0:384]]

    def index_turn(nxt, cur):
        if nxt:
            t, k = 2 * nxt[0] + nxt[1], nxt[1]
            act.wait_ge(m.s_a_iqt, t + 1)
            act.activation(m.a_iqt[:, k], m.g[:, k, 0:T], ACT.Copy).then_inc(m.s_a_iqc, 1)
        if cur:
            t, k = 2 * cur[0] + cur[1], cur[1]
            act.wait_ge(m.s_a_dots, t + 1)
            act.activation(m.a_rl[:, k], banks[k], ACT.Relu, scale=IDX_D ** -0.5 * IDX_H ** -0.5).then_inc(m.s_a_relu, 1)

    heads_in_turn(lane, {}, index_turn, IDX_H // 4, 2)

    def a_turn(nxt, cur):
        if nxt:
            t, k = 4 * nxt[0] + nxt[1], nxt[1] % 2
            act.wait_ge(m.s_a_qtp, t + 1)
            act.activation(m.a_qt[:, k], m.g[:, k, 0:T], ACT.Copy).then_inc(m.s_a_qtc, 1)
        if cur:
            tc, kc, h = 4 * cur[0] + cur[1], cur[1] % 2, 4 * cur[1] + cur[0]
            act.wait_ge(m.s_a_ptp, tc + 1)
            act.activation(m.a_pt[:, kc], m.u[:, kc, 0:384], ACT.Copy).then_inc(m.s_a_ptc, 1)
        if nxt:
            act.wait_ge(m.s_a_nmax, t + 1)
            for rb, cols in enumerate((slice(0, P), slice(P, 384))):
                act.activation(m.a_lg[:, k, cols], m.a_lg[:, k, cols], ACT.Exp, bias=m.a_nm[:, k, rb:rb + 1],
                               accum_out=m.a_sum[:, k, rb:rb + 1]).then_inc(m.s_a_p, 1)
        if cur:
            act.wait_ge(m.s_a_ogt, tc + 1)
            act.activation(m.xh[:, bass.ds(h, 1), :].rearrange("p k t -> p (k t)"), m.t[:, kc, T:2 * T], ACT.Copy).then_inc(m.s_a_xh, 1)

    heads_in_turn(lane, {}, a_turn)

    def norm_and_embed(name_out, name_ple, layer):
        gemm(name_out, nothing)
        std(layer + 1)
        high_columns(0, 8)
        n = lane.n["T"]
        act.wait_ge(m.s_t_full[n % 2], n // 2 + 1)
        act.activation(m.ple_pt[:], m.t[:, n % 2, :].rearrange("p (k t) -> p k t", k=2), ACT.Copy).then_inc(m.s_t_free[n % 2], 1)
        lane.n["T"] += 1

        def gate(st, i, k):
            src = product(st, i, k)
            act.activation(m.ple_s[:, k], src, ACT.Sigmoid).then_inc(m.s_g_free[k], 1)

        gemm(name_ple, gate)

    norm_and_embed("a_out", "ple0", 0)
    high_columns(0, 8)
    gemm("b_kvq", keep(m.pb, 0))
    gemm("b_gate", keep(m.pb, 3072, ACT.Silu))

    act.wait_ge(m.s_b_k_t, 1)
    act.activation(m.b_kt[:].rearrange("p (a k) t -> p a (k t)", a=2), m.g[:, 2:4, :], ACT.Copy).then_inc(m.s_b_k_copied, 1)
    scale = HD ** -0.5

    def b_turn(nxt, cur):
        if nxt:
            t, k = 4 * nxt[0] + nxt[1], nxt[1] % 2
            act.wait_ge(m.s_b_qtp, t + 1)
            act.activation(m.b_qt[:, 0], m.g[:, k, 0:T], ACT.Copy).then_inc(m.s_b_qtc, 1)
            act.wait_ge(m.s_b_z, t + 1)
            act.activation(m.b_e[:], m.g[:, 2 + k, 0:384], ACT.Abs, scale=scale).then_inc(m.s_b_abs, 1)
            act.wait_ge(m.s_b_abs, t + 1)
            lane.link(act.activation(m.b_e[:], m.b_e[:], ACT.Exp, scale=-1.0))
            act.activation(m.b_e[:], m.b_e[:], ACT.Ln, bias=1.0).then_inc(m.s_b_l, 1)
        if cur:
            tc, kc, h = 4 * cur[0] + cur[1], cur[1] % 2, 4 * cur[1] + cur[0]
            act.wait_ge(m.s_b_ogt, tc + 1)
            act.activation(m.xh[:, bass.ds(h, 1), :].rearrange("p k t -> p (k t)"), m.t[:, kc, T:2 * T], ACT.Copy).then_inc(m.s_b_xh, 1)
        if nxt:
            act.wait_ge(m.s_b_a1, t + 1)
            act.activation(m.b_a[:, 0], m.b_a[:, 0], ACT.Exp).then_inc(m.s_b_ex, 1)

    heads_in_turn(lane, {"step": 4}, b_turn)
    norm_and_embed("b_out", "ple1", 1)
    std(3)
    high_columns(0, 8)
    act.wait_ge(m.s_res_stored, 16)
    gemm("c_hq", keep(m.pc, 0))
    gemm("c_f", keep(m.pc, 1024, ACT.Sigmoid))
    gemm("c_hi", keep(m.pc, 3072))
    gemm("c_hg", keep(m.pc, 4096, ACT.Silu))
    gemm("c_mla", keep(m.pm, 0))
    std(4, 2 * RB)
    high_columns(8, 3)
    uq, ukv = PLAN["uq"], PLAN["ukv"]
    for j in range(4):
        high(ukv, ukv.v0, ukv.g0, [j])
        act.wait_ge(m.s_w_used, 4 * uq.g0 + 4 + j + 1)
        act.activation(m.mq[:, :, 384 * j:384 * j + 384], m.g[:, 2 * (j % 2):2 * (j % 2) + 2, 0:384], ACT.Copy).then_inc(m.s_g_free[j % 2], 1)
    for j in range(4):
        act.wait_ge(m.s_w_used, 4 * ukv.g0 + 4 + j + 1)
        act.activation(m.mkv[:, :, 512 * j:512 * j + 512], m.g[:, 2 * (j % 2):2 * (j % 2) + 2, :], ACT.Copy).then_inc(m.s_g_free[j % 2], 1)
    act.wait_ge(m.s_m_krt_t, 1)
    act.activation(m.m_krt[:], m.t[:, 0, 0:T], ACT.Copy).then_inc(m.s_m_krt_c, 1)
    mscale = (NOPE + ROPE) ** -0.5

    def m_turn(nxt, cur):
        if nxt:
            t, k = 2 * nxt[0] + nxt[1], nxt[1]
            act.wait_ge(m.s_m_qtp, t + 1)
            act.activation(m.m_qt[:, k].rearrange("p a t -> p (a t)"), m.g[:, k, :], ACT.Copy).then_inc(m.s_m_qtc, 1)
            act.activation(m.m_ktt[:, k], m.t[:, k, 0:T], ACT.Copy).then_inc(m.s_m_qtc, 1)
        if cur:
            tc, kc = 2 * cur[0] + cur[1], cur[1]
            act.wait_ge(m.s_m_ptp, tc + 1)
            act.activation(m.m_pt[:, kc].rearrange("p a t -> p (a t)"), m.u[:, kc, :], ACT.Copy).then_inc(m.s_m_ptc, 1)
        if nxt:
            act.wait_ge(m.s_m_nmax, t + 1)
            for rb in range(RB):
                act.activation(m.m_lg[:, k, rb], m.g[:, 2 + k, T * rb:T * rb + T], ACT.Exp, scale=mscale, bias=m.m_nm[:, k, rb:rb + 1],
                               accum_out=m.m_sum[:, k, rb:rb + 1]).then_inc(m.s_m_p, 1)
        if cur:
            act.wait_ge(m.s_m_ogt, tc + 1)
            act.activation(m.xh[:, bass.ds(tc, 1), :].rearrange("p k t -> p (k t)"), m.t[:, kc, T:2 * T], ACT.Copy).then_inc(m.s_m_xh, 1)

    heads_in_turn(lane, {}, m_turn, MH // 2, 2)
    act.wait_ge(m.s_h_lb, 1)
    act.activation(m.h_l0[:, 0], m.h_l0[:, 0], ACT.Sigmoid).then_inc(m.s_h_lbs, 1)

    def h_head(t):
        act.wait_ge(m.s_h_q, 3 * t + 3)
        act.activation(m.h_lf[:], m.h_fs[:], ACT.Ln).then_inc(m.s_h_logf, 1)
        act.wait_ge(m.s_h_tr, t + 1)
        act.activation(m.h_qt[:], m.g[:, 0, 0:T], ACT.Copy).then_inc(m.s_h_qc, 1)
        dbanks = [m.g[:, 2], m.g[:, 3], m.u[:, 0], m.u[:, 1]]
        for grp in range(2):
            act.wait_ge(m.s_h_d, 2 * t + grp + 1)
            for b in range(4):
                act.activation(m.h_e[:, b // 2, :, P * (b % 2):P * (b % 2) + P], dbanks[b].rearrange("p (l t) -> p l t", l=4), ACT.Exp)\
                   .then_inc(m.s_h_ex, 1)
        act.wait_ge(m.s_h_am, 3 * t + 1)
        act.activation(m.h_at[:, 1:3, :], m.g[:, 0, 0:T].rearrange("p (a t) -> p a t", a=2), ACT.Copy).then_inc(m.s_h_off, 1)
        act.wait_ge(m.s_h_o, t + 1)
        act.activation(m.pc[:, :, bass.ds(HD * t, HD)], m.g[:, 2, 0:T].rearrange("p (r e) -> p r e", r=2), ACT.Copy).then_inc(m.s_h_oc, 1)

    lane.loop(HH, {}, h_head)
    act.wait_ge(m.s_h_ms1, 1)
    act.activation(m.h_r[:], m.h_ms[:], ACT.Sqrt).then_inc(m.s_h_std, 1)
    high_columns(8, 4)
    high_unit("c_out", 0, 0)
    gemm("c_out", nothing)
    std(5)
    std(6)
    high_columns(0, 8)
    mlp = PLAN["mlp"]

    def mlp_high(q, k):
        high(mlp, mlp.v0 + 8 * q + k, mlp.g0 + 8 * q + k)

    def squares(q, k):
        act.wait_ge(m.s_w_used, 4 * (mlp.g0 + 8 * q + k) + 8)
        lane.did(act.activation(m.ur[:, k % 2], m.g[:, 2 * (k % 2):2 * (k % 2) + 2, :], ACT.Relu))
        act.wait_ge(m.s_act_step, lane.at())
        act.activation(m.ur[:, k % 2], m.ur[:, k % 2], ACT.Square).then_inc(m.s_g_free[k % 2], 1)

    def u_high(q, k):
        for half in range(2):
            b = (mlp_t0 + half) % 2
            act.wait_ge(m.s_t_full[b], (mlp_t0 + half) // 2 + 4 * q + k + 1)
            act.activation(m.uh[:, 4 * k + 2 * half:4 * k + 2 * half + 2, :], m.t[:, b, :].rearrange("p (k t) -> p k t", k=2), ACT.Copy)\
               .then_inc(m.s_x_high_ready, 1)

    mlp_t0 = lane.n["T"]

    def quarter(q, last):
        for k in range(8):
            if k < 7 or not last:
                mlp_high(q, k + 1)
            if k < 4:
                squares(q, k)
            if 1 <= k <= 3:
                u_high(q, k - 1)
            if k == 3:
                u_high(q, 3)

    lane.loop(3, {"step": 4}, lambda q: quarter(q, False))
    quarter(3, True)
    std(7)


def vector_program(nc, dve, m, d):
    lane = Lane(dve, m.s_dve_step)
    stt = dve.scalar_tensor_tensor

    def low(st, v, g):
        for j in range(4):
            dve.wait_ge(m.s_w_high, 4 * g + j + 1)
            s = (slice(None), j, slice(0, st.kq), slice(0, st.width))
            dve.tensor_tensor(m.lo[s], m.raw[s], m.hi[s].bitcast(F32), ALU.subtract).then_inc(m.s_raw_used, 1)

    def low_unit(name, i, k):
        st = PLAN[name]
        low(st, v_of(st, i, k), st.g0 + 2 * i + k)

    def mod_piece(st, i):
        n, v = st.m0 + i, v_mod(st, i)
        dve.wait_ge(m.s_mod_summed, n + 1)
        dve.wait_ge(m.s_mod_stored, 16 * n + 16)
        for j in range(4):
            dve.wait_ge(m.s_landed[j], 16 * v + 16)
            for kk in range(4):
                c = 4 * j + kk
                if c == 0:
                    ins = dve.tensor_scalar(m.acc[:], m.raw[:, j, kk, :], m.ct[:, c:c + 1], None, ALU.mult)
                else:
                    ins = stt(m.acc[:], m.raw[:, j, kk, :], m.ct[:, c:c + 1], m.acc[:], ALU.mult, ALU.add)
                if kk < 3:
                    lane.link(ins)
                else:
                    ins.then_inc(m.s_raw_used, 1)
                    if j < 3:
                        dve.wait_ge(m.s_raw_used, 4 * v + j + 5)

    def mod_row(st, i):
        n = st.m0 + i
        dve.wait_ge(m.s_mod_summed, n + 2)
        dve.wait_ge(m.s_brow_landed, 16 * n + 16)
        dve.tensor_tensor(m.acc[0:1, :], m.u[0:1, 0, :], m.brow[:], ALU.add).then_inc(m.s_mod_row, 1)

    def gemm(name, take=None, next_too=True):
        st = PLAN[name]

        def after(i, k):
            if take:
                dve.wait_ge(m.s_w_used, 4 * (st.g0 + 2 * i + k) + 8)
                take(st, i, k)

        def turn(i):
            low_unit(name, i, 1)
            if st.mods:
                mod_piece(st, i)
            after(i, 0)
            low_unit(name, i, 2)
            after(i, 1)
            if st.mods:
                mod_row(st, i)

        def tail(i):
            low_unit(name, i, 1)
            if st.mods:
                mod_piece(st, i)
            after(i, 0)
            if next_too:
                low_unit(st.next, 0, 0)
            after(i, 1)
            if st.mods:
                mod_row(st, i)

        gemm_turns(lane, st, {"step": 12} if st.mods else {}, turn, tail)

    def low_columns(k0, uses):
        for q in range(uses):
            n = lane.n["T"]
            dve.wait_ge(m.s_x_high_ready, lane.n["xh"] + 1)
            k = slice(k0 + 2 * q, k0 + 2 * q + 2)
            dve.tensor_tensor(m.xl[:, k, :], m.t[:, n % 2, :].rearrange("p (k t) -> p k t", k=2), m.xh[:, k, :].bitcast(F32), ALU.subtract)\
               .then_inc(m.s_t_free[n % 2], 1)
            lane.n["T"] += 1
            lane.n["xh"] += 1

    def products_kept(name):
        st = PLAN[name]
        used = st.s0 + (4 if st.units == 1 else st.units)
        for b in range(2):
            dve.wait_ge(m.s_g_free[b], used // 2 + 1)

    def rope(x, heads, half, rates, rb, tmp, out=None):
        out = x if out is None else out
        view = [m.cs[:, c, rb, rates:rates + half].unsqueeze(1).unsqueeze(1).broadcast_to((P, heads, 2, half)) for c in range(2)]
        halves = x.rearrange("p h (a e) -> p h a e", a=2)
        by = [tmp[:, c, 0:heads * 2 * half].rearrange("p (h a e) -> p h a e", h=heads, a=2) for c in range(2)]
        for c in range(2):
            lane.did(dve.tensor_tensor(by[c], halves, view[c], ALU.mult))
        lane.sync()
        lane.did(dve.tensor_tensor(out[:, :, 0:half], by[0][:, :, 0, :], by[1][:, :, 1, :], ALU.subtract))
        lane.link(dve.tensor_tensor(out[:, :, half:2 * half], by[1][:, :, 0, :], by[0][:, :, 1, :], ALU.add))

    def inverse_std(n, columns=RB):
        dve.wait_ge(m.s_std_ready, n)
        lane.link(dve.reciprocal(m.rstd[:, 0:columns], m.rstd[:, 0:columns]))

    def spread(n_chunks):
        for rb in range(RB):
            lane.did(dve.bn_aggr(m.mv[:, rb, :], m.st[:, rb, 0:n_chunks, :]))
        lane.sync()

    def mean_square():
        mean, var = m.mv[:, 0:RB, 0], m.mv[:, 0:RB, 1]
        lane.link(dve.tensor_tensor(m.msq[:, 0:RB], mean, mean, ALU.mult))
        stt(m.msq[:, 0:RB], m.msq[:, 0:RB], RMS_EPS, var, ALU.add, ALU.add).then_inc(m.s_var_ready, 1)

    def chunk(c):
        return slice(512 * c, 512 * c + 512)

    dve.wait_ge(m.s_pos_landed, 48)
    lane.link(dve.tensor_copy(m.posf[:], m.posi[:]))
    na = ROT_A + ROT_I
    for rb in range(RB):
        lane.did(dve.tensor_scalar(m.ang[:, rb, 0:na], m.rot[:, 0:na], m.posf[:, rb:rb + 1], None, ALU.mult))
        lane.did(dve.tensor_scalar(m.ang[:, rb, na:], m.rot[:, na:], m.posf[:, RB + rb:RB + rb + 1], None, ALU.mult))
    lane.sync()
    lane.link(dve.tensor_scalar(m.turns[:], m.ang[:], 0.15915494309189535, ROUND, ALU.mult, ALU.add))
    lane.link(dve.tensor_scalar(m.turns[:], m.turns[:], ROUND, None, ALU.subtract))
    for part in (TWO_PI_HI, TWO_PI_MID, TWO_PI_LO):
        lane.link(stt(m.ang[:], m.turns[:], -part, m.ang[:], ALU.mult, ALU.add))
    lane.link(dve.tensor_scalar(m.ang[:], m.ang[:], -3.1415925, 3.1415925, ALU.max, ALU.min))
    lane.link(stt(m.turns[:], m.ang[:], -1.0, m.ang[:], ALU.mult, ALU.max))
    dve.tensor_scalar(m.turns[:], m.turns[:], -1.0, 1.5707963267948966, ALU.mult, ALU.add).then_inc(m.s_angles_ready, 1)
    lane.n["T"] = 1
    low_unit("a_qkv", 0, 0)
    low_columns(0, 8)
    gemm("a_qkv")
    gemm("a_gate")
    gemm("a_idx")

    products_kept("a_idx")
    dve.wait_ge(m.s_sin_ready, 2)
    for rb in range(RB):
        rope(m.pa[:, rb, 0:(NH + NKV) * HD].rearrange("p (h e) -> p h e", e=HD)[:, :, 0:2 * ROT_A], NH + NKV, ROT_A, 0, rb, m.a_rope)
        rope(m.pa[:, rb, 5120:5120 + (IDX_H + 1) * IDX_D].rearrange("p (h e) -> p h e", e=IDX_D)[:, :, 0:2 * ROT_I], IDX_H + 1, ROT_I, ROT_A, rb, m.a_rope)
    dve.memset(m.a_bias0[:, P:T], 0.0)
    dve.tensor_copy(m.a_bias0[:, 0:P], m.tri)
    lane.link(dve.tensor_copy(m.a_bias0[:, T:384], m.tri))
    dve.tensor_copy(m.a_score[:], m.a_bias0[:]).then_inc(m.s_a_ready, 1)
    dve.wait_ge(m.s_a_ready, 1)
    blocks = (slice(0, P), slice(P, 384))

    def index_turn(i):
        for k in range(2):
            t = 2 * i + k
            dve.wait_ge(m.s_a_relu, t + 1)
            for hh in range(2):
                for rb in range(RB):
                    s = m.a_score[:, blocks[rb]]
                    ins = stt(s, m.a_rl[:, k, hh, blocks[rb]], m.a_iws[:, k, rb, hh:hh + 1], s, ALU.mult, ALU.add)
                    if (hh, rb) != (1, 1):
                        lane.did(ins)
                if hh == 0:
                    lane.sync()
            ins.then_inc(m.s_a_idx_done, 1)
            dve.wait_ge(m.s_a_idx_done, t + 3)

    lane.loop(4, {"step": 6}, index_turn)
    for r in range(N_SEL // 8):
        for rb in range(RB):
            lane.did(dve.max(m.a_top[:, rb, :], m.a_score[:, blocks[rb]]))
        lane.sync()
        for rb in range(RB):
            lane.did(dve.match_replace(m.a_score[:, blocks[rb]], m.a_top[:, rb, :], m.a_score[:, blocks[rb]], TAKEN))
        lane.sync()
    lane.link(dve.tensor_scalar(m.a_bias[:], m.a_score[:], -2e38, NEG, ALU.is_gt, ALU.mult))
    dve.tensor_tensor(m.a_bias[:], m.a_bias[:], m.a_bias0[:], ALU.add).then_inc(m.s_a_biased, 1)
    dve.wait_ge(m.s_a_biased, 1)

    def gated(t_bank, og, gate_col, proj, scale=None):
        for rb in range(RB):
            src, gate = m.t[:, t_bank, P * rb:P * rb + P], proj[:, rb, bass.ds(gate_col, HD)]
            if scale is None:
                ins = dve.tensor_tensor(og[:, rb], src, gate, ALU.mult)
            else:
                ins = stt(og[:, rb], src, scale[:, rb:rb + 1], gate, ALU.mult, ALU.mult)
            if rb == 0:
                lane.did(ins)
        return ins

    def head_low(bank, h):
        xl, xh = (x[:, bass.ds(h, 1), :].rearrange("p k t -> p (k t)") for x in (m.xl, m.xh))
        return dve.tensor_tensor(xl, m.t[:, bank, T:2 * T], xh.bitcast(F32), ALU.subtract)

    def a_turn(nxt, cur):
        if nxt:
            t, k = 4 * nxt[0] + nxt[1], nxt[1] % 2
            dve.wait_ge(m.s_a_s, t + 1)
            lane.link(stt(m.a_lg[:, k], m.g[:, 2 + k, 0:384], HD ** -0.5, m.a_bias[:], ALU.mult, ALU.add))
            lane.did(dve.tensor_reduce(m.a_nm[:, k, 0:1], m.a_lg[:, k, blocks[0]], AXX, ALU.max, negate=True))
            dve.tensor_reduce(m.a_nm[:, k, 1:2], m.a_lg[:, k, blocks[1]], AXX, ALU.max, negate=True).then_inc(m.s_a_nmax, 1)
        if cur:
            t, k, h = 4 * cur[0] + cur[1], cur[1] % 2, 4 * cur[1] + cur[0]
            dve.wait_ge(m.s_a_p, 2 * t + 2)
            lane.link(dve.reciprocal(m.a_rs[:, k], m.a_sum[:, k]))
            dve.wait_ge(m.s_a_o, t + 1)
            gated(k, m.a_og, 3072 + HD * h, m.pa, m.a_rs[:, k]).then_inc(m.s_a_ogr, 1)
            dve.wait_ge(m.s_a_xh, t + 1)
            head_low(k, h).then_inc(m.s_a_done, 1)

    heads_in_turn(lane, {"step": 16}, a_turn)

    def norm_and_embed(name_out, name_ple, layer):
        dve.wait_ge(m.s_x_landed, 32)

        def add(st, i, k):
            u, s = 2 * i + k, st.s0 // 2 + i
            stt(m.res[:, :, chunk(u)], m.res[:, :, chunk(u)], ALPHA, m.g[:, 2 * k:2 * k + 2, :], ALU.mult, ALU.add).then_inc(m.s_g_free[k], 1)
            dve.wait_ge(m.s_g_free[k], s + 2)
            for rb in range(RB):
                lane.did(dve.bn_stats(m.st[:, rb, u, :], m.res[:, rb, chunk(u)]))

        gemm(name_out, add)
        lane.sync()
        spread(4)
        dve.tensor_scalar(m.msq[:, 0:RB], m.mv[:, 0:RB, 1], LN_EPS, None, ALU.add).then_inc(m.s_var_ready, 1)
        dve.wait_ge(m.s_rows_landed, 32 * (layer + 1))
        inverse_std(layer + 1)
        for c in range(4):
            x = [m.res[:, rb, chunk(c)] for rb in range(RB)]
            for rb in range(RB):
                lane.did(stt(x[rb], x[rb], m.mv[:, rb, 0:1], m.row_g[:, chunk(c)], ALU.subtract, ALU.mult))
            lane.sync()
            for rb in range(RB):
                stt(x[rb], x[rb], m.rstd[:, rb:rb + 1], m.row_b[:, chunk(c)], ALU.mult, ALU.add).then_inc(m.s_y_ready, 1)
                lane.n["y"] += 1
            if c:
                low_columns(4 * c - 4, 2)
        low_columns(12, 2)
        lane.n["T"] += 1
        dve.wait_ge(m.s_y_ready, lane.n["y"])

        def embed(st, i, k):
            u, s = 2 * i + k, st.s0 // 2 + i
            x = m.res[:, :, chunk(u)]
            dve.wait_ge(m.s_g_free[k], s + 2)
            dve.wait_ge(m.s_ple_full, 4 * layer + u + 1)
            dve.tensor_tensor(m.ple_s[:, k], m.ple_s[:, k], m.u[:], ALU.mult).then_inc(m.s_ple_free, 1)
            dve.wait_ge(m.s_ple_free, 4 * layer + u + 2)
            ins = dve.tensor_tensor(x, x, m.ple_s[:, k], ALU.add)
            if layer == 0:
                ins.then_inc(m.s_y_ready, 1)
                lane.n["y"] += 1
            else:
                ins.then_inc(m.s_x4_ready, 1)
                dve.wait_ge(m.s_x4_ready, u + 1)
                for rb in range(RB):
                    lane.did(dve.bn_stats(m.st[:, rb, u, :], m.res[:, rb, chunk(u)]))

        gemm(name_ple, embed)

    norm_and_embed("a_out", "ple0", 0)
    low_columns(0, 8)
    gemm("b_kvq")
    gemm("b_gate")

    products_kept("b_gate")
    dve.tensor_copy(m.b_mask[:, 0:P], m.lt)
    dve.tensor_copy(m.b_mask[:, P:T], m.ones)
    dve.tensor_copy(m.b_mask[:, T:384], m.lt).then_inc(m.s_b_ready, 1)
    dve.wait_ge(m.s_b_ready, 1)

    def b_turn(nxt, cur):
        if cur:
            tc, kc, h = 4 * cur[0] + cur[1], cur[1] % 2, 4 * cur[1] + cur[0]
            dve.wait_ge(m.s_b_o, tc + 1)
            gated(kc, m.b_og, 3072 + HD * h, m.pb).then_inc(m.s_b_ogr, 1)
        if nxt:
            t, k = 4 * nxt[0] + nxt[1], nxt[1] % 2
            z = m.g[:, 2 + k, 0:384]
            dve.wait_ge(m.s_b_abs, t + 1)
            lane.link(dve.tensor_scalar(m.b_sp[:], z, HD ** -0.5, 0.0, ALU.mult, ALU.max))
            dve.wait_ge(m.s_b_l, t + 1)
            lane.link(dve.tensor_tensor(m.b_sp[:], m.b_sp[:], m.b_e[:], ALU.add))
            stt(m.b_lom[:], m.b_sp[:], -1.0, m.b_mask[:], ALU.mult, ALU.mult).then_inc(m.s_b_lomr, 1)
            lane.did(stt(m.b_sp[:], z, HD ** -0.5, m.b_sp[:], ALU.mult, ALU.subtract))
        if cur:
            dve.wait_ge(m.s_b_xh, tc + 1)
            head_low(kc, h).then_inc(m.s_b_done, 1)
        if nxt:
            lane.sync()
            dve.wait_ge(m.s_b_sfx, t + 1)
            dve.tensor_tensor(m.b_a[:, 0], m.b_sp[:], m.u[:, k, 0:384], ALU.add).then_inc(m.s_b_a1, 1)
            dve.wait_ge(m.s_b_ex, t + 1)
            dve.tensor_tensor(m.b_a[:, 0], m.b_a[:, 0], m.b_mask[:], ALU.mult).then_inc(m.s_b_w, 1)

    heads_in_turn(lane, {"step": 16}, b_turn)
    norm_and_embed("b_out", "ple1", 1)

    def normed(x, gain, shift, out):
        for c in range(4):
            for rb in range(RB):
                lane.did(stt(out[:, rb, chunk(c)], x[:, rb, chunk(c)], m.rstd[:, rb:rb + 1], gain[:, chunk(c)], ALU.mult, ALU.mult))
            lane.sync()
            o = out[:, :, chunk(c)]
            dve.tensor_tensor(o, o, shift[:, chunk(c)].unsqueeze(1).broadcast_to((P, RB, 512)), ALU.add).then_inc(m.s_y_ready, 1)
            lane.n["y"] += 1
            if c:
                low_columns(4 * c - 4, 2)
        low_columns(12, 2)

    lane.sync()
    spread(4)
    mean_square()
    dve.wait_ge(m.s_rows2_landed, 48)
    lane.link(stt(m.c_g1[:], m.c_sc[:], 1.0, m.c_g1[:], ALU.add, ALU.mult))
    inverse_std(3)
    normed(m.res, m.c_g1, m.c_sh, m.c_h)
    for name in ("c_hq", "c_f", "c_hi", "c_hg", "c_mla"):
        gemm(name)

    products_kept("c_mla")
    parts = ((slice(0, QRANK), 0), (slice(QRANK, QRANK + KVRANK), RB))
    for s, n in parts:
        for rb in range(RB):
            lane.did(dve.bn_stats(m.st[:, rb, n // RB, :], m.pm[:, rb, s]))
    lane.sync()
    for s, n in parts:
        for rb in range(RB):
            lane.did(dve.bn_aggr(m.mv[:, n + rb, :], m.st[:, rb, n // RB:n // RB + 1, :]))
    lane.sync()
    lane.link(dve.tensor_tensor(m.msq[:], m.mv[:, :, 0], m.mv[:, :, 0], ALU.mult))
    stt(m.msq[:], m.msq[:], RMS_EPS, m.mv[:, :, 1], ALU.add, ALU.add).then_inc(m.s_var_ready, 1)
    dve.wait_ge(m.s_mod_stored, 16 * (PLAN["c_mla"].m0 + 1) + 16)
    lane.link(dve.memset(m.m_krd[:], 0.0))
    for rb in range(RB):
        rope(m.pm[:, rb:rb + 1, QRANK + KVRANK:], 1, ROT_M, na, rb, m.m_rope, m.m_krd[:, rb:rb + 1, 0:ROPE])
    dve.wait_ge(m.s_rows2_landed, 80)
    inverse_std(4, 2 * RB)
    for s, n in parts:
        for rb in range(RB):
            ins = stt(m.pm[:, rb, s], m.pm[:, rb, s], m.rstd[:, n + rb:n + rb + 1], m.m_rg[:, s], ALU.mult, ALU.mult)
            if n + rb < 2 * RB - 1:
                lane.did(ins)
    ins.then_inc(m.s_y_ready, 1)
    lane.n["y"] += 1
    low_columns(8, 3)
    ukv = PLAN["ukv"]
    low(ukv, ukv.v0, ukv.g0)
    products_kept("uq")
    dve.wait_ge(m.s_raw_used, 4 * ukv.v0 + 8)
    for rb in range(RB):
        rope(m.mq[:, rb, :].rearrange("p (h e) -> p h e", e=NOPE + ROPE)[:, :, NOPE:], MH, ROT_M, na, rb, m.m_rope2)
    products_kept("ukv")
    dve.memset(m.m_nm[:], 0.0).then_inc(m.s_m_ready, 1)
    dve.wait_ge(m.s_m_ready, 1)
    mscale = (NOPE + ROPE) ** -0.5

    def m_turn(nxt, cur):
        if nxt:
            t, k = 2 * nxt[0] + nxt[1], nxt[1]
            dve.wait_ge(m.s_m_s, t + 1)
            lane.link(dve.tensor_reduce(m.m_nm[:, k], m.g[:, 2 + k, :].rearrange("p (r s) -> p r s", r=RB), AXX, ALU.max, negate=True))
            dve.tensor_scalar(m.m_nm[:, k], m.m_nm[:, k], mscale, None, ALU.mult).then_inc(m.s_m_nmax, 1)
        if cur:
            t, k = 2 * cur[0] + cur[1], cur[1]
            dve.wait_ge(m.s_m_p, 2 * t + 2)
            lane.link(dve.reciprocal(m.m_rs[:, k], m.m_sum[:, k]))
            dve.wait_ge(m.s_m_o, t + 1)
            for rb in range(RB):
                ins = dve.tensor_scalar(m.m_og[:, rb], m.t[:, k, P * rb:P * rb + P], m.m_rs[:, k, rb:rb + 1], None, ALU.mult)
                if rb == 0:
                    lane.did(ins)
            ins.then_inc(m.s_m_ogr, 1)
            dve.wait_ge(m.s_m_xh, t + 1)
            head_low(k, t).then_inc(m.s_m_done, 1)

    heads_in_turn(lane, {"step": 6}, m_turn, MH // 2, 2)

    dve.wait_ge(m.s_h_rows, 80)
    dve.tensor_tensor(m.h_l0[:, 0], m.h_l0[:, 0], m.h_l0[:, 1], ALU.subtract).then_inc(m.s_h_lb, 1)
    f = m.pc[:, :, 1024:3072]
    lane.link(dve.tensor_scalar(m.h_t[:], f, -1.0, 1.0, ALU.mult, ALU.add))
    dve.wait_ge(m.s_h_lbs, 1)
    bound = m.h_l0[:, 0].rearrange("p a b -> p (a b)").unsqueeze(1).broadcast_to((P, RB, 2048))
    lane.link(dve.tensor_tensor(m.h_t[:], m.h_t[:], bound, ALU.mult))
    for rb in range(RB):
        dve.tensor_tensor(f[:, rb], f[:, rb], m.h_t[:, rb], ALU.add).then_inc(m.s_h_fr, 1)
    dve.wait_ge(m.s_h_consts, 32)

    def decayed(t, group):
        for l in range(4):
            half = P >> (4 * group + l)

            def side(ap, s):
                return ap.rearrange("p (b s h) -> p b s h", s=2, h=half)[:, :, s, :]

            e = [m.h_e[:, dr, l] for dr in range(2)]
            for s in range(2):
                lane.did(dve.tensor_tensor(side(m.h_kq[:, 0, l], s), side(m.h_kt[:, s], s), side(e[s], s), ALU.mult))
                ins = dve.tensor_tensor(side(m.h_kq[:, 1, l], s), side(m.h_qt[:], s), side(e[1 - s], s), ALU.mult)
                if (l, s) != (3, 1):
                    lane.did(ins)
        ins.then_inc(m.s_h_mul, 1)

    def masked(levels, n0):
        n = len(levels)
        return dve.tensor_tensor(m.h_tm[:, :, n0:n0 + n, :], m.t[:, :, 0:P * n].rearrange("p b (l t) -> p b l t", l=n),
                                 m.h_mask[:, n0:n0 + n, :].unsqueeze(1).broadcast_to((P, RB, n, P)), ALU.mult)

    def h_head(t):
        dve.wait_ge(m.s_h_tr, t + 1)
        lane.link(dve.tensor_scalar(m.h_kt[:].rearrange("p a t -> p (a t)"), m.g[:, 1, :], -1.0, 1.0, ALU.mult, ALU.add))
        dve.tensor_tensor(m.h_ks[:], m.h_kt[:, 0], m.h_kt[:, 1], ALU.add).then_inc(m.s_h_kc, 1)
        dve.wait_ge(m.s_h_qc, t + 1)
        dve.wait_ge(m.s_h_ex, 8 * t + 4)
        decayed(t, 0)
        dve.wait_ge(m.s_h_am, 3 * t + 1)
        lane.did(masked(range(3), 0))
        dve.memset(m.h_r[:], 0.0).then_inc(m.s_h_msk, 1)
        dve.wait_ge(m.s_h_ex, 8 * t + 8)
        decayed(t, 1)
        dve.wait_ge(m.s_h_am, 3 * t + 3)
        lane.did(masked(range(4), 3))
        lane.link(dve.tensor_tensor(m.h_tm[:, :, 7, :], m.g[:, 1, 0:T].rearrange("p (b t) -> p b t", b=RB),
                                    m.h_mask[:, 7:8, :].broadcast_to((P, RB, P)), ALU.mult))
        lane.did(dve.tensor_reduce(m.h_at[:, 0], m.h_tm[:, 0].rearrange("p l t -> p t l"), AXX, ALU.add))
        dve.tensor_reduce(m.h_at[:, 3], m.h_tm[:, 1].rearrange("p l t -> p t l"), AXX, ALU.add).then_inc(m.s_h_red, 1)

    lane.loop(HH, {"step": 35}, h_head)
    dve.wait_ge(m.s_h_oc, HH + 1)
    o = m.pc[:, :, 0:1024]
    lane.link(dve.tensor_tensor(m.h_sq[:], o, o, ALU.mult))
    lane.link(dve.tensor_reduce(m.h_ms[:], m.h_sq[:].rearrange("p r (h e) -> p r h e", h=HH), AXX, ALU.add))
    dve.tensor_scalar(m.h_ms[:], m.h_ms[:], 1.0 / HD, RMS_EPS, ALU.mult, ALU.add).then_inc(m.s_h_ms1, 1)
    dve.wait_ge(m.s_h_std, 1)
    lane.link(dve.reciprocal(m.h_r[:], m.h_r[:]))
    for rb in range(RB):
        heads = o[:, rb].rearrange("p (h e) -> p h e", h=HH)
        lane.link(dve.tensor_tensor(heads, heads, m.h_r[:, rb].unsqueeze(2).broadcast_to((P, HH, HD)), ALU.mult))
        lane.link(dve.tensor_tensor(heads, heads, m.h_ng[:].unsqueeze(1).broadcast_to((P, HH, HD)), ALU.mult))
    dve.tensor_tensor(o, o, m.pc[:, :, 4096:5120], ALU.mult).then_inc(m.s_y_ready, 1)
    lane.n["y"] += 1
    low_columns(8, 4)

    low_unit("c_out", 0, 0)

    def keep_mix(st, i, k):
        u, s = 2 * i + k, st.s0 // 2 + i
        dve.tensor_copy(m.mix[:, :, chunk(u)], m.g[:, 2 * k:2 * k + 2, :]).then_inc(m.s_g_free[k], 1)
        dve.wait_ge(m.s_g_free[k], s + 2)
        for rb in range(RB):
            lane.did(dve.bn_stats(m.st[:, rb, u, :], m.mix[:, rb, chunk(u)]))

    def into_residual(y, gain, stats):
        for c in range(4):
            for rb in range(RB):
                lane.did(stt(y[:, rb, chunk(c)], y[:, rb, chunk(c)], m.rstd[:, rb:rb + 1], gain[:, chunk(c)], ALU.mult, ALU.mult))
            lane.sync()
            ins = dve.tensor_tensor(m.res[:, :, chunk(c)], m.res[:, :, chunk(c)], y[:, :, chunk(c)], ALU.add)
            if stats:
                lane.link(ins)
                for rb in range(RB):
                    lane.did(dve.bn_stats(m.st[:, rb, c, :], m.res[:, rb, chunk(c)]))
            else:
                ins.then_inc(m.s_mlp_done, 1)

    gemm("c_out", keep_mix)
    lane.sync()
    spread(4)
    mean_square()
    dve.wait_ge(m.s_rows2_landed, 160)
    lane.did(dve.tensor_tensor(m.x_pg[:], m.x_pg[:], m.x_ga[:], ALU.mult))
    lane.did(stt(m.x_g1[:], m.x_sc[:], 1.0, m.x_g1[:], ALU.add, ALU.mult))
    dve.wait_ge(m.s_res2_landed, 16)
    inverse_std(5)
    into_residual(m.mix, m.x_pg, True)
    lane.sync()
    spread(4)
    mean_square()
    inverse_std(6)
    normed(m.res, m.x_g1, m.x_sh, m.mix)

    lane.link(dve.memset(m.y[:], 0.0))
    mlp = PLAN["mlp"]
    t0, x0 = lane.n["T"], lane.n["xh"]

    def hidden_low(q, k):
        for half in range(2):
            b = (t0 + half) % 2
            dve.wait_ge(m.s_x_high_ready, x0 + 8 * q + 2 * k + half + 1)
            s = slice(4 * k + 2 * half, 4 * k + 2 * half + 2)
            dve.tensor_tensor(m.ul[:, s, :], m.t[:, b, :].rearrange("p (k t) -> p k t", k=2), m.uh[:, s, :].bitcast(F32), ALU.subtract)\
               .then_inc(m.s_t_free[b], 1)

    def hidden_quarter(q, last):
        for k in range(8):
            if k < 7 or not last:
                low(mlp, mlp.v0 + 8 * q + k + 1, mlp.g0 + 8 * q + k + 1)
            if 1 <= k <= 3:
                hidden_low(q, k - 1)
            if k == 3:
                hidden_low(q, 3)
            if k >= 4:
                dve.wait_ge(m.s_w_used, 4 * (mlp.g0 + 8 * q + k) + 8)
                y = m.y[:, :, chunk(k - 4)]
                dve.tensor_tensor(y, y, m.g[:, 2 * (k % 2):2 * (k % 2) + 2, :], ALU.add).then_inc(m.s_g_free[k % 2], 1)

    lane.loop(3, {}, lambda q: hidden_quarter(q, False))
    hidden_quarter(3, True)
    products_kept("mlp")
    for c in range(4):
        for rb in range(RB):
            lane.did(dve.bn_stats(m.st[:, rb, c, :], m.y[:, rb, chunk(c)]))
    lane.sync()
    spread(4)
    mean_square()
    dve.wait_ge(m.s_rows2_landed, 192)
    lane.link(dve.tensor_tensor(m.z_pg[:], m.z_pg[:], m.z_gm[:], ALU.mult))
    inverse_std(7)
    into_residual(m.y, m.z_pg, False)


def tensor_program(nc, pe, m, d):
    lane = Lane(pe, m.s_pe_step)

    def quarter(st, v, g, j, pair, x0, first, last, xh=m.xh, xl=m.xl):
        pe.wait_ge(m.s_raw_used, 4 * v + j + 5)
        for kk in range(st.kq):
            for rb in range(RB):
                a, w = slice(P * rb, P * rb + P), (j, kk, slice(0, st.width))
                bank = m.g[:, 2 * pair + rb, 0:st.width]
                parts = ((xh, m.hi), (xh, m.lo), (xl, m.hi))
                for n, (x, wt) in enumerate(parts):
                    ins = pe.matmul(bank, x[:, x0 + kk, a], wt[(slice(None),) + w],
                                    start=first and kk == 0 and n == 0, stop=last and kk == st.kq - 1 and n == 2)
        ins.then_inc(m.s_w_used, 1)

    def unit(st, v, g, half_s, pair, xh=m.xh, xl=m.xl):
        pe.wait_ge(m.s_g_free[pair], half_s + 1)
        for j in range(4):
            quarter(st, v, g, j, pair, 4 * j, j == 0, j == 3, xh, xl)

    def gemm(name, after=None):
        st = PLAN[name]

        def pair(i):
            for k in range(2):
                unit(st, v_of(st, i, k), st.g0 + 2 * i + k, st.s0 // 2 + i, k)
                if after:
                    after(2 * i + k)
            if st.mods:
                pe.wait_ge(m.s_raw_used, 4 * v_mod(st, i) + 8)
                pe.matmul(m.u[0:1, 0, :], m.ones[:, 0:1], m.acc[:], start=True, stop=True).then_inc(m.s_mod_summed, 1)

        lane.loop(st.units // 2, {}, pair)

    def bank_for_columns():
        n = lane.n["T"]
        pe.wait_ge(m.s_t_free[n % 2], n // 2 + 1)
        lane.n["T"] += 1
        return n % 2

    def blocks(b, src):
        for kt in range(2):
            for rb in range(RB):
                ins = pe.transpose(m.t[:, b, T * kt + P * rb:T * kt + P * rb + P], src(kt, rb), m.ident)
        ins.then_inc(m.s_t_full[b], 1)

    def columns(x, uses, y_total=0, per_chunk=0):
        base = lane.n["y"]
        for q in range(uses):
            if per_chunk:
                pe.wait_ge(m.s_y_ready, base + per_chunk * (q // 2 + 1))
            b = bank_for_columns()
            blocks(b, lambda kt, rb: x[:, rb, T * q + P * kt:T * q + P * kt + P])
        lane.n["y"] += y_total

    def columns_split():
        n = lane.n["T"]
        for b in range(2):
            pe.wait_ge(m.s_t_free[b], (n + 1 - b) // 2 + 1)

    def pieces(dst, src, n, sem):
        for a in range(n):
            ins = pe.transpose(dst(a), src(a), m.ident)
        ins.then_inc(sem, 1)

    pe.wait_ge(m.s_const_landed, 32)
    b = bank_for_columns()
    pe.transpose(m.t[:, b, 0:KT], m.crow[:], m.const[0:KT, C_IDENT:C_IDENT + KT]).then_inc(m.s_t_full[b], 1)
    pe.wait_ge(m.s_x_landed, 16)
    columns(m.res, 8)
    columns_split()
    gemm("a_qkv")
    gemm("a_gate")
    gemm("a_idx")

    def keys(src, col0):
        for kv in range(NKV):
            for rb in range(RB):
                c = T * (kv % 2) + P * rb
                ins = pe.transpose(m.g[:, 2 + kv // 2, c:c + P], src[:, rb, col0 + HD * kv:col0 + HD * kv + HD], m.ident)
        return ins

    pe.wait_ge(m.s_a_ready, 1)
    keys(m.pa, 2048).then_inc(m.s_a_ktp, 1)
    pe.wait_ge(m.s_a_k_t, 2)
    pieces(lambda rb: m.g[:, 0, P * rb:P * rb + P], lambda rb: m.a_ikd[:, rb].rearrange("p a e -> p (a e)"), RB, m.s_a_ktp)
    pe.wait_ge(m.s_a_k_copied, 2)
    index_banks = [[m.g[:, 2], m.g[:, 3]], [m.u[:, 0], m.u[:, 1]]]

    def index_turn(nxt, cur):
        if nxt:
            t, k = 2 * nxt[0] + nxt[1], nxt[1]
            pe.wait_ge(m.s_a_iq, 2 * t + 2)
            pieces(lambda rb: m.g[:, k, P * rb:P * rb + P], lambda rb: m.a_iqs[:, k, rb], RB, m.s_a_iqt)
        if cur:
            t, k = 2 * cur[0] + cur[1], cur[1]
            pe.wait_ge(m.s_a_iqc, t + 1)
            for hh in range(2):
                e = slice(IDX_D * hh, IDX_D * hh + IDX_D)
                pe.matmul(index_banks[k][hh][:, 0:P], m.a_iqt[e, k, 0:P], m.a_ikt[e, 0:P], start=True, stop=True)
                ins = pe.matmul(index_banks[k][hh][:, P:384], m.a_iqt[e, k, P:T], m.a_ikt[e, :], start=True, stop=True)
            ins.then_inc(m.s_a_dots, 1)

    heads_in_turn(lane, {}, index_turn, IDX_H // 4, 2)

    def attend(probs, v, out):
        pe.matmul(out[:, 0:P], probs[:, 0:P], v(0), start=True, stop=True)
        pe.matmul(out[:, P:T], probs[:, P:T], v(0), start=True, stop=False)
        return pe.matmul(out[:, P:T], probs[:, T:384], v(1), start=False, stop=True)

    def a_turn(nxt, cur):
        if nxt:
            t, kv, k = 4 * nxt[0] + nxt[1], nxt[1], nxt[1] % 2
            pe.wait_ge(m.s_a_q, t + 1)
            pieces(lambda rb: m.g[:, k, P * rb:P * rb + P], lambda rb: m.a_qs[:, k, rb], RB, m.s_a_qtp)
            pe.wait_ge(m.s_a_qtc, t + 1)
            pe.matmul(m.g[:, 2 + k, 0:P], m.a_qt[:, k, 0:P], m.a_kt[:, kv, 0:P], start=True, stop=True)
            pe.matmul(m.g[:, 2 + k, P:384], m.a_qt[:, k, P:T], m.a_kt[:, kv, :], start=True, stop=True).then_inc(m.s_a_s, 1)
        if cur:
            t, kv, k = 4 * cur[0] + cur[1], cur[1], cur[1] % 2
            pe.wait_ge(m.s_a_p, 2 * t + 2)
            pieces(lambda a: m.u[:, k, P * a:P * a + P], lambda a: m.a_lg[:, k, P * a:P * a + P], 3, m.s_a_ptp)
            pe.wait_ge(m.s_a_ptc, t + 1)
            v = 2560 + HD * kv
            attend(m.a_pt[:, k], lambda s: m.pa[:, s, v:v + HD], m.t[:, k]).then_inc(m.s_a_o, 1)
            pe.wait_ge(m.s_a_ogr, t + 1)
            pieces(lambda rb: m.t[:, k, T + P * rb:T + P * rb + P], lambda rb: m.a_og[:, rb], RB, m.s_a_ogt)

    heads_in_turn(lane, {}, a_turn)
    pe.wait_ge(m.s_a_done, NH + 2)

    def norm_and_embed(name_out, name_ple, layer):
        gemm(name_out)
        columns(m.res, 8, 8, 2)
        pe.wait_ge(m.s_ple_landed, 32 * (layer + 1))
        blocks(bank_for_columns(), lambda kt, rb: m.ple_p[:, rb, P * kt:P * kt + P])
        columns_split()

        def embed(u):
            pe.wait_ge(m.s_ple_free, 4 * layer + u + 1)
            for rb in range(RB):
                for k in range(2):
                    ins = pe.matmul(m.u[:, rb, :], m.ple_pt[:, k, P * rb:P * rb + P], m.ple_w[:, k, bass.ds(512 * u, 512)],
                                    start=k == 0, stop=k == 1)
            ins.then_inc(m.s_ple_full, 1)

        gemm(name_ple, embed)

    norm_and_embed("a_out", "ple0", 0)
    columns(m.res, 8, 4, 1)
    columns_split()
    gemm("b_kvq")
    gemm("b_gate")

    pe.wait_ge(m.s_b_ready, 1)
    keys(m.pb, 0).then_inc(m.s_b_k_t, 1)
    pe.wait_ge(m.s_b_k_copied, 1)

    def b_turn(nxt, cur):
        if nxt:
            t, kv, k = 4 * nxt[0] + nxt[1], nxt[1], nxt[1] % 2
            pe.wait_ge(m.s_b_q, t + 1)
            pieces(lambda rb: m.g[:, k, P * rb:P * rb + P], lambda rb: m.b_qs[:, k, rb], RB, m.s_b_qtp)
            pe.wait_ge(m.s_b_qtc, t + 1)
            pe.matmul(m.g[:, 2 + k, 0:T], m.b_kt[:, kv, 0:P], m.b_qt[:, 0, :], start=True, stop=True)
            pe.matmul(m.g[:, 2 + k, T:384], m.b_kt[:, kv, P:T], m.b_qt[:, 0, P:T], start=True, stop=True).then_inc(m.s_b_z, 1)
        if cur:
            tc, kvc, kc = 4 * cur[0] + cur[1], cur[1], cur[1] % 2
            pe.wait_ge(m.s_b_w, tc + 1)
            v = 512 + HD * kvc
            attend(m.b_a[:, 0], lambda s: m.pb[:, s, v:v + HD], m.t[:, kc]).then_inc(m.s_b_o, 1)
            pe.wait_ge(m.s_b_ogr, tc + 1)
            pieces(lambda rb: m.t[:, kc, T + P * rb:T + P * rb + P], lambda rb: m.b_og[:, rb], RB, m.s_b_ogt)
        if nxt:
            pe.wait_ge(m.s_b_lomr, t + 1)
            pe.matmul(m.u[:, k, 0:P], m.gt, m.b_lom[:, 0:P], start=True, stop=True)
            pe.matmul(m.u[:, k, P:T], m.gt, m.b_lom[:, P:T], start=True, stop=False)
            pe.matmul(m.u[:, k, P:T], m.ones, m.b_lom[:, T:384], start=False, stop=True)
            pe.matmul(m.u[:, k, T:384], m.gt, m.b_lom[:, T:384], start=True, stop=True).then_inc(m.s_b_sfx, 1)

    heads_in_turn(lane, {}, b_turn)
    pe.wait_ge(m.s_b_done, NH + 2)
    norm_and_embed("b_out", "ple1", 1)
    columns(m.c_h, 8, 4, 1)
    columns_split()
    for name in ("c_hq", "c_f", "c_hi", "c_hg", "c_mla"):
        gemm(name)
    pe.wait_ge(m.s_y_ready, lane.n["y"] + 1)
    columns(m.pm, 3, 1)
    columns_split()
    for name, x0 in (("uq", 8), ("ukv", 12)):
        st = PLAN[name]
        for j in range(4):
            pe.wait_ge(m.s_g_free[j % 2], (st.s0 + j) // 2 + 1)
            quarter(st, st.v0, st.g0, j, j % 2, x0, True, True)
    pe.wait_ge(m.s_m_ready, 1)
    pieces(lambda rb: m.t[:, 0, P * rb:P * rb + P], lambda rb: m.m_krd[:, rb], RB, m.s_m_krt_t)
    pe.wait_ge(m.s_m_krt_c, 1)

    def m_turn(nxt, cur):
        if nxt:
            t, k = 2 * nxt[0] + nxt[1], nxt[1]
            pe.wait_ge(m.s_m_q, 2 * t + 2)
            for part in range(2):
                for rb in range(RB):
                    c = T * part + P * rb
                    pe.transpose(m.g[:, k, c:c + P], m.m_qs[:, k, rb, P * part:P * part + P], m.ident)
            pieces(lambda rb: m.t[:, k, P * rb:P * rb + P], lambda rb: m.m_ks[:, k, rb], RB, m.s_m_qtp)
            pe.wait_ge(m.s_m_qtc, 2 * t + 2)
            for rb in range(RB):
                rows_ = slice(P * rb, P * rb + P)
                pe.matmul(m.g[:, 2 + k, T * rb:T * rb + T], m.m_qt[:, k, 0, rows_], m.m_ktt[:, k], start=True, stop=False)
                ins = pe.matmul(m.g[:, 2 + k, T * rb:T * rb + T], m.m_qt[:, k, 1, rows_], m.m_krt[:], start=False, stop=True)
            ins.then_inc(m.s_m_s, 1)
        if cur:
            t, k = 2 * cur[0] + cur[1], cur[1]
            pe.wait_ge(m.s_m_p, 2 * t + 2)
            pieces(lambda a: m.u[:, k, P * a:P * a + P], lambda a: m.m_lg[:, k, a // 2, P * (a % 2):P * (a % 2) + P], 4, m.s_m_ptp)
            pe.wait_ge(m.s_m_ptc, t + 1)
            for rb in range(RB):
                for s in range(RB):
                    ins = pe.matmul(m.t[:, k, P * rb:P * rb + P], m.m_pt[:, k, rb, P * s:P * s + P],
                                    m.mkv[:, s, bass.ds((NOPE + VD) * t + NOPE, VD)], start=s == 0, stop=s == 1)
            ins.then_inc(m.s_m_o, 1)
            pe.wait_ge(m.s_m_ogr, t + 1)
            pieces(lambda rb: m.t[:, k, T + P * rb:T + P * rb + P], lambda rb: m.m_og[:, rb], RB, m.s_m_ogt)

    heads_in_turn(lane, {}, m_turn, MH // 2, 2)
    pe.wait_ge(m.s_m_done, MH + 2)
    pe.wait_ge(m.s_h_consts, 32)

    def spans(group):
        for dr in range(2):
            for blk, bank in enumerate(((m.g[:, 2], m.g[:, 3]), (m.u[:, 0], m.u[:, 1]))[dr]):
                lf = m.h_lf[:, dr, blk, :]
                if group:
                    ins = pe.matmul(bank, lf, m.h_md[:, dr, 5:9, :].rearrange("p l t -> p (l t)"), start=True, stop=True)
                elif blk == 0:
                    ins = pe.matmul(bank, lf, m.h_md[:, dr, 0:4, :].rearrange("p l t -> p (l t)"), start=True, stop=True)
                else:
                    pe.matmul(bank[:, 0:P], lf, m.h_md[:, dr, 4, :], start=True, stop=True)
                    ins = pe.matmul(bank[:, P:512], lf, m.h_md[:, dr, 1:4, :].rearrange("p l t -> p (l t)"), start=True, stop=True)
        ins.then_inc(m.s_h_d, 1)

    def block_products(levels):
        for blk in range(RB):
            b = slice(P * blk, P * blk + P)
            for n, l in enumerate(levels):
                ins = pe.matmul(m.t[:, blk, P * n:P * n + P], m.h_kq[:, 0, l, b], m.h_kq[:, 1, l, b], start=True, stop=True)
        ins.then_inc(m.s_h_am, 1)

    def h_head(t):
        pe.wait_ge(m.s_h_q, 3 * t + 3)
        for rb in range(RB):
            pe.transpose(m.g[:, 0, P * rb:P * rb + P], m.h_qs[:, rb], m.ident)
        pieces(lambda a: m.g[:, 1, P * a:P * a + P], lambda a: m.h_fs[:, a // 2, a % 2], 4, m.s_h_tr)
        pe.wait_ge(m.s_h_logf, t + 1)
        spans(0)
        pe.wait_ge(m.s_h_mul, 2 * t + 1)
        spans(1)
        pe.matmul(m.g[:, 0, 0:P], m.h_kq[:, 0, 0, 0:P], m.h_kq[:, 1, 0, P:T], start=True, stop=True)
        pe.matmul(m.g[:, 0, P:T], m.h_kq[:, 0, 0, P:T], m.h_kq[:, 1, 0, 0:P], start=True, stop=True)
        block_products(range(1, 4))
        pe.wait_ge(m.s_h_mul, 2 * t + 2)
        pe.wait_ge(m.s_h_msk, t + 1)
        block_products(range(4))
        pe.wait_ge(m.s_h_kc, t + 1)
        for blk in range(RB):
            b = slice(P * blk, P * blk + P)
            ins = pe.matmul(m.g[:, 1, b], m.h_ks[:, b], m.h_qt[:, b], start=True, stop=True)
        ins.then_inc(m.s_h_am, 1)
        pe.wait_ge(m.s_h_red, t + 1)
        pe.wait_ge(m.s_h_off, t + 1)
        for blk in range(RB):
            for s in range(RB):
                ins = pe.matmul(m.g[:, 2, P * blk:P * blk + P], m.h_at[:, 2 * s + blk, :], m.pc[:, s, bass.ds(3072 + HD * t, HD)],
                                start=s == 0, stop=s == 1)
        ins.then_inc(m.s_h_o, 1)

    lane.loop(HH, {}, h_head)
    pe.wait_ge(m.s_y_ready, lane.n["y"] + 1)
    columns(m.pc, 4, 1)
    columns_split()
    gemm("c_out")
    columns(m.mix, 8, 4, 1)
    columns_split()

    mlp = PLAN["mlp"]
    t0 = lane.n["T"]

    def hidden_columns(q, k):
        pe.wait_ge(m.s_g_free[k % 2], mlp.s0 // 2 + 4 * q + k // 2 + 2)
        for half in range(2):
            b = (t0 + half) % 2
            pe.wait_ge(m.s_t_free[b], (t0 + half) // 2 + 4 * q + k + 1)
            blocks(b, lambda kt, rb: m.ur[:, k % 2, rb, T * half + P * kt:T * half + P * kt + P])

    def hidden_quarter(q):
        for k in range(8):
            if k == 4:
                for half in range(2):
                    pe.wait_ge(m.s_t_free[(t0 + half) % 2], (t0 + half) // 2 + 4 * q + 5)
            xs = (m.xh, m.xl) if k < 4 else (m.uh, m.ul)
            unit(mlp, mlp.v0 + 8 * q + k, mlp.g0 + 8 * q + k, mlp.s0 // 2 + 4 * q + k // 2, k % 2, *xs)
            if 1 <= k <= 3:
                hidden_columns(q, k - 1)
            if k == 3:
                hidden_columns(q, 3)

    lane.loop(4, {}, hidden_quarter)


def shape_constants():
    import numpy as np

    i = np.arange(P)
    s, t = i[:, None], i[None, :]
    const = np.concatenate([np.eye(P), np.ones((P, P)), np.where(t <= s, 0.0, NEG), s < t, s > t], axis=1)

    def inverse(base, half):
        return 1.0 / np.float32(base) ** (np.arange(half, dtype=np.float32) / np.float32(half))

    rates = np.tile(np.concatenate([inverse(500000.0, ROT_A), inverse(500000.0, ROT_I), inverse(10000.0, ROT_M)]), (P, 1))
    tau, spans = s, np.zeros((P, 2, 9, P))

    def span(mid, right):
        fwd = np.where(right, (mid <= tau) & (tau <= t), (t < tau) & (tau < mid))
        bwd = np.where(right, (mid <= tau) & (tau < t), (t <= tau) & (tau < mid))
        return fwd, bwd

    def level(l):
        half = P >> l
        return span(t // (2 * half) * (2 * half) + half, t % (2 * half) >= half)

    order = [span(P, np.zeros((1, P), bool))] + [level(l) for l in range(1, 4)]
    order += [span(0, np.ones((1, P), bool))] + [level(l) for l in range(4, LEVELS)]
    for n, pair in enumerate(order):
        for dr in range(2):
            spans[:, dr, n] = pair[dr]
    masks = [(s // (P >> l) // 2 == t // (P >> l) // 2) & (s // (P >> l) != t // (P >> l)) for l in range(1, LEVELS)]
    masks = np.stack(masks + [s == t], axis=1)
    out = {"consts": const, "rates": rates, "spans": spans.reshape(P, -1), "level_masks": masks.reshape(P, -1)}
    return {k: np.ascontiguousarray(v, dtype=np.float32) for k, v in out.items()}


def program(nc, arrays):
    import numpy as np

    a = {}
    for name, x in arrays.items():
        a[name] = nc.dram_tensor(f"in_{name}", x.shape, mybir.dt.from_np(np.dtype(x.dtype)), kind="ExternalInput").ap()
    out = nc.dram_tensor("out", (1, T, D), F32, kind="ExternalOutput").ap()
    d = Names()
    d.x = a["x"][0]
    d.p = a["p"][:, 0]
    d.positions = a["positions"]
    d.positions_2 = a["positions_2"]
    d.w_in_a = a["w_in_a"][0]
    d.w_o_a = a["w_o_a"][0]
    d.w_kv_b = a["w_kv_b"]
    d.w_in_b = a["w_in_b"][0]
    d.w_o_b = a["w_o_b"][0]
    d.ln_g = a["ln_g"]
    d.ln_b = a["ln_b"]
    d.w_ple = a["w_ple"]
    d.w_g0 = a["w_ple_gate"][0]
    d.w_g1 = a["w_ple_gate"][1]
    d.c = a["c_2"]
    d.w_mod = a["w_mod_2"][0]
    d.b_mod = a["b_mod_2"][0]
    d.pre_mix_g = a["pre_mix_g_2"][0]
    d.post_mix_g = a["post_mix_g_2"][0]
    d.pre_mlp_g = a["pre_mlp_g_2"][0]
    d.post_mlp_g = a["post_mlp_g_2"][0]
    d.w_in_c = a["w_in_2"][0]
    d.q_norm_g = a["q_norm_g_2"][0]
    d.kv_norm_g = a["kv_norm_g_2"][0]
    d.w_uq = a["w_uq_2"][0]
    d.w_ukv = a["w_ukv_2"][0]
    d.hgrn_g = a["hgrn_norm_g_2"][0]
    d.lb_f = a["hgrn_lb_logits_fwd_2"]
    d.lb_b = a["hgrn_lb_logits_bwd_2"]
    d.w_out = a["w_out_2"][0]
    d.w_up = a["w_up_2"][0]
    d.w_down = a["w_down_2"][0]
    d.consts = a["consts"]
    d.rates = a["rates"]
    d.spans = a["spans"]
    d.level_masks = a["level_masks"]
    build(nc, d, out[0])


def kernel(**inputs):
    import concourse.bacc as bacc
    import numpy as np
    from concourse.bass_utils import run_bass_kernel_spmd

    arrays = {k: np.ascontiguousarray(v) for k, v in inputs.items()}
    arrays.update(shape_constants())
    nc = bacc.Bacc("TRN2", target_bir_lowering=False, num_devices=1)
    program(nc, arrays)
    r = run_bass_kernel_spmd(nc, [{f"in_{k}": v for k, v in arrays.items()}], core_ids=[0])
    return r.results[0]["out"]
```

```python
from collections import defaultdict, namedtuple
from contextlib import ExitStack

import concourse.bass as bass
from concourse import mybir

F32 = mybir.dt.float32
F32R = mybir.dt.float32r
I32 = mybir.dt.int32
ACT = mybir.ActivationFunctionType
ALU = mybir.AluOpType
AXX = mybir.AxisListType.X

P = 128
RB = 2
T = RB * P
D = 2048
KT = D // P
HD = 128
NH = 16
NKV = 4
GROUP = NH // NKV
N_SEL = T // 4
IDX_H, IDX_D = 16, 64
ROT_A, ROT_I, ROT_M = 16, 8, 32
NROT = ROT_A + ROT_I + ROT_M
ALPHA = 4.0 ** 0.25
LN_EPS, RMS_EPS = 1e-5, 1e-6
NEG = -1e30
TAKEN = -3e38
MH, NOPE, ROPE, VD = 8, 128, 64, 128
QRANK, KVRANK = 512, 256
HH = 8
LEVELS = 8
WORDS = 18432
TWO_PI_HI, TWO_PI_MID, TWO_PI_LO = 6.28125, 1.9350051879882812e-03, 3.0199159819545e-07
ROUND = 12582912.0

PAIRS = IDX_H // 2
B_PAIRS = NH // 2
KEYS_AT, DOTS_AT, BEST_AT = 3, 6, 14

C_IDENT, C_ONES, C_TRI, C_LT, C_GT, C_ROT = 0, 128, 256, 384, 512, 640
NCONST = C_ROT

STAGES = [
    ("a_qkv", 6, True, 4, 512), ("a_idx", 4, True, 4, 276), ("a_gate", 4, True, 4, 512),
    ("a_out", 4, True, 4, 512), ("ple0", 4, False, 4, 512),
    ("b_kvq", 6, True, 4, 512), ("b_gate", 4, True, 4, 512), ("b_out", 4, True, 4, 512), ("ple1", 4, False, 4, 512),
    ("c_hq", 2, True, 4, 512), ("c_f", 4, True, 4, 512), ("c_hi", 2, True, 4, 512), ("c_hg", 2, True, 4, 512),
    ("c_mla", 2, True, 4, 416), ("uq", 1, False, 4, 384), ("ukv", 1, False, 2, 512),
    ("c_out", 4, True, 4, 512), ("mlp", 32, False, 4, 512),
]


Stage = namedtuple("Stage", "name units mods kq width v0 g0 s0 m0 next per")


class Names:
    pass


def plan():
    out, v, g, s, m = {}, 0, 0, 0, 0
    for n, (name, units, mods, kq, width) in enumerate(STAGES):
        nxt = STAGES[n + 1][0] if n + 1 < len(STAGES) else None
        out[name] = Stage(name=name, units=units, mods=mods, kq=kq, width=width, v0=v, g0=g, s0=s, m0=m,
                                    next=nxt, per=3 if mods else 2)
        v += units + (units // 2 if mods else 0)
        m += units // 2 if mods else 0
        g += units
        s += 4 if units == 1 else units
    return out


PLAN = plan()


def v_of(st, i, k):
    return st.v0 + st.per * i + (0, 1, st.per)[k]


def v_mod(st, i):
    return st.v0 + st.per * i + 2


class Lane:

    def __init__(self, eng, step):
        self.eng, self.step = eng, step
        self.base, self.n = {}, defaultdict(int)

    def at(self, key="step"):
        return self.base.get(key, 0) + self.n[key]

    def did(self, ins):
        ins.then_inc(self.step, 1)
        self.n["step"] += 1

    def sync(self):
        self.eng.wait_ge(self.step, self.at())

    def link(self, ins):
        self.did(ins)
        self.sync()

    def loop(self, count, per, body, first=0):
        if count == 1:
            body(first)
            return
        if count <= 0:
            return
        start = {k: self.at(k) for k in set(per) | set(self.n)}
        with self.eng.Fori(0, count) as i:
            self.base = {k: start[k] + i * per[k] if per.get(k) else start[k] for k in start}
            self.n = defaultdict(int)
            body(i + first if first else i)
            got = {k: n for k, n in self.n.items() if n}
            assert got == {k: n for k, n in per.items() if n}, f"a turn counts {got}"
        self.base = {}
        self.n = defaultdict(int, {k: start[k] + count * per.get(k, 0) for k in start})


def heads_in_turn(lane, per, turn, count=4, unroll=4):
    turn((0, 0), None)

    def body(i):
        for k in range(unroll):
            turn((i, k + 1) if k + 1 < unroll else (i + 1, 0), (i, k))

    lane.loop(count - 1, per, body)
    last = count - 1
    for k in range(unroll):
        turn((last, k + 1) if k + 1 < unroll else None, (last, k))


def heads_three_deep(lane, per, turn, count, unroll):
    def head(i, j):
        return unroll * i + j, j % unroll, i + j // unroll

    def three(i, j):
        return [head(i, j + 2 - back) for back in range(3)]

    turn(head(0, 0), None, None)
    turn(head(0, 1), head(0, 0), None)
    turns = (count - 2) // unroll

    def body(i):
        for j in range(unroll):
            turn(*three(i, j))

    lane.loop(turns, per, body)
    for j in range(unroll * turns, count):
        turn(*[head(0, j + 2 - back) if j + 2 - back < count else None for back in range(3)])


def build(nc, d, out):
    ctx = ExitStack()
    with ctx:
        m = memory(nc, ctx, d, out)
        block = ctx.enter_context(nc.Block())

        @block.sync
        def _(eng):
            sync_program(nc, eng, m, d, out)

        @block.gpsimd
        def _(eng):
            pool_program(nc, eng, m, d)

        @block.scalar
        def _(eng):
            scalar_program(nc, eng, m, d)

        @block.vector
        def _(eng):
            vector_program(nc, eng, m, d)

        @block.tensor
        def _(eng):
            tensor_program(nc, eng, m, d)


def memory(nc, ctx, d, out):
    m = Names()

    def sb(name, shape, dt=F32):
        return ctx.enter_context(nc.sbuf_tensor(name, shape, dt))

    def ps(name, shape):
        return ctx.enter_context(nc.psum_tensor(name, shape, F32))

    def sem(name):
        return ctx.enter_context(nc.semaphore(name))

    arena = nc.alloc_sbuf_tensor("arena", [P, WORDS], F32)
    base = nc.lookup_mloc(arena).addr

    def at(name, word, shape, dt=F32):
        n = 1
        for x in shape[1:]:
            n *= x
        assert word + n <= WORDS, (name, word + n)
        return nc.alloc_sbuf_tensor_at(name, shape, dt, offset=base + 4 * word)

    raw_words = 4 * 4 * 512
    raw_arena = nc.alloc_sbuf_tensor("raw", [P, 4, 4, 512], F32)
    raw_base = nc.lookup_mloc(raw_arena).addr
    m.raw = raw_arena

    def at_raw(name, word, shape, dt=F32):
        n = 1
        for x in shape[1:]:
            n *= x
        assert word + n <= raw_words, (name, word + n)
        return nc.alloc_sbuf_tensor_at(name, shape, dt, offset=raw_base + 4 * word)

    m.hi, m.lo = sb("w_high", [P, 4, 4, 512], F32R), sb("w_low", [P, 4, 4, 512], F32R)
    m.xh, m.xl = sb("x_high", [P, KT, T], F32R), sb("x_low", [P, KT, T], F32R)
    m.const = sb("const", [P, NCONST])
    m.ident, m.ones = m.const[:, C_IDENT:C_IDENT + P], m.const[:, C_ONES:C_ONES + P]
    m.tri, m.lt, m.gt = (m.const[:, c:c + P] for c in (C_TRI, C_LT, C_GT))
    m.acc = sb("mod_sum", [P, 512])
    m.ct = sb("cond_columns", [P, KT])
    m.cs = sb("cos_sin", [P, 2, RB, NROT])
    m.st = sb("stats", [P, RB, 4, 6])
    m.mv = sb("mean_var", [P, 2 * RB, 2])
    m.rstd = sb("rstd", [P, 2 * RB])
    m.msq = sb("mean_square", [P, 2 * RB])
    m.x_sq = sb("x_square_sums", [P, RB, 4])
    m.brow = sb("mod_bias", [1, 512])
    m.dummy = sb("credit_word", [P, 1])

    m.res = at("residual", 0, [P, RB, D])
    m.posi = at("positions_i", 4096, [P, 2 * RB], I32)
    m.posf = at("positions_f", 4104, [P, 2 * RB])
    m.ang = at("angles", 4112, [P, RB, NROT])
    m.turns = at("angle_turns", 4112 + 2 * NROT, [P, RB, NROT])
    m.crow = at("cond_rows", 4112 + 4 * NROT, [KT, P])
    m.rot = at("rotary_rates", 4112 + 4 * NROT + P, [P, NROT])
    m.pa = at("proj_a", 4096, [P, RB, 6224])
    m.a_kt = at("a_keys_t", 0, [P, NKV, T])
    m.a_ikt = at("a_index_keys_t", 1024, [P, T])
    m.a_ikd = at("a_index_keys_twice", 1280, [P, RB, 2, IDX_D])
    m.a_bias0 = at("a_causal_bias", 1536, [P, 384])
    m.a_bias = at("a_bias", 1920, [P, 384])
    m.a_score = at("a_index_score", 2304, [P, 384])
    m.a_top = at("a_top8", 2688, [P, 2, 8])
    m.a_rope = at("a_rope", 2704, [P, 2, 20 * 2 * ROT_A])
    m.a_iqs = at("a_index_q", 2704, [P, 2, RB, P])
    m.a_iws = at("a_index_w", 16544, [P, 2, RB, 2])
    m.a_iqt = at("a_index_q_t", 3216, [P, 2, T])
    m.a_rl = at("a_index_relu", 16552, [P, 2, 2, 384])
    m.a_qs = at("a_q", 2704, [P, 2, RB, P])
    m.a_qt = at("a_q_t", 3216, [P, 2, T])
    m.a_lg = at("a_logits", 16544, [P, 2, 384])
    m.a_pt = at("a_probs_t", 17312, [P, 2, 384])
    m.a_og = at("a_out_gated", 2304, [P, RB, P])
    m.a_nm = at("a_neg_max", 2560, [P, 2, RB])
    m.a_sum = at("a_sum", 2568, [P, 2, RB])
    m.a_rs = at("a_inverse_sum", 2576, [P, 2, RB])
    m.row_g = at("row_g", 4096, [P, D])
    m.row_b = at("row_b", 6144, [P, D])
    m.ple_w = at("ple_w", 8192, [P, 2, D])
    m.ple_p = at("ple_p", 12288, [P, RB, 256])
    m.ple_pt = at("ple_p_t", 12800, [P, 2, T])
    m.ple_s = at("ple_gate", 13312, [P, 2, RB, 512])
    m.pb = at("proj_b", 4096, [P, RB, 5120])
    m.b_kt = at("b_keys_t", 14336, [P, NKV, T])
    m.b_z11 = at("b_scores_11", 15360, [P, NH * HD])
    m.b_qt = at("b_q_t", 17408, [P, 2, 2 * T])
    m.c_g1 = at("c_row_gain", 4096, [P, D])
    m.c_sc = at("c_row_scale", 6144, [P, D])
    m.c_sh = at("c_row_shift", 15360, [P, D])
    m.c_h = at("c_normed", 10240, [P, RB, D])
    m.pc = at("proj_c", 0, [P, RB, 5120])
    m.pm = at("proj_mla", 10240, [P, RB, 832])
    m.m_rg = at("m_norm_rows", 11904, [P, QRANK + KVRANK])
    m.m_rope = at("m_rope", 12672, [P, 2, 512])
    m.m_krd = m.acc[:, 0:RB * P].rearrange("p (r e) -> p r e", r=RB)
    m.mq = at("mla_q", 11264, [P, RB, 1536])
    m.mkv = at("mla_kv", 14336, [P, RB, 2048])
    m.m_rope2 = at_raw("m_rope2", 0, [P, 2, 512])
    m.m_qs = at_raw("m_q", 1024, [P, 2, RB, 256])
    m.m_qt = at_raw("m_q_t", 2560, [P, 2, 2, T])
    m.m_krt = at_raw("m_k_rope_t", 4096, [P, T])
    m.m_lg = at_raw("m_logits", 4352, [P, 2, RB, T])
    m.m_pt = at_raw("m_probs_t", 5376, [P, 2, RB, T])
    m.m_og = at_raw("m_out", 6400, [P, RB, P])
    m.m_nm = at_raw("m_neg_max", 6656, [P, 2, RB])
    m.m_sum = at_raw("m_sum", 6664, [P, 2, RB])
    m.m_rs = at_raw("m_inverse_sum", 6672, [P, 2, RB])
    def at_ring(ring):
        start = nc.lookup_mloc(ring).addr

        def place(name, word, shape):
            n = 1
            for x in shape[1:]:
                n *= x
            assert word + n <= raw_words, (name, word + n)
            return nc.alloc_sbuf_tensor_at(name, shape, F32, offset=start + 4 * word)

        return place

    at_hi, at_lo = at_ring(m.hi), at_ring(m.lo)
    m.b_e = at_hi("b_exp", 0, [P, NKV, 3, GROUP * HD])
    m.b_sp = at_lo("b_softplus", 0, [P, NKV, 3, GROUP * HD])
    m.b_og = at_lo("b_out_gated", 6144, [P, 2, RB, GROUP * HD])
    m.h_l0 = at("h_bound_logits", 14336, [P, 2, 2, 1024])
    m.h_t = at("h_one_minus", 12288, [P, RB, 1024])
    m.h_md = at_hi("h_spans", 0, [P, 2, 9, P])
    m.h_e = at_hi("h_decay", 2304, [P, 2, 2, 4, T])
    m.m_ktt = at_hi("m_keys_t", 2304, [P, MH, T])
    m.h_kt = at_hi("h_k_t", 6400, [P, 2, 2, T])
    m.h_ks = at_hi("h_k_sum", 7424, [P, 2, T])
    m.h_lfa = at_lo("h_log_f_all", 0, [P, RB, 2048])
    m.h_mask = at_lo("h_level_masks", 4096, [P, LEVELS, P])
    m.h_qt = at_lo("h_q_t", 5120, [P, 2, T])
    m.h_at = at_lo("h_weights_t", 5632, [P, 4, P])
    m.h_fs = at_lo("h_f", 6144, [P, 2, 2, RB, P])
    m.h_qs = at_lo("h_q", 7168, [P, 2, RB, P])
    m.h_ng = at_lo("h_norm_g", 7680, [P, P])
    m.h_sq = at_lo("h_squares", 7808, [P, RB, P])
    m.h_kq = at("h_keys_queries", 10240, [P, 2, 2, 4, T])
    m.h_tm = at("h_masked", 14336, [P, 2, LEVELS, P])
    m.h_lf = at("h_log_f", 16384, [P, 2, 2, RB, P])
    m.h_ms = at("h_mean_sq", 17408, [P, RB, HH])
    m.h_r = at("h_rstd", 17424, [P, RB, HH])
    m.mix = at("mix", 4096, [P, RB, D])
    m.x_ga = at("x_row_gate", 8192, [P, D])
    m.x_pg = at("x_row_post", 10240, [P, D])
    m.x_g1 = at("x_row_gain", 12288, [P, D])
    m.x_sc = at("x_row_scale", 14336, [P, D])
    m.x_sh = at("x_row_shift", 16384, [P, D])
    m.y = at("mlp_sum", 4096, [P, RB, D])
    m.uh = at("u_high", 8192, [P, KT, T], F32R)
    m.ul = at("u_low", 12288, [P, KT, T], F32R)
    m.ur = at("u_rows", 16384, [P, 2, RB, 512])
    m.z_gm = at_raw("z_row_gate", 0, [P, D])
    m.z_pg = at_raw("z_row_post", 2048, [P, D])

    m.g = ps("products", [P, 4, 512])
    m.t = ps("transposed", [P, 2, 512])
    m.u = ps("aside", [P, 2, 512])

    m.mod_d = nc.dram_tensor("mod_row", (6 * D,), F32).ap()
    m.res_d = nc.dram_tensor("residual_kept", (T, D), F32).ap()

    m.s_landed = [sem(f"quarter_landed_{j}") for j in range(4)]
    m.s_raw_used = sem("raw_used")
    m.s_w_high = sem("w_high")
    m.s_w_used = sem("w_used")
    m.s_x_high_ready = sem("x_high_ready")
    m.s_y_ready = sem("y_ready")
    m.s_const_landed = sem("const_landed")
    m.s_x_landed = sem("x_landed")
    m.s_pos_landed = sem("pos_landed")
    m.s_rows_landed = sem("rows_landed")
    m.s_rows2_landed = sem("rows2_landed")
    m.s_ple_landed = sem("ple_landed")
    m.s_res_stored = sem("res_stored")
    m.s_out_stored = sem("out_stored")
    m.s_mod_summed = sem("mod_summed")
    m.s_mod_row = sem("mod_row")
    m.s_brow_landed = sem("brow_landed")
    m.s_mod_stored = sem("mod_stored")
    m.s_pool_step = sem("pool_step")
    m.s_act_step = sem("act_step")
    m.s_dve_step = sem("dve_step")
    m.s_pe_step = sem("pe_step")
    m.s_angles_ready = sem("angles_ready")
    m.s_sin_ready = sem("sin_ready")
    m.s_var_ready = sem("var_ready")
    m.s_std_ready = sem("std_ready")
    m.s_ple_full = sem("ple_full")
    m.s_ple_free = sem("ple_free")
    m.s_x4_ready = sem("x4_ready")
    m.s_mlp_done = sem("mlp_done")
    m.s_res2_landed = sem("res2_landed")
    m.s_a_ready = sem("a_ready")
    m.s_a_k_t = sem("a_k_t")
    m.s_a_ktp = sem("a_ktp")
    m.s_a_k_copied = sem("a_k_copied")
    m.s_a_iq = sem("a_iq")
    m.s_a_iqt = sem("a_iqt")
    m.s_a_iqc = sem("a_iqc")
    m.s_a_dots = sem("a_dots")
    m.s_a_relu = sem("a_relu")
    m.s_a_idx_done = sem("a_idx_done")
    m.s_a_biased = sem("a_biased")
    m.s_a_q = sem("a_q")
    m.s_a_qtp = sem("a_qtp")
    m.s_a_qtc = sem("a_qtc")
    m.s_a_s = sem("a_s")
    m.s_a_nmax = sem("a_nmax")
    m.s_a_p = sem("a_p")
    m.s_a_ptp = sem("a_ptp")
    m.s_a_ptc = sem("a_ptc")
    m.s_a_o = sem("a_o")
    m.s_a_ogr = sem("a_ogr")
    m.s_a_ogt = sem("a_ogt")
    m.s_a_xh = sem("a_xh")
    m.s_a_done = sem("a_done")
    m.s_b_k_t = sem("b_k_t")
    m.s_b_k_copied = sem("b_k_copied")
    m.s_b_qtp = sem("b_qtp")
    m.s_b_qtc = sem("b_qtc")
    m.s_b_z = sem("b_z")
    m.s_b_zc = sem("b_z_copied")
    m.s_b_l = sem("b_l")
    m.s_b_spr = sem("b_softplus_ready")
    m.s_b_sfx = sem("b_sfx")
    m.s_b_a1 = sem("b_a1")
    m.s_b_ex = sem("b_ex")
    m.s_b_w = sem("b_w")
    m.s_b_o = sem("b_o")
    m.s_b_ogr = sem("b_ogr")
    m.s_b_ogt = sem("b_ogt")
    m.s_b_xh = sem("b_xh")
    m.s_b_done = sem("b_done")
    m.s_m_ready = sem("m_ready")
    m.s_m_krt_t = sem("m_krt_t")
    m.s_m_krt_c = sem("m_krt_c")
    m.s_m_q = sem("m_q")
    m.s_m_qtp = sem("m_qtp")
    m.s_m_qtc = sem("m_qtc")
    m.s_m_s = sem("m_s")
    m.s_m_nmax = sem("m_nmax")
    m.s_m_p = sem("m_p")
    m.s_m_ptp = sem("m_ptp")
    m.s_m_ptc = sem("m_ptc")
    m.s_m_o = sem("m_o")
    m.s_m_ogr = sem("m_ogr")
    m.s_m_ogt = sem("m_ogt")
    m.s_m_xh = sem("m_xh")
    m.s_m_done = sem("m_done")
    m.s_m_qkv = sem("m_qkv")
    m.s_m_ktp = sem("m_ktp")
    m.s_m_ktc = sem("m_ktc")
    m.s_h_lb = sem("h_lb")
    m.s_h_lbs = sem("h_lbs")
    m.s_h_fr = sem("h_fr")
    m.s_h_rows = sem("h_rows")
    m.s_h_consts = sem("h_consts")
    m.s_h_q = sem("h_q")
    m.s_h_logf = sem("h_logf")
    m.s_h_tr = sem("h_tr")
    m.s_h_qc = sem("h_qc")
    m.s_h_kc = sem("h_kc")
    m.s_h_k1 = sem("h_keys")
    m.s_h_ms = sem("h_squares_summed")
    m.s_x_sq = sem("x_squares")
    m.s_x_added = sem("x_added")
    m.s_h_d = sem("h_d")
    m.s_h_ex = sem("h_ex")
    m.s_h_mul = sem("h_mul")
    m.s_h_am = sem("h_am")
    m.s_h_dg = sem("h_dg")
    m.s_h_gain = sem("h_gain")
    m.s_h_msk = sem("h_msk")
    m.s_h_off = sem("h_off")
    m.s_h_red = sem("h_red")
    m.s_h_o = sem("h_o")
    m.s_h_oc = sem("h_oc")
    m.s_h_ms1 = sem("h_ms1")
    m.s_h_std = sem("h_std")
    m.s_g_free = [sem(f"product_free_{b}") for b in range(2)]
    m.s_t_full = [sem(f"transposed_full_{b}") for b in range(2)]
    m.s_t_free = [sem(f"transposed_free_{b}") for b in range(2)]
    return m


def gemm_turns(lane, st, per, turn, tail):
    n = st.units // 2
    lane.loop(n - 1, per, turn)
    tail(n - 1)


def rows(ap, n):
    return ap.rearrange("(o n) -> o n", o=1).broadcast_to((P, n))


def scores(m, c):
    w = GROUP * HD
    return m.pb[:, :, 1024 + w * c:1024 + w * c + w], m.b_z11[:, w * c:w * c + w]


def sync_program(nc, sp, m, d, out):
    lane = Lane(sp, m.s_pe_step)

    def load(st, v, src):
        for j in range(4):
            sp.wait_ge(m.s_raw_used, 4 * v + j + 1)
            sp.dma_start(m.raw[:, j, 0:st.kq, 0:st.width], src(j)).then_inc(m.s_landed[j], 16)

    def tiles(w, j, col, width, row=0):
        return w.rearrange("(k p) n -> p k n", p=P)[:, row + 4 * j:row + 4 * j + 4, bass.ds(col, width)]

    def source(name, u):
        col = {"a_qkv": 0, "a_gate": 3072, "a_idx": 5120, "b_gate": 2048, "c_hq": 832, "c_f": 1856,
               "c_hi": 3904, "c_hg": 4928}.get(name, 0)
        width = PLAN[name].width
        if name == "b_kvq":
            w, c = (d.w_kv_b, 512 * u) if isinstance(u, int) and u < 2 else (d.w_in_b, 512 * (u - 2))
        elif name == "uq":
            return lambda j: d.w_uq.rearrange("(k p) n -> p k n", p=P)[:, :, 384 * j:384 * j + 384]
        elif name == "ukv":
            return lambda j: d.w_ukv.rearrange("(k p) n -> p k n", p=P)[:, :, 512 * j:512 * j + 512]
        else:
            w = {"a": d.w_in_a, "b": d.w_in_b, "c": d.w_in_c}.get(name[0])
            w = {"a_out": d.w_o_a, "b_out": d.w_o_b, "c_out": d.w_out, "ple0": d.w_g0, "ple1": d.w_g1}.get(name, w)
            c = col + width * u
        c = sp.snap(c) if not isinstance(c, int) else c
        return lambda j: tiles(w, j, c, width)

    def load_unit(name, i, k):
        st = PLAN[name]
        load(st, v_of(st, i, k), source(name, 2 * i + k))

    def load_mod(name, i):
        st = PLAN[name]
        c = 512 * (st.m0 + i)
        c = sp.snap(c) if not isinstance(c, int) else c
        load(PLAN["a_qkv"], v_mod(st, i), lambda j: tiles(d.w_mod, j, c, 512))

    def gemm(name, before_tail=None, next_too=True):
        st = PLAN[name]

        def turn(i):
            load_unit(name, i, 1)
            if st.mods:
                load_mod(name, i)
            load_unit(name, i, 2)

        def tail(i):
            if before_tail:
                before_tail()
            load_unit(name, i, 1)
            if st.mods:
                load_mod(name, i)
            if next_too:
                load_unit(st.next, 0, 0)

        n = st.units // 2
        if name == "b_kvq":
            for i in range(n - 1):
                turn(i)
        else:
            lane.loop(n - 1, {}, turn)
        tail(n - 1)

    def bring(tile, src, s):
        sp.dma_start(tile, src).then_inc(s, 16)

    tokens = "(r p) n -> p r n"
    bring(m.const[:], d.consts, m.s_const_landed)
    bring(m.crow[:], d.c.rearrange("o (k p) -> (o k) p", p=P), m.s_const_landed)
    bring(m.res[:], d.x.rearrange(tokens, p=P), m.s_x_landed)
    with nc.allow_non_contiguous_dma(reason="512 positions"):
        bring(m.posi[:, 0:RB], d.positions.rearrange("o (r p) -> p (o r)", p=P), m.s_pos_landed)
        bring(m.posi[:, RB:2 * RB], d.positions_2.rearrange("o (r p) -> p (o r)", p=P), m.s_pos_landed)
    bring(m.rot[:], d.rates, m.s_pos_landed)
    load_unit("a_qkv", 0, 0)
    for name in ("a_qkv", "a_idx", "a_gate"):
        gemm(name)

    def norm_rows(layer):
        def go():
            if layer:
                sp.wait_ge(m.s_b_done, NKV)
            bring(m.row_g[:], rows(d.ln_g[layer], D), m.s_rows_landed)
            bring(m.row_b[:], rows(d.ln_b[layer], D), m.s_rows_landed)
            bring(m.ple_w[:], d.w_ple[layer].rearrange("(k p) n -> p k n", p=P), m.s_ple_landed)
            bring(m.ple_p[:], d.p[layer].rearrange(tokens, p=P), m.s_ple_landed)
        return go

    sp.wait_ge(m.s_a_done, NH + 2)
    bring(m.res[:], d.x.rearrange(tokens, p=P), m.s_x_landed)
    gemm("a_out", norm_rows(0))
    gemm("ple0")
    gemm("b_kvq")
    gemm("b_gate")
    gemm("b_out", norm_rows(1))

    def c_rows():
        sp.wait_ge(m.s_y_ready, 20)
        bring(m.c_g1[:], rows(d.pre_mix_g, D), m.s_rows2_landed)
        sp.wait_ge(m.s_mod_stored, 16 * 9)
        bring(m.c_sh[:], rows(m.mod_d[0:D], D), m.s_rows2_landed)
        bring(m.c_sc[:], rows(m.mod_d[D:2 * D], D), m.s_rows2_landed)

    gemm("ple1", c_rows)
    sp.wait_ge(m.s_x4_ready, 4)
    bring(m.res_d.rearrange(tokens, p=P), m.res[:], m.s_res_stored)
    gemm("c_hq")
    gemm("c_f")
    sp.wait_ge(m.s_w_used, 4 * PLAN["c_f"].g0 + 4)
    for dr, lb in enumerate((d.lb_f, d.lb_b)):
        for slot in range(2):
            bring(m.h_l0[:, dr, slot, :], rows(lb[slot], 1024), m.s_h_rows)
    gemm("c_hi")
    gemm("c_hg")
    sp.wait_ge(m.s_h_fr, 2)
    bring(m.m_rg[:, 0:QRANK], rows(d.q_norm_g, QRANK), m.s_rows2_landed)
    bring(m.m_rg[:, QRANK:], rows(d.kv_norm_g, KVRANK), m.s_rows2_landed)
    gemm("c_mla")
    load_unit("ukv", 0, 0)
    sp.wait_ge(m.s_w_used, 4 * PLAN["ukv"].g0 + 8)
    bring(m.h_md[:], d.spans.rearrange("p (a b c) -> p a b c", a=2, b=9), m.s_h_consts)
    bring(m.h_mask[:], d.level_masks.rearrange("p (a b) -> p a b", a=LEVELS), m.s_h_consts)
    bring(m.h_ng[:], rows(d.hgrn_g, P), m.s_h_consts)
    sp.wait_ge(m.s_m_done, MH + 2)
    load_unit("c_out", 0, 0)
    for b in range(2):
        sp.wait_ge(m.s_t_free[b], 26)
    sp.wait_ge(m.s_res_stored, 16)
    bring(m.res[:], m.res_d.rearrange(tokens, p=P), m.s_res2_landed)

    def x_rows():
        sp.wait_ge(m.s_mod_stored, 16 * 21)
        bring(m.x_ga[:], rows(m.mod_d[2 * D:3 * D], D), m.s_rows2_landed)
        bring(m.x_pg[:], rows(d.post_mix_g, D), m.s_rows2_landed)
        bring(m.x_g1[:], rows(d.pre_mlp_g, D), m.s_rows2_landed)
        bring(m.x_sc[:], rows(m.mod_d[4 * D:5 * D], D), m.s_rows2_landed)
        bring(m.x_sh[:], rows(m.mod_d[3 * D:4 * D], D), m.s_rows2_landed)

    gemm("c_out", x_rows, next_too=False)
    mlp = PLAN["mlp"]

    def mlp_load(q, k):
        if k < 4:
            c = 2048 * q + 512 * k
            c = sp.snap(c) if not isinstance(c, int) else c
            load(mlp, mlp.v0 + 8 * q + k, lambda j: tiles(d.w_up, j, c, 512))
        else:
            if isinstance(q, int):
                load(mlp, mlp.v0 + 8 * q + k,
                     lambda j: tiles(d.w_down, j, 512 * (k - 4), 512, row=KT * q))
            else:
                off = sp.snap(2048 * q)
                w = d.w_down[bass.ds(off, 2048), :]
                load(mlp, mlp.v0 + 8 * q + k, lambda j: tiles(w, j, 512 * (k - 4), 512))

    lane.loop(4, {}, lambda q: [mlp_load(q, k) for k in range(8)])
    sp.wait_ge(m.s_raw_used, 4 * (mlp.v0 + 32) + 1)
    sp.wait_ge(m.s_mod_stored, 16 * 25)
    bring(m.z_gm[:], rows(m.mod_d[5 * D:6 * D], D), m.s_rows2_landed)
    sp.wait_ge(m.s_raw_used, 4 * (mlp.v0 + 32) + 2)
    bring(m.z_pg[:], rows(d.post_mlp_g, D), m.s_rows2_landed)
    for c in range(4):
        sp.wait_ge(m.s_mlp_done, c + 1)
        bring(out.rearrange(tokens, p=P)[:, :, 512 * c:512 * c + 512], m.res[:, :, 512 * c:512 * c + 512], m.s_out_stored)
    sp.wait_ge(m.s_out_stored, 64)


def pool_program(nc, pool, m, d):
    lane = Lane(pool, m.s_pool_step)
    credits = [(m.s_raw_used, 4), (m.s_w_used, 4), (m.s_mod_summed, 1), (m.s_mod_stored, 16), (m.s_h_d, 4), (m.s_h_mul, 2),
               (m.s_a_done, 2), (m.s_m_done, 2), (m.s_a_qtp, 2), (m.s_m_qtp, 2), (m.s_a_idx_done, 2), (m.s_ple_free, 1)]
    credits += [(s, 1) for s in m.s_g_free + m.s_t_free]
    for n, (s, k) in enumerate(credits):
        if n:
            pool.wait_ge(credits[n - 1][0], 1)
        nc.gpsimd.memset(m.dummy[:], 0.0).then_inc(s, k)

    pool.wait_ge(m.s_a_ready, 1)
    nc.gpsimd.tensor_copy(m.a_ikd[:, :, 0, :], m.pa[:, :, 6144:6208]).then_inc(m.s_a_k_t, 1)
    nc.gpsimd.tensor_copy(m.a_ikd[:, :, 1, :], m.pa[:, :, 6144:6208]).then_inc(m.s_a_k_t, 1)

    def index_pair(i):
        for k in range(2):
            t = 2 * i + k
            pool.wait_ge(m.s_a_idx_done, t + 1)
            nc.gpsimd.tensor_copy(m.a_iws[:, k], m.pa[:, :, bass.ds(6208 + 2 * t, 2)]).then_inc(m.s_a_iq, 1)
            nc.gpsimd.tensor_copy(m.a_iqs[:, k], m.pa[:, :, bass.ds(5120 + P * t, P)]).then_inc(m.s_a_iq, 1)

    lane.loop(4, {}, index_pair)

    pool.wait_ge(m.s_a_biased, 1)

    def a_heads(i):
        for k in range(GROUP):
            pool.wait_ge(m.s_a_qtp, 4 * i + k + 1)
            nc.gpsimd.tensor_copy(m.a_qs[:, k % 2], m.pa[:, :, bass.ds(HD * (4 * k + i), HD)]).then_inc(m.s_a_q, 1)

    lane.loop(GROUP, {}, a_heads)
    pool.wait_ge(m.s_m_ready, 1)
    nc.gpsimd.memset(m.m_qs[:], 0.0).then_inc(m.s_m_qkv, 1)
    pool.wait_ge(m.s_m_qkv, 1)

    def m_heads(i):
        for k in range(2):
            t = 2 * i + k
            pool.wait_ge(m.s_m_qtp, t + 1)
            nc.gpsimd.tensor_copy(m.m_qs[:, k, :, 0:NOPE + ROPE], m.mq[:, :, bass.ds((NOPE + ROPE) * t, NOPE + ROPE)]).then_inc(m.s_m_q, 1)

    lane.loop(MH // 2, {}, m_heads)
    pool.wait_ge(m.s_m_done, MH + 2)
    pool.wait_ge(m.s_h_logf, RB)

    def h_heads(i):
        for k in range(2):
            t = 2 * i + k
            pool.wait_ge(m.s_h_d, 2 * t + 2)
            nc.gpsimd.tensor_copy(m.h_qs[:, k], m.pc[:, :, bass.ds(HD * t, HD)]).then_inc(m.s_h_q, 1)
            for dr in range(2):
                nc.gpsimd.tensor_copy(m.h_fs[:, k, dr], m.pc[:, :, bass.ds(1024 * (dr + 1) + HD * t, HD)]).then_inc(m.s_h_q, 1)
            for dr in range(2):
                nc.gpsimd.tensor_copy(m.h_lf[:, k, dr], m.h_lfa[:, :, bass.ds(1024 * dr + HD * t, HD)]).then_inc(m.s_h_q, 1)

    lane.loop(HH // 2, {}, h_heads)
    pool.wait_ge(m.s_h_consts, 48)
    for rb in range(RB):
        gate = m.pc[:, rb, 4096:5120].rearrange("p (h e) -> p h e", h=HH)
        nc.gpsimd.tensor_tensor(gate, gate, m.h_ng[:].unsqueeze(1).broadcast_to((P, HH, HD)), ALU.mult).then_inc(m.s_h_gain, 1)


def scalar_program(nc, act, m, d):
    lane = Lane(act, m.s_act_step)

    def high(st, v, g, js=range(4), aside=None):
        for j in js:
            act.wait_ge(m.s_landed[j], 16 * v + 16)
            act.wait_ge(m.s_w_used, 4 * g + j + 1)
            act.activation(m.hi[:, j, 0:st.kq, 0:st.width], m.raw[:, j, 0:st.kq, 0:st.width], ACT.Copy).then_inc(m.s_w_high, 1)
            if aside:
                aside(j)

    def high_unit(name, i, k, js=range(4), aside=None):
        st = PLAN[name]
        high(st, v_of(st, i, k), st.g0 + 2 * i + k, js, aside)

    def product(st, i, k):
        act.wait_ge(m.s_w_used, 4 * (st.g0 + 2 * i + k) + 8)
        return m.g[:, 2 * k:2 * k + 2, 0:st.width]

    def mod_io(st, i):
        n = st.m0 + i
        act.wait_ge(m.s_mod_row, n + 1)
        act.dma_start(m.mod_d[bass.ds(512 * n, 512)].rearrange("(o n) -> o n", o=1), m.acc[0:1, :]).then_inc(m.s_mod_stored, 16)
        if not (isinstance(n, int) and n == 23):
            act.dma_start(m.brow[:], d.b_mod[bass.ds(512 * n + 512, 512)].rearrange("(o n) -> o n", o=1)).then_inc(m.s_brow_landed, 16)

    def gemm(name, take, next_too=True, per={}, late=0, aside=None):
        st = PLAN[name]

        def by(u):
            return aside and (lambda j: aside(4 * u + j))

        def turn(i):
            high_unit(name, i, 1, aside=by(2 * i))
            take(st, i, 0)
            high_unit(name, i, 2, aside=by(2 * i + 1))
            take(st, i, 1)
            if st.mods:
                mod_io(st, i)

        def tail(i):
            high_unit(name, i, 1, aside=by(2 * i))
            take(st, i, 0)
            if next_too:
                high_unit(st.next, 0, 0, range(min(3, 4 - late)), by(2 * i + 1))
            if aside and late:
                for j in range(min(3, 4 - late), 4):
                    aside(4 * (2 * i + 1) + j)
            take(st, i, 1)
            if next_too and not late:
                high_unit(st.next, 0, 0, [3], by(2 * i + 1))
            if st.mods:
                mod_io(st, i)

        gemm_turns(lane, st, per, turn, tail)

    def keep(tile, col, func=ACT.Copy):
        def take(st, i, k):
            src = product(st, i, k)
            act.activation(tile[:, :, bass.ds(col + st.width * (2 * i + k), st.width)], src, func).then_inc(m.s_g_free[k], 1)
        return take

    def nothing(st, i, k):
        pass

    def high_columns(k0, uses):
        for q in range(uses):
            n = lane.n["T"]
            act.wait_ge(m.s_t_full[n % 2], n // 2 + 1)
            act.activation(m.xh[:, k0 + 2 * q:k0 + 2 * q + 2, :], m.t[:, n % 2, :].rearrange("p (k t) -> p k t", k=2), ACT.Copy)\
               .then_inc(m.s_x_high_ready, 1)
            lane.n["T"] += 1

    def std(n, columns=RB):
        act.wait_ge(m.s_var_ready, n)
        act.activation(m.rstd[:, 0:columns], m.msq[:, 0:columns], ACT.Sqrt).then_inc(m.s_std_ready, 1)

    act.dma_start(m.brow[:], d.b_mod[0:512].rearrange("(o n) -> o n", o=1)).then_inc(m.s_brow_landed, 16)
    act.wait_ge(m.s_t_full[0], 1)
    act.activation(m.ct[:], m.t[:, 0, 0:KT], ACT.Silu).then_inc(m.s_t_free[0], 1)
    lane.n["T"] += 1
    for c in range(4):
        high_columns(4 * c, 2)
        high_unit("a_qkv", 0, 0, [c])
    act.wait_ge(m.s_angles_ready, 1)
    act.activation(m.cs[:, 0], m.turns[:], ACT.Sin).then_inc(m.s_sin_ready, 1)
    act.activation(m.cs[:, 1], m.ang[:], ACT.Sin).then_inc(m.s_sin_ready, 1)
    act.wait_ge(m.s_sin_ready, 2)
    gemm("a_qkv", keep(m.pa, 0))
    gemm("a_idx", keep(m.pa, 5120))

    def index_aside(b):
        if b == KEYS_AT:
            act.wait_ge(m.s_a_ktp, 2)
            act.activation(m.a_kt[:].rearrange("p (a k) t -> p a (k t)", a=2), m.t[:], ACT.Copy).then_inc(m.s_a_k_copied, 1)
            act.activation(m.a_ikt[:], m.u[:, 1, 0:T], ACT.Copy).then_inc(m.s_a_k_copied, 1)
        t = b - DOTS_AT
        if 0 <= t < PAIRS:
            for hh, bank in enumerate((m.t[:, 1, 0:384], m.u[:, 1, 0:384])):
                act.wait_ge(m.s_a_dots, t + 1)
                act.activation(m.a_rl[:, t % 2, hh], bank, ACT.Relu, scale=IDX_D ** -0.5 * IDX_H ** -0.5).then_inc(m.s_a_relu, 1)
        t = b - DOTS_AT + 1
        if 0 <= t < PAIRS:
            act.wait_ge(m.s_a_iqt, t + 1)
            act.activation(m.a_iqt[:, t % 2], m.t[:, 0, 0:T], ACT.Copy).then_inc(m.s_a_iqc, 1)

    gemm("a_gate", keep(m.pa, 3072, ACT.Silu), aside=index_aside)

    def head_high(bank, h):
        return act.activation(m.xh[:, bass.ds(h, 1), :].rearrange("p k t -> p (k t)"), m.t[:, bank, T:2 * T], ACT.Copy)

    def a_turn(nxt, cur, prev):
        if nxt:
            n, k = nxt[0], nxt[1] % 2
            act.wait_ge(m.s_a_qtp, n + 3)
            act.activation(m.a_qt[:, k], m.g[:, k, 0:T], ACT.Copy).then_inc(m.s_a_qtc, 1)
        if cur:
            t, kc = cur[0], cur[1] % 2
            act.wait_ge(m.s_a_ptp, t + 1)
            act.activation(m.a_pt[:, kc], m.u[:, kc, 0:384], ACT.Copy).then_inc(m.s_a_ptc, 1)
        if prev:
            act.wait_ge(m.s_a_ogt, prev[0] + 1)
            head_high(prev[1] % 2, 4 * prev[1] + prev[2]).then_inc(m.s_a_xh, 1)
        if nxt:
            act.wait_ge(m.s_a_nmax, n + 1)
            for rb, cols in enumerate((slice(0, P), slice(P, 384))):
                act.activation(m.a_lg[:, k, cols], m.a_lg[:, k, cols], ACT.Exp, bias=m.a_nm[:, k, rb:rb + 1],
                               accum_out=m.a_sum[:, k, rb:rb + 1]).then_inc(m.s_a_p, 1)

    heads_three_deep(lane, {}, a_turn, NH, GROUP)

    def norm_and_embed(name_out, name_ple, layer):
        gemm(name_out, nothing, late=2)
        n = lane.n["T"]
        act.wait_ge(m.s_t_full[n % 2], n // 2 + 1)
        act.activation(m.ple_pt[:], m.t[:, n % 2, :].rearrange("p (k t) -> p k t", k=2), ACT.Copy).then_inc(m.s_t_free[n % 2], 1)
        lane.n["T"] += 1
        std(layer + 1)
        high_unit(name_ple, 0, 0, [2])
        high_columns(0, 2)
        high_unit(name_ple, 0, 0, [3])
        high_columns(4, 6)

        def gate(st, i, k):
            src = product(st, i, k)
            act.activation(m.ple_s[:, k], src, ACT.Sigmoid).then_inc(m.s_g_free[k], 1)

        gemm(name_ple, gate)

    norm_and_embed("a_out", "ple0", 0)
    high_columns(0, 8)
    gemm("b_kvq", keep(m.pb, 0))

    def scores_aside(b):
        if b == KEYS_AT:
            act.wait_ge(m.s_b_k_t, 1)
            act.activation(m.b_kt[:].rearrange("p (a k) t -> p a (k t)", a=2), m.t[:], ACT.Copy).then_inc(m.s_b_k_copied, 1)
        t = b - DOTS_AT
        if 0 <= t < B_PAIRS:
            act.wait_ge(m.s_b_z, t + 1)
            for hh, bank in enumerate((m.t[:, 1], m.u[:, 1])):
                h = HD * (2 * t + hh)
                act.activation(m.pb[:, :, 1024 + h:1024 + h + HD], bank[:, 0:T].rearrange("p (r e) -> p r e", r=RB), ACT.Copy, scale=HD ** -0.5)\
                   .then_inc(m.s_b_zc, 1)
                act.activation(m.b_z11[:, h:h + HD], bank[:, T:384], ACT.Copy, scale=HD ** -0.5).then_inc(m.s_b_zc, 1)
        t = b - DOTS_AT + 1
        if 0 <= t < B_PAIRS:
            act.wait_ge(m.s_b_qtp, t + 1)
            act.activation(m.b_qt[:, t % 2], m.t[:, 0, :], ACT.Copy).then_inc(m.s_b_qtc, 1)

    gemm("b_gate", keep(m.pb, 3072, ACT.Silu), late=4, aside=scores_aside)
    act.wait_ge(m.s_b_zc, 4 * B_PAIRS)

    def log_parts(cs):
        for c in cs:
            for e, z in zip((m.b_e[:, c, 0:2], m.b_e[:, c, 2]), scores(m, c)):
                lane.did(act.activation(e, z, ACT.Abs))
        lane.sync()
        for c in cs:
            lane.did(act.activation(m.b_e[:, c], m.b_e[:, c], ACT.Exp, scale=-1.0))
        lane.sync()

    def logs(cs):
        for c in cs:
            act.activation(m.b_e[:, c], m.b_e[:, c], ACT.Ln, bias=1.0).then_inc(m.s_b_l, 1)

    def weights(c):
        act.wait_ge(m.s_b_a1, c + 1)
        act.activation(m.b_e[:, c], m.b_e[:, c], ACT.Exp).then_inc(m.s_b_ex, 1)

    def group_high(c):
        act.wait_ge(m.s_b_ogt, c + 1)
        act.activation(m.xh[:, GROUP * c:GROUP * c + GROUP, :].rearrange("p (a k) t -> p a (k t)", a=2), m.t[:], ACT.Copy).then_inc(m.s_b_xh, 1)

    def next_high(j):
        act.wait_ge(m.s_b_o, min(j + 2, NKV))
        high_unit("b_out", 0, 0, [j])

    log_parts((0, 1))
    logs((0, 1))
    log_parts((2, 3))
    weights(0)
    logs((2, 3))
    weights(1)
    group_high(0)
    weights(2)
    group_high(1)
    weights(3)
    next_high(0)
    group_high(2)
    next_high(1)
    group_high(3)
    next_high(2)
    next_high(3)
    norm_and_embed("b_out", "ple1", 1)
    std(3)
    high_columns(0, 8)
    act.wait_ge(m.s_res_stored, 16)
    gemm("c_hq", keep(m.pc, 0))
    gemm("c_f", keep(m.pc, 1024, ACT.Sigmoid))
    def bounds(dr):
        act.wait_ge(m.s_h_lb, dr + 1)
        act.activation(m.h_l0[:, dr, 0], m.h_l0[:, dr, 0], ACT.Sigmoid).then_inc(m.s_h_lbs, 1)

    gemm("c_hi", keep(m.pc, 3072))
    bounds(0)
    gemm("c_hg", keep(m.pc, 4096, ACT.Silu))
    bounds(1)
    gemm("c_mla", keep(m.pm, 0))
    std(4, 2 * RB)
    high_columns(8, 3)
    uq, ukv = PLAN["uq"], PLAN["ukv"]
    for j in range(4):
        high(ukv, ukv.v0, ukv.g0, [j])
        act.wait_ge(m.s_w_used, 4 * uq.g0 + 4 + j + 1)
        act.activation(m.mq[:, :, 384 * j:384 * j + 384], m.g[:, 2 * (j % 2):2 * (j % 2) + 2, 0:384], ACT.Copy).then_inc(m.s_g_free[j % 2], 1)
    act.wait_ge(m.s_h_fr, 2)
    for j in range(4):
        act.wait_ge(m.s_w_used, 4 * ukv.g0 + 4 + j + 1)
        act.activation(m.mkv[:, :, 512 * j:512 * j + 512], m.g[:, 2 * (j % 2):2 * (j % 2) + 2, :], ACT.Copy).then_inc(m.s_g_free[j % 2], 1)
        if 1 <= j <= 2:
            act.activation(m.h_lfa[:, j - 1], m.pc[:, j - 1, 1024:3072], ACT.Ln).then_inc(m.s_h_logf, 1)
    act.wait_ge(m.s_m_krt_t, 1)
    act.activation(m.m_krt[:], m.t[:, 0, 0:T], ACT.Copy).then_inc(m.s_m_krt_c, 1)
    mscale = (NOPE + ROPE) ** -0.5

    for c in range(4):
        act.wait_ge(m.s_m_ktp, c + 1)
        act.activation(m.m_ktt[:, 2 * c:2 * c + 2, :], m.g[:, c, :].rearrange("p (h t) -> p h t", h=2), ACT.Copy).then_inc(m.s_m_ktc, 1)

    def m_turn(nxt, cur, prev):
        if nxt:
            n, k, _ = nxt
            act.wait_ge(m.s_m_qtp, n + 3)
            act.activation(m.m_qt[:, k].rearrange("p a t -> p (a t)"), m.g[:, k, :], ACT.Copy).then_inc(m.s_m_qtc, 1)
        if cur:
            t, kc, _ = cur
            act.wait_ge(m.s_m_ptp, t + 1)
            act.activation(m.m_pt[:, kc].rearrange("p a t -> p (a t)"), m.u[:, kc, :], ACT.Copy).then_inc(m.s_m_ptc, 1)
        if prev:
            act.wait_ge(m.s_m_ogt, prev[0] + 1)
            head_high(prev[1], prev[0]).then_inc(m.s_m_xh, 1)
        if nxt:
            act.wait_ge(m.s_m_nmax, n + 1)
            for rb in range(RB):
                act.activation(m.m_lg[:, k, rb], m.g[:, 2 + k, T * rb:T * rb + T], ACT.Exp, scale=mscale, bias=m.m_nm[:, k, rb:rb + 1],
                               accum_out=m.m_sum[:, k, rb:rb + 1]).then_inc(m.s_m_p, 1)

    heads_three_deep(lane, {}, m_turn, MH, 2)
    span_banks = [m.g[:, 2], m.g[:, 3], m.u[:, 0], m.u[:, 1]]

    def decays(n, group, banks=range(4)):
        act.wait_ge(m.s_h_mul, 2 * n + group + 1)
        act.wait_ge(m.s_h_d, 2 * n + group + 5)
        for b in banks:
            act.activation(m.h_e[:, group, b // 2, :, P * (b % 2):P * (b % 2) + P], span_banks[b].rearrange("p (l t) -> p l t", l=4), ACT.Exp)\
               .then_inc(m.s_h_ex, 1)

    def h_turn(nxt, cur, prev):
        if nxt:
            n, k, _ = nxt
            act.wait_ge(m.s_h_tr, n + 1)
            act.activation(m.h_qt[:, k], m.g[:, 0, 0:T], ACT.Copy).then_inc(m.s_h_qc, 1)
            act.activation(m.h_kt[:, k].rearrange("p a t -> p (a t)"), m.g[:, 1, :], ACT.Identity, scale=-1.0, bias=1.0).then_inc(m.s_h_k1, 1)
            decays(n, 0, (0, 1))
        if prev:
            act.wait_ge(m.s_h_o, prev[0] + 1)
            act.activation(m.pc[:, :, bass.ds(HD * prev[0], HD)], m.t[:, 0, 0:T].rearrange("p (r e) -> p r e", r=2), ACT.Copy).then_inc(m.s_h_oc, 1)
        if nxt:
            decays(n, 0, (2, 3))
        if cur:
            act.wait_ge(m.s_h_am, 3 * cur[0] + 1)
            act.activation(m.h_at[:, 1:3, :], m.g[:, 0, T:2 * T].rearrange("p (a t) -> p a t", a=2), ACT.Copy).then_inc(m.s_h_off, 1)
        if nxt:
            decays(n, 1)
        if prev:
            act.wait_ge(m.s_h_oc, prev[0] + 1)
            lane.sync()
            for rb in range(RB):
                lane.did(act.activation(m.h_sq[:, rb], m.pc[:, rb, bass.ds(HD * prev[0], HD)], ACT.Square,
                                        accum_out=m.h_ms[:, rb, bass.ds(prev[0], 1)]))

    heads_three_deep(lane, {"step": 4}, h_turn, HH, 2)
    lane.sync()
    act.activation(m.h_sq[:, 0, 0:1], m.h_sq[:, 0, 0:1], ACT.Copy).then_inc(m.s_h_ms, 1)
    act.wait_ge(m.s_h_ms1, 1)
    act.activation(m.h_r[:], m.h_ms[:], ACT.Sqrt).then_inc(m.s_h_std, 1)
    high_columns(8, 4)
    high_unit("c_out", 0, 0)
    gemm("c_out", nothing, late=2)
    std(5)
    high_unit("mlp", 0, 0, [2, 3])
    for c in range(4):
        act.wait_ge(m.s_x_added, c + 1)
        for rb in range(RB):
            act.activation(m.mix[:, rb, 512 * c:512 * c + 512], m.res[:, rb, 512 * c:512 * c + 512], ACT.Square, accum_out=m.x_sq[:, rb, c:c + 1]).then_inc(m.s_x_sq, 1)
    std(6)
    high_columns(0, 8)
    mlp = PLAN["mlp"]

    def mlp_high(q, k, js=range(4)):
        high(mlp, mlp.v0 + 8 * q + k, mlp.g0 + 8 * q + k, js)

    def squares(q, k):
        act.wait_ge(m.s_w_used, 4 * (mlp.g0 + 8 * q + k) + 8)
        lane.did(act.activation(m.ur[:, k % 2], m.g[:, 2 * (k % 2):2 * (k % 2) + 2, :], ACT.Relu))
        act.wait_ge(m.s_act_step, lane.at())
        act.activation(m.ur[:, k % 2], m.ur[:, k % 2], ACT.Square).then_inc(m.s_g_free[k % 2], 1)

    def u_high(q, k):
        for half in range(2):
            b = (mlp_t0 + half) % 2
            act.wait_ge(m.s_t_full[b], (mlp_t0 + half) // 2 + 4 * q + k + 1)
            act.activation(m.uh[:, 4 * k + 2 * half:4 * k + 2 * half + 2, :], m.t[:, b, :].rearrange("p (k t) -> p k t", k=2), ACT.Copy)\
               .then_inc(m.s_x_high_ready, 1)

    mlp_t0 = lane.n["T"]

    def quarter(q, last):
        for k in range(8):
            if k == 4:
                mlp_high(q, 5, (0, 1))
                u_high(q, 3)
                mlp_high(q, 5, (2, 3))
            elif k < 7 or not last:
                mlp_high(q, k + 1)
            if k < 4:
                squares(q, k)
            if 1 <= k <= 3:
                u_high(q, k - 1)

    lane.loop(3, {"step": 4}, lambda q: quarter(q, False))
    quarter(3, True)
    std(7)


def vector_program(nc, dve, m, d):
    lane = Lane(dve, m.s_dve_step)
    stt = dve.scalar_tensor_tensor

    def low(st, v, g, js=range(4), aside=None):
        for j in js:
            dve.wait_ge(m.s_w_high, 4 * g + j + 1)
            s = (slice(None), j, slice(0, st.kq), slice(0, st.width))
            dve.tensor_tensor(m.lo[s], m.raw[s], m.hi[s].bitcast(F32), ALU.subtract).then_inc(m.s_raw_used, 1)
            if aside:
                aside(j)

    def low_unit(name, i, k, js=range(4), aside=None):
        st = PLAN[name]
        low(st, v_of(st, i, k), st.g0 + 2 * i + k, js, aside)

    def mod_piece(st, i):
        n, v = st.m0 + i, v_mod(st, i)
        dve.wait_ge(m.s_mod_summed, n + 1)
        dve.wait_ge(m.s_mod_stored, 16 * n + 16)
        for j in range(4):
            dve.wait_ge(m.s_landed[j], 16 * v + 16)
            for kk in range(4):
                c = 4 * j + kk
                if c == 0:
                    ins = dve.tensor_scalar(m.acc[:], m.raw[:, j, kk, :], m.ct[:, c:c + 1], None, ALU.mult)
                else:
                    ins = stt(m.acc[:], m.raw[:, j, kk, :], m.ct[:, c:c + 1], m.acc[:], ALU.mult, ALU.add)
                if kk < 3:
                    lane.link(ins)
                else:
                    ins.then_inc(m.s_raw_used, 1)
                    if j < 3:
                        dve.wait_ge(m.s_raw_used, 4 * v + j + 5)

    def mod_row(st, i):
        n = st.m0 + i
        dve.wait_ge(m.s_mod_summed, n + 2)
        dve.wait_ge(m.s_brow_landed, 16 * n + 16)
        dve.tensor_tensor(m.acc[0:1, :], m.u[0:1, 0, :], m.brow[:], ALU.add).then_inc(m.s_mod_row, 1)

    def gemm(name, take=None, next_too=True, late=0, aside=None, before_tail=None):
        st = PLAN[name]

        def by(u):
            return aside and (lambda j: aside(4 * u + j))

        def after(i, k):
            if take:
                dve.wait_ge(m.s_w_used, 4 * (st.g0 + 2 * i + k) + 8)
                take(st, i, k)

        def turn(i):
            low_unit(name, i, 1, aside=by(2 * i))
            if st.mods:
                mod_piece(st, i)
            after(i, 0)
            low_unit(name, i, 2, aside=by(2 * i + 1))
            after(i, 1)
            if st.mods:
                mod_row(st, i)

        def tail(i):
            if before_tail:
                before_tail()
            low_unit(name, i, 1, aside=by(2 * i))
            if late:
                after(i, 0)
            if st.mods:
                mod_piece(st, i)
            if not late:
                after(i, 0)
            if next_too:
                low_unit(st.next, 0, 0, range(min(3, 4 - late)), by(2 * i + 1))
            after(i, 1)
            if st.mods:
                mod_row(st, i)
            if next_too and not late:
                low_unit(st.next, 0, 0, [3], by(2 * i + 1))

        gemm_turns(lane, st, {"step": 12} if st.mods else {}, turn, tail)

    def low_columns(k0, uses):
        for q in range(uses):
            n = lane.n["T"]
            dve.wait_ge(m.s_x_high_ready, lane.n["xh"] + 1)
            k = slice(k0 + 2 * q, k0 + 2 * q + 2)
            dve.tensor_tensor(m.xl[:, k, :], m.t[:, n % 2, :].rearrange("p (k t) -> p k t", k=2), m.xh[:, k, :].bitcast(F32), ALU.subtract)\
               .then_inc(m.s_t_free[n % 2], 1)
            lane.n["T"] += 1
            lane.n["xh"] += 1

    def products_kept(name):
        st = PLAN[name]
        used = st.s0 + (4 if st.units == 1 else st.units)
        for b in range(2):
            dve.wait_ge(m.s_g_free[b], used // 2 + 1)

    def rope(x, heads, half, rates, rb, tmp, out=None):
        out = x if out is None else out
        view = [m.cs[:, c, rb, rates:rates + half].unsqueeze(1).unsqueeze(1).broadcast_to((P, heads, 2, half)) for c in range(2)]
        halves = x.rearrange("p h (a e) -> p h a e", a=2)
        by = [tmp[:, c, 0:heads * 2 * half].rearrange("p (h a e) -> p h a e", h=heads, a=2) for c in range(2)]
        for c in range(2):
            lane.did(dve.tensor_tensor(by[c], halves, view[c], ALU.mult))
        lane.sync()
        lane.did(dve.tensor_tensor(out[:, :, 0:half], by[0][:, :, 0, :], by[1][:, :, 1, :], ALU.subtract))
        lane.link(dve.tensor_tensor(out[:, :, half:2 * half], by[1][:, :, 0, :], by[0][:, :, 1, :], ALU.add))

    def inverse_std(n, columns=RB):
        dve.wait_ge(m.s_std_ready, n)
        lane.link(dve.reciprocal(m.rstd[:, 0:columns], m.rstd[:, 0:columns]))

    def spread(n_chunks):
        for rb in range(RB):
            lane.did(dve.bn_aggr(m.mv[:, rb, :], m.st[:, rb, 0:n_chunks, :]))
        lane.sync()

    def mean_square():
        mean, var = m.mv[:, 0:RB, 0], m.mv[:, 0:RB, 1]
        lane.link(dve.tensor_tensor(m.msq[:, 0:RB], mean, mean, ALU.mult))
        stt(m.msq[:, 0:RB], m.msq[:, 0:RB], RMS_EPS, var, ALU.add, ALU.add).then_inc(m.s_var_ready, 1)

    def chunk(c):
        return slice(512 * c, 512 * c + 512)

    lane.n["T"] = 1
    for c in range(4):
        low_columns(4 * c, 2)
        low_unit("a_qkv", 0, 0, [c])
    dve.wait_ge(m.s_pos_landed, 48)
    lane.link(dve.tensor_copy(m.posf[:], m.posi[:]))
    na = ROT_A + ROT_I
    for rb in range(RB):
        lane.did(dve.tensor_scalar(m.ang[:, rb, 0:na], m.rot[:, 0:na], m.posf[:, rb:rb + 1], None, ALU.mult))
        lane.did(dve.tensor_scalar(m.ang[:, rb, na:], m.rot[:, na:], m.posf[:, RB + rb:RB + rb + 1], None, ALU.mult))
    lane.sync()
    lane.link(dve.tensor_scalar(m.turns[:], m.ang[:], 0.15915494309189535, ROUND, ALU.mult, ALU.add))
    lane.link(dve.tensor_scalar(m.turns[:], m.turns[:], ROUND, None, ALU.subtract))
    for part in (TWO_PI_HI, TWO_PI_MID, TWO_PI_LO):
        lane.link(stt(m.ang[:], m.turns[:], -part, m.ang[:], ALU.mult, ALU.add))
    lane.link(dve.tensor_scalar(m.ang[:], m.ang[:], -3.1415925, 3.1415925, ALU.max, ALU.min))
    lane.link(stt(m.turns[:], m.ang[:], -1.0, m.ang[:], ALU.mult, ALU.max))
    dve.tensor_scalar(m.turns[:], m.turns[:], -1.0, 1.5707963267948966, ALU.mult, ALU.add).then_inc(m.s_angles_ready, 1)
    gemm("a_qkv")
    gemm("a_idx")

    products_kept("a_idx")
    dve.wait_ge(m.s_sin_ready, 2)
    for rb in range(RB):
        rope(m.pa[:, rb, 0:(NH + NKV) * HD].rearrange("p (h e) -> p h e", e=HD)[:, :, 0:2 * ROT_A], NH + NKV, ROT_A, 0, rb, m.a_rope)
        rope(m.pa[:, rb, 5120:5120 + (IDX_H + 1) * IDX_D].rearrange("p (h e) -> p h e", e=IDX_D)[:, :, 0:2 * ROT_I], IDX_H + 1, ROT_I, ROT_A, rb, m.a_rope)
    dve.memset(m.a_bias0[:, P:T], 0.0)
    dve.tensor_copy(m.a_bias0[:, 0:P], m.tri)
    lane.link(dve.tensor_copy(m.a_bias0[:, T:384], m.tri))
    dve.tensor_copy(m.a_score[:], m.a_bias0[:]).then_inc(m.s_a_ready, 1)
    dve.wait_ge(m.s_a_ready, 1)
    blocks = (slice(0, P), slice(P, 384))

    def index_aside(b):
        t, k = b - DOTS_AT, (b - DOTS_AT) % 2
        if 0 <= t < PAIRS:
            dve.wait_ge(m.s_a_relu, 2 * t + 2)
            for hh in range(2):
                for rb in range(RB):
                    s = m.a_score[:, blocks[rb]]
                    ins = stt(s, m.a_rl[:, k, hh, blocks[rb]], m.a_iws[:, k, rb, hh:hh + 1], s, ALU.mult, ALU.add)
                    if (hh, rb) != (1, 1):
                        lane.did(ins)
                if hh == 0:
                    lane.sync()
            ins.then_inc(m.s_a_idx_done, 1)
            dve.wait_ge(m.s_a_idx_done, t + 3)
        if b == BEST_AT:
            for _ in range(N_SEL // 8):
                for rb in range(RB):
                    lane.did(dve.max(m.a_top[:, rb, :], m.a_score[:, blocks[rb]]))
                lane.sync()
                for rb in range(RB):
                    lane.did(dve.match_replace(m.a_score[:, blocks[rb]], m.a_top[:, rb, :], m.a_score[:, blocks[rb]], TAKEN))
                lane.sync()
            lane.link(dve.tensor_scalar(m.a_bias[:], m.a_score[:], -2e38, NEG, ALU.is_gt, ALU.mult))
            dve.tensor_tensor(m.a_bias[:], m.a_bias[:], m.a_bias0[:], ALU.add).then_inc(m.s_a_biased, 1)
            dve.wait_ge(m.s_a_biased, 1)

    gemm("a_gate", aside=index_aside)
    products_kept("a_gate")

    def gated(t_bank, og, gate_col, proj, scale=None):
        for rb in range(RB):
            src, gate = m.t[:, t_bank, P * rb:P * rb + P], proj[:, rb, bass.ds(gate_col, HD)]
            if scale is None:
                ins = dve.tensor_tensor(og[:, rb], src, gate, ALU.mult)
            else:
                ins = stt(og[:, rb], src, scale[:, rb:rb + 1], gate, ALU.mult, ALU.mult)
            if rb == 0:
                lane.did(ins)
        return ins

    def head_low(bank, h):
        xl, xh = (x[:, bass.ds(h, 1), :].rearrange("p k t -> p (k t)") for x in (m.xl, m.xh))
        return dve.tensor_tensor(xl, m.t[:, bank, T:2 * T], xh.bitcast(F32), ALU.subtract)

    def a_turn(nxt, cur, prev):
        if prev:
            dve.wait_ge(m.s_a_xh, prev[0] + 1)
            head_low(prev[1] % 2, 4 * prev[1] + prev[2]).then_inc(m.s_a_done, 1)
        if nxt:
            n, k = nxt[0], nxt[1] % 2
            dve.wait_ge(m.s_a_s, n + 1)
            lane.link(stt(m.a_lg[:, k], m.g[:, 2 + k, 0:384], HD ** -0.5, m.a_bias[:], ALU.mult, ALU.add))
            lane.did(dve.tensor_reduce(m.a_nm[:, k, 0:1], m.a_lg[:, k, blocks[0]], AXX, ALU.max, negate=True))
            dve.tensor_reduce(m.a_nm[:, k, 1:2], m.a_lg[:, k, blocks[1]], AXX, ALU.max, negate=True).then_inc(m.s_a_nmax, 1)
        if cur:
            t, kc, h = cur[0], cur[1] % 2, 4 * cur[1] + cur[2]
            dve.wait_ge(m.s_a_p, 2 * t + 2)
            lane.link(dve.reciprocal(m.a_rs[:, kc], m.a_sum[:, kc]))
            dve.wait_ge(m.s_a_o, t + 1)
            gated(kc, m.a_og, 3072 + HD * h, m.pa, m.a_rs[:, kc]).then_inc(m.s_a_ogr, 1)

    heads_three_deep(lane, {"step": 16}, a_turn, NH, GROUP)

    def norm_and_embed(name_out, name_ple, layer):
        dve.wait_ge(m.s_x_landed, 32)

        def add(st, i, k):
            u, s = 2 * i + k, st.s0 // 2 + i
            stt(m.res[:, :, chunk(u)], m.res[:, :, chunk(u)], ALPHA, m.g[:, 2 * k:2 * k + 2, :], ALU.mult, ALU.add).then_inc(m.s_g_free[k], 1)
            dve.wait_ge(m.s_g_free[k], s + 2)
            for rb in range(RB):
                lane.did(dve.bn_stats(m.st[:, rb, u, :], m.res[:, rb, chunk(u)]))

        gemm(name_out, add, late=4)
        lane.sync()
        spread(4)
        dve.tensor_scalar(m.msq[:, 0:RB], m.mv[:, 0:RB, 1], LN_EPS, None, ALU.add).then_inc(m.s_var_ready, 1)
        lane.n["T"] += 1
        low_unit(name_ple, 0, 0, [0])
        dve.wait_ge(m.s_rows_landed, 32 * (layer + 1))
        inverse_std(layer + 1)
        for c in range(4):
            x = [m.res[:, rb, chunk(c)] for rb in range(RB)]
            for rb in range(RB):
                lane.did(stt(x[rb], x[rb], m.mv[:, rb, 0:1], m.row_g[:, chunk(c)], ALU.subtract, ALU.mult))
            lane.sync()
            for rb in range(RB):
                stt(x[rb], x[rb], m.rstd[:, rb:rb + 1], m.row_b[:, chunk(c)], ALU.mult, ALU.add).then_inc(m.s_y_ready, 1)
                lane.n["y"] += 1
            if c < 3:
                low_unit(name_ple, 0, 0, [c + 1])
            low_columns(4 * c, 2)
        dve.wait_ge(m.s_y_ready, lane.n["y"])

        def embed(st, i, k):
            u, s = 2 * i + k, st.s0 // 2 + i
            x = m.res[:, :, chunk(u)]
            if (layer, u) == (1, 2):
                dve.wait_ge(m.s_rows2_landed, 48)
                lane.did(stt(m.c_g1[:], m.c_sc[:], 1.0, m.c_g1[:], ALU.add, ALU.mult))
            dve.wait_ge(m.s_g_free[k], s + 2)
            dve.wait_ge(m.s_ple_full, 4 * layer + u + 1)
            dve.tensor_tensor(m.ple_s[:, k], m.ple_s[:, k], m.u[:], ALU.mult).then_inc(m.s_ple_free, 1)
            dve.wait_ge(m.s_ple_free, 4 * layer + u + 2)
            ins = dve.tensor_tensor(x, x, m.ple_s[:, k], ALU.add)
            if layer == 0:
                ins.then_inc(m.s_y_ready, 1)
                lane.n["y"] += 1
            else:
                ins.then_inc(m.s_x4_ready, 1)
                dve.wait_ge(m.s_x4_ready, u + 1)
                for rb in range(RB):
                    lane.did(dve.bn_stats(m.st[:, rb, u, :], m.res[:, rb, chunk(u)]))

        gemm(name_ple, embed, late=layer)

    norm_and_embed("a_out", "ple0", 0)
    low_columns(0, 8)
    gemm("b_kvq")
    gemm("b_gate", late=4)

    products_kept("b_gate")

    def masked_diagonal(x):
        x = x[:, 0:3:2, :].rearrange("p b (h t) -> p b h t", h=GROUP)
        return dve.tensor_tensor(x, x, m.lt.unsqueeze(1).unsqueeze(1).broadcast_to((P, 2, GROUP, P)), ALU.mult)

    def softplus(c):
        dve.wait_ge(m.s_b_l, c + 1)
        z, e = scores(m, c), (m.b_e[:, c, 0:2], m.b_e[:, c, 2])
        for n, sp in enumerate((m.b_sp[:, c, 0:2], m.b_sp[:, c, 2])):
            lane.did(stt(sp, z[n], 0.0, e[n], ALU.max, ALU.add))
        lane.sync()
        masked_diagonal(m.b_sp[:, c]).then_inc(m.s_b_spr, 1)
        for n in range(2):
            lane.did(stt(e[n], z[n], 0.0, e[n], ALU.min, ALU.subtract))

    def less_later(c):
        dve.wait_ge(m.s_b_sfx, c + 1)
        lane.sync()
        dve.tensor_tensor(m.b_e[:, c], m.b_e[:, c], m.g[:, 0:3, :], ALU.subtract).then_inc(m.s_b_a1, 1)

    def weights(c):
        dve.wait_ge(m.s_b_ex, c + 1)
        masked_diagonal(m.b_e[:, c]).then_inc(m.s_b_w, 1)

    def gate_group(c):
        dve.wait_ge(m.s_b_o, c + 1)
        g = 3072 + GROUP * HD * c
        dve.tensor_tensor(m.b_og[:, c % 2], m.u[:], m.pb[:, :, g:g + GROUP * HD], ALU.mult).then_inc(m.s_b_ogr, 1)

    def group_low(c):
        dve.wait_ge(m.s_b_xh, c + 1)
        xl, xh = (x[:, GROUP * c:GROUP * c + GROUP, :].rearrange("p (a k) t -> p a (k t)", a=2) for x in (m.xl, m.xh))
        dve.tensor_tensor(xl, m.t[:], xh.bitcast(F32), ALU.subtract).then_inc(m.s_b_done, 1)

    softplus(0)
    softplus(1)
    less_later(0)
    weights(0)
    less_later(1)
    softplus(2)
    gate_group(0)
    weights(1)
    less_later(2)
    softplus(3)
    group_low(0)
    gate_group(1)
    weights(2)
    less_later(3)
    group_low(1)
    gate_group(2)
    weights(3)
    low_unit("b_out", 0, 0, [0])
    group_low(2)
    gate_group(3)
    low_unit("b_out", 0, 0, [1])
    group_low(3)
    low_unit("b_out", 0, 0, [2, 3])
    norm_and_embed("b_out", "ple1", 1)

    def normed(x, gain, shift, out, following, left):
        for c in range(4):
            for rb in range(RB):
                lane.did(stt(out[:, rb, chunk(c)], x[:, rb, chunk(c)], m.rstd[:, rb:rb + 1], gain[:, chunk(c)], ALU.mult, ALU.mult))
            lane.sync()
            o = out[:, :, chunk(c)]
            dve.tensor_tensor(o, o, shift[:, chunk(c)].unsqueeze(1).broadcast_to((P, RB, 512)), ALU.add).then_inc(m.s_y_ready, 1)
            lane.n["y"] += 1
            if c < len(left):
                low_unit(following, 0, 0, [left[c]])
            low_columns(4 * c, 2)

    lane.sync()
    spread(4)
    mean_square()
    inverse_std(3)
    normed(m.res, m.c_g1, m.c_sh, m.c_h, "c_hq", [3])
    def forget_gates(dr):
        products_kept("c_f")
        dve.wait_ge(m.s_h_rows, 64)
        bound = m.h_l0[:, dr, 0]
        dve.tensor_tensor(bound, bound, m.h_l0[:, dr, 1], ALU.subtract).then_inc(m.s_h_lb, 1)
        f = m.pc[:, :, 1024 * (dr + 1):1024 * (dr + 2)]
        lane.link(dve.tensor_scalar(m.h_t[:], f, -1.0, 1.0, ALU.mult, ALU.add))
        dve.wait_ge(m.s_h_lbs, dr + 1)
        lane.link(dve.tensor_tensor(m.h_t[:], m.h_t[:], bound.unsqueeze(1).broadcast_to((P, RB, 1024)), ALU.mult))
        dve.tensor_tensor(f, f, m.h_t[:], ALU.add).then_inc(m.s_h_fr, 1)
        dve.wait_ge(m.s_h_fr, dr + 1)

    gemm("c_hq")
    gemm("c_f")
    gemm("c_hi")
    forget_gates(0)
    gemm("c_hg")
    forget_gates(1)
    gemm("c_mla")

    products_kept("c_mla")
    parts = ((slice(0, QRANK), 0), (slice(QRANK, QRANK + KVRANK), RB))
    for s, n in parts:
        for rb in range(RB):
            lane.did(dve.bn_stats(m.st[:, rb, n // RB, :], m.pm[:, rb, s]))
    lane.sync()
    for s, n in parts:
        for rb in range(RB):
            lane.did(dve.bn_aggr(m.mv[:, n + rb, :], m.st[:, rb, n // RB:n // RB + 1, :]))
    lane.sync()
    lane.link(dve.tensor_tensor(m.msq[:], m.mv[:, :, 0], m.mv[:, :, 0], ALU.mult))
    stt(m.msq[:], m.msq[:], RMS_EPS, m.mv[:, :, 1], ALU.add, ALU.add).then_inc(m.s_var_ready, 1)
    dve.wait_ge(m.s_mod_stored, 16 * (PLAN["c_mla"].m0 + 1) + 16)
    lane.link(dve.memset(m.m_krd[:], 0.0))
    for rb in range(RB):
        rope(m.pm[:, rb:rb + 1, QRANK + KVRANK:], 1, ROT_M, na, rb, m.m_rope, m.m_krd[:, rb:rb + 1, 0:ROPE])
    dve.wait_ge(m.s_rows2_landed, 80)
    inverse_std(4, 2 * RB)
    for s, n in parts:
        for rb in range(RB):
            ins = stt(m.pm[:, rb, s], m.pm[:, rb, s], m.rstd[:, n + rb:n + rb + 1], m.m_rg[:, s], ALU.mult, ALU.mult)
            if n + rb < 2 * RB - 1:
                lane.did(ins)
    ins.then_inc(m.s_y_ready, 1)
    lane.n["y"] += 1
    low_columns(8, 3)
    ukv = PLAN["ukv"]
    low(ukv, ukv.v0, ukv.g0)
    products_kept("uq")
    dve.wait_ge(m.s_raw_used, 4 * ukv.v0 + 8)
    for rb in range(RB):
        rope(m.mq[:, rb, :].rearrange("p (h e) -> p h e", e=NOPE + ROPE)[:, :, NOPE:], MH, ROT_M, na, rb, m.m_rope2)
    products_kept("ukv")
    dve.memset(m.m_nm[:], 0.0).then_inc(m.s_m_ready, 1)
    dve.wait_ge(m.s_m_ready, 1)
    mscale = (NOPE + ROPE) ** -0.5

    def m_turn(nxt, cur, prev):
        if prev:
            dve.wait_ge(m.s_m_xh, prev[0] + 1)
            head_low(prev[1], prev[0]).then_inc(m.s_m_done, 1)
        if nxt:
            n, k, _ = nxt
            dve.wait_ge(m.s_m_s, n + 1)
            lane.link(dve.tensor_reduce(m.m_nm[:, k], m.g[:, 2 + k, :].rearrange("p (r s) -> p r s", r=RB), AXX, ALU.max, negate=True))
            dve.tensor_scalar(m.m_nm[:, k], m.m_nm[:, k], mscale, None, ALU.mult).then_inc(m.s_m_nmax, 1)
        if cur:
            t, kc, _ = cur
            dve.wait_ge(m.s_m_p, 2 * t + 2)
            lane.link(dve.reciprocal(m.m_rs[:, kc], m.m_sum[:, kc]))
            dve.wait_ge(m.s_m_o, t + 1)
            for rb in range(RB):
                ins = dve.tensor_scalar(m.m_og[:, rb], m.t[:, kc, P * rb:P * rb + P], m.m_rs[:, kc, rb:rb + 1], None, ALU.mult)
                if rb == 0:
                    lane.did(ins)
            ins.then_inc(m.s_m_ogr, 1)

    heads_three_deep(lane, {"step": 6}, m_turn, MH, 2)
    dve.wait_ge(m.s_h_consts, 48)

    def decayed(k, group):
        for l in range(4):
            half = P >> (4 * group + l)

            def side(ap, s):
                return ap.rearrange("p (b s h) -> p b s h", s=2, h=half)[:, :, s, :]

            e = [m.h_e[:, group, dr, l] for dr in range(2)]
            for s in range(2):
                lane.did(dve.tensor_tensor(side(m.h_kq[:, group, 0, l], s), side(m.h_kt[:, k, s], s), side(e[s], s), ALU.mult))
                ins = dve.tensor_tensor(side(m.h_kq[:, group, 1, l], s), side(m.h_qt[:, k], s), side(e[1 - s], s), ALU.mult)
                if (l, s) != (3, 1):
                    lane.did(ins)
        ins.then_inc(m.s_h_mul, 1)

    def masked(levels, n0):
        n = len(levels)
        return dve.tensor_tensor(m.h_tm[:, :, n0:n0 + n, :], m.t[:, :, 0:P * n].rearrange("p b (l t) -> p b l t", l=n),
                                 m.h_mask[:, n0:n0 + n, :].unsqueeze(1).broadcast_to((P, RB, n, P)), ALU.mult)

    def h_turn(nxt, cur, prev):
        if nxt:
            n, k, _ = nxt
            dve.wait_ge(m.s_h_k1, n + 1)
            dve.tensor_tensor(m.h_ks[:, k], m.h_kt[:, k, 0], m.h_kt[:, k, 1], ALU.add).then_inc(m.s_h_kc, 1)
        if cur:
            t = cur[0]
            dve.wait_ge(m.s_h_am, 3 * t + 1)
            masked(range(3), 0).then_inc(m.s_h_msk, 1)
        if nxt:
            dve.wait_ge(m.s_h_qc, n + 1)
            dve.wait_ge(m.s_h_ex, 8 * n + 4)
            decayed(k, 0)
        if cur:
            dve.wait_ge(m.s_h_am, 3 * t + 3)
            dve.tensor_tensor(m.h_tm[:, :, 7, :], m.g[:, 1, 0:T].rearrange("p (b t) -> p b t", b=RB),
                              m.h_mask[:, 7:8, :].broadcast_to((P, RB, P)), ALU.mult).then_inc(m.s_h_dg, 1)
            lane.link(masked(range(4), 3))
            dve.wait_ge(m.s_h_dg, t + 1)
            if prev:
                dve.wait_ge(m.s_h_o, prev[0] + 1)
            lane.did(dve.tensor_reduce(m.h_at[:, 0], m.h_tm[:, 0].rearrange("p l t -> p t l"), AXX, ALU.add))
            dve.tensor_reduce(m.h_at[:, 3], m.h_tm[:, 1].rearrange("p l t -> p t l"), AXX, ALU.add).then_inc(m.s_h_red, 1)
        if nxt:
            dve.wait_ge(m.s_h_ex, 8 * n + 8)
            decayed(k, 1)

    heads_three_deep(lane, {"step": 64}, h_turn, HH, 2)
    dve.wait_ge(m.s_h_ms, 1)
    o = m.pc[:, :, 0:1024]
    dve.tensor_scalar(m.h_ms[:], m.h_ms[:], 1.0 / HD, RMS_EPS, ALU.mult, ALU.add).then_inc(m.s_h_ms1, 1)
    dve.wait_ge(m.s_h_std, 1)
    lane.link(dve.reciprocal(m.h_r[:], m.h_r[:]))
    for rb in range(RB):
        heads = o[:, rb].rearrange("p (h e) -> p h e", h=HH)
        lane.did(dve.tensor_tensor(heads, heads, m.h_r[:, rb].unsqueeze(2).broadcast_to((P, HH, HD)), ALU.mult))
    lane.sync()
    dve.wait_ge(m.s_h_gain, RB)
    dve.tensor_tensor(o, o, m.pc[:, :, 4096:5120], ALU.mult).then_inc(m.s_y_ready, 1)
    lane.n["y"] += 1
    low_columns(8, 4)

    low_unit("c_out", 0, 0)

    def keep_mix(st, i, k):
        u, s = 2 * i + k, st.s0 // 2 + i
        dve.tensor_copy(m.mix[:, :, chunk(u)], m.g[:, 2 * k:2 * k + 2, :]).then_inc(m.s_g_free[k], 1)
        dve.wait_ge(m.s_g_free[k], s + 2)
        for rb in range(RB):
            lane.did(dve.bn_stats(m.st[:, rb, u, :], m.mix[:, rb, chunk(u)]))

    def gains():
        dve.wait_ge(m.s_rows2_landed, 160)
        lane.did(dve.tensor_tensor(m.x_pg[:], m.x_pg[:], m.x_ga[:], ALU.mult))
        lane.did(stt(m.x_g1[:], m.x_sc[:], 1.0, m.x_g1[:], ALU.add, ALU.mult))

    def into_residual(y, gain, done):
        for c in range(4):
            for rb in range(RB):
                lane.did(stt(y[:, rb, chunk(c)], y[:, rb, chunk(c)], m.rstd[:, rb:rb + 1], gain[:, chunk(c)], ALU.mult, ALU.mult))
            lane.sync()
            ins = dve.tensor_tensor(m.res[:, :, chunk(c)], m.res[:, :, chunk(c)], y[:, :, chunk(c)], ALU.add)
            ins.then_inc(done, 1)

    gemm("c_out", keep_mix, late=4, before_tail=gains)
    lane.sync()
    spread(4)
    mean_square()
    dve.wait_ge(m.s_res2_landed, 16)
    inverse_std(5)
    into_residual(m.mix, m.x_pg, m.s_x_added)
    low_unit("mlp", 0, 0, [0])
    dve.wait_ge(m.s_x_sq, 2 * 4)
    lane.link(dve.tensor_reduce(m.msq[:, 0:RB], m.x_sq[:], AXX, ALU.add))
    dve.tensor_scalar(m.msq[:, 0:RB], m.msq[:, 0:RB], 1.0 / D, RMS_EPS, ALU.mult, ALU.add).then_inc(m.s_var_ready, 1)
    inverse_std(6)
    normed(m.res, m.x_g1, m.x_sh, m.mix, "mlp", [1, 2, 3])

    lane.link(dve.memset(m.y[:], 0.0))
    mlp = PLAN["mlp"]
    t0, x0 = lane.n["T"], lane.n["xh"]

    def hidden_low(q, k):
        for half in range(2):
            b = (t0 + half) % 2
            dve.wait_ge(m.s_x_high_ready, x0 + 8 * q + 2 * k + half + 1)
            s = slice(4 * k + 2 * half, 4 * k + 2 * half + 2)
            dve.tensor_tensor(m.ul[:, s, :], m.t[:, b, :].rearrange("p (k t) -> p k t", k=2), m.uh[:, s, :].bitcast(F32), ALU.subtract)\
               .then_inc(m.s_t_free[b], 1)

    def hidden_quarter(q, last):
        for k in range(8):
            if k == 4:
                low(mlp, mlp.v0 + 8 * q + 5, mlp.g0 + 8 * q + 5, (0, 1))
                hidden_low(q, 3)
                low(mlp, mlp.v0 + 8 * q + 5, mlp.g0 + 8 * q + 5, (2, 3))
            elif k < 7 or not last:
                low(mlp, mlp.v0 + 8 * q + k + 1, mlp.g0 + 8 * q + k + 1)
            if 1 <= k <= 3:
                hidden_low(q, k - 1)
            if k >= 4:
                dve.wait_ge(m.s_w_used, 4 * (mlp.g0 + 8 * q + k) + 8)
                y = m.y[:, :, chunk(k - 4)]
                dve.tensor_tensor(y, y, m.g[:, 2 * (k % 2):2 * (k % 2) + 2, :], ALU.add).then_inc(m.s_g_free[k % 2], 1)
                if last:
                    dve.wait_ge(m.s_g_free[k % 2], mlp.s0 // 2 + 4 * q + k // 2 + 2)
                    for rb in range(RB):
                        lane.did(dve.bn_stats(m.st[:, rb, k - 4, :], m.y[:, rb, chunk(k - 4)]))
                if last and k == 6:
                    dve.wait_ge(m.s_rows2_landed, 192)
                    lane.did(dve.tensor_tensor(m.z_pg[:], m.z_pg[:], m.z_gm[:], ALU.mult))

    lane.loop(3, {}, lambda q: hidden_quarter(q, False))
    hidden_quarter(3, True)
    lane.sync()
    spread(4)
    mean_square()
    inverse_std(7)
    into_residual(m.y, m.z_pg, m.s_mlp_done)


def tensor_program(nc, pe, m, d):
    lane = Lane(pe, m.s_pe_step)

    def quarter(st, v, g, j, pair, x0, first, last, xh=m.xh, xl=m.xl):
        pe.wait_ge(m.s_raw_used, 4 * v + j + 5)
        for kk in range(st.kq):
            for rb in range(RB):
                a, w = slice(P * rb, P * rb + P), (j, kk, slice(0, st.width))
                bank = m.g[:, 2 * pair + rb, 0:st.width]
                parts = ((xh, m.hi), (xh, m.lo), (xl, m.hi))
                for n, (x, wt) in enumerate(parts):
                    ins = pe.matmul(bank, x[:, x0 + kk, a], wt[(slice(None),) + w],
                                    start=first and kk == 0 and n == 0, stop=last and kk == st.kq - 1 and n == 2)
        ins.then_inc(m.s_w_used, 1)

    def unit(st, v, g, half_s, pair, xh=m.xh, xl=m.xl, aside=None):
        pe.wait_ge(m.s_g_free[pair], half_s + 1)
        for j in range(4):
            quarter(st, v, g, j, pair, 4 * j, j == 0, j == 3, xh, xl)
            if aside:
                aside(j)

    def gemm(name, after=None, first=None, aside=None):
        st = PLAN[name]

        def pair(i, first=None):
            for k in range(2):
                if first and k == 0:
                    first(st)
                else:
                    unit(st, v_of(st, i, k), st.g0 + 2 * i + k, st.s0 // 2 + i, k, aside=aside and (lambda j: aside(4 * (2 * i + k) + j)))
                if after:
                    after(2 * i + k)
            if st.mods:
                pe.wait_ge(m.s_raw_used, 4 * v_mod(st, i) + 8)
                pe.matmul(m.u[0:1, 0, :], m.ones[:, 0:1], m.acc[:], start=True, stop=True).then_inc(m.s_mod_summed, 1)

        if aside:
            for i in range(st.units // 2):
                pair(i)
        elif first:
            pair(0, first)
            lane.loop(st.units // 2 - 1, {}, pair, 1)
        else:
            lane.loop(st.units // 2, {}, pair)

    def bank_for_columns():
        n = lane.n["T"]
        pe.wait_ge(m.s_t_free[n % 2], n // 2 + 1)
        lane.n["T"] += 1
        return n % 2

    def blocks(b, src):
        for kt in range(2):
            for rb in range(RB):
                ins = pe.transpose(m.t[:, b, T * kt + P * rb:T * kt + P * rb + P], src(kt, rb), m.ident)
        ins.then_inc(m.s_t_full[b], 1)

    def columns(x, uses, y_total=0, per_chunk=0):
        base = lane.n["y"]
        for q in range(uses):
            if per_chunk:
                pe.wait_ge(m.s_y_ready, base + per_chunk * (q // 2 + 1))
            b = bank_for_columns()
            blocks(b, lambda kt, rb: x[:, rb, T * q + P * kt:T * q + P * kt + P])
        lane.n["y"] += y_total

    def arriving(x, y_total, per_chunk):
        def go(st):
            n, y = lane.n["T"], lane.n["y"]
            pe.wait_ge(m.s_g_free[0], st.s0 // 2 + 1)

            def product(j):
                for b in range(2):
                    pe.wait_ge(m.s_t_free[b], (n + 2 * j + 2 + 1 - b) // 2 + 1)
                quarter(st, st.v0, st.g0, j, 0, 4 * j, j == 0, j == 3)

            for c in range(4):
                if per_chunk:
                    pe.wait_ge(m.s_y_ready, y + per_chunk * (c + 1))
                for q in (2 * c, 2 * c + 1):
                    blocks(bank_for_columns(), lambda kt, rb: x[:, rb, T * q + P * kt:T * q + P * kt + P])
                if c:
                    product(c - 1)
            product(3)
            lane.n["y"] += y_total
        return go

    def columns_split():
        n = lane.n["T"]
        for b in range(2):
            pe.wait_ge(m.s_t_free[b], (n + 1 - b) // 2 + 1)

    def pieces(dst, src, n, sem):
        for a in range(n):
            ins = pe.transpose(dst(a), src(a), m.ident)
        ins.then_inc(sem, 1)

    pe.wait_ge(m.s_const_landed, 32)
    b = bank_for_columns()
    pe.transpose(m.t[:, b, 0:KT], m.crow[:], m.const[0:KT, C_IDENT:C_IDENT + KT]).then_inc(m.s_t_full[b], 1)
    pe.wait_ge(m.s_x_landed, 16)
    gemm("a_qkv", None, arriving(m.res, 0, 0))
    gemm("a_idx")

    def keys(src, col0, banks):
        for kv in range(NKV):
            for rb in range(RB):
                c = T * (kv % 2) + P * rb
                ins = pe.transpose(banks[:, kv // 2, c:c + P], src[:, rb, col0 + HD * kv:col0 + HD * kv + HD], m.ident)
        return ins

    def index_aside(b):
        if b == KEYS_AT:
            pe.wait_ge(m.s_a_ready, 1)
            keys(m.pa, 2048, m.t).then_inc(m.s_a_ktp, 1)
            pe.wait_ge(m.s_a_k_t, 2)
            pieces(lambda rb: m.u[:, 1, P * rb:P * rb + P], lambda rb: m.a_ikd[:, rb].rearrange("p a e -> p (a e)"), RB, m.s_a_ktp)
        t = b - DOTS_AT
        if 0 <= t < PAIRS:
            pe.wait_ge(m.s_a_iqc, t + 1)
            if t:
                pe.wait_ge(m.s_a_relu, 2 * t)
            for hh, bank in enumerate((m.t[:, 1], m.u[:, 1])):
                e = slice(IDX_D * hh, IDX_D * hh + IDX_D)
                pe.matmul(bank[:, 0:P], m.a_iqt[e, t % 2, 0:P], m.a_ikt[e, 0:P], start=True, stop=True)
                ins = pe.matmul(bank[:, P:384], m.a_iqt[e, t % 2, P:T], m.a_ikt[e, :], start=True, stop=True)
            ins.then_inc(m.s_a_dots, 1)
        t = b - DOTS_AT + 1
        if 0 <= t < PAIRS:
            pe.wait_ge(m.s_a_iq, 2 * t + 2)
            if t == 0:
                pe.wait_ge(m.s_a_k_copied, 2)
            pieces(lambda rb: m.t[:, 0, P * rb:P * rb + P], lambda rb: m.a_iqs[:, t % 2, rb], RB, m.s_a_iqt)

    gemm("a_gate", aside=index_aside)
    gate = PLAN["a_gate"]
    for b in range(2):
        pe.wait_ge(m.s_g_free[b], (gate.s0 + gate.units) // 2 + 1)

    def attend(probs, v, out):
        pe.matmul(out[:, 0:P], probs[:, 0:P], v(0), start=True, stop=True)
        pe.matmul(out[:, P:T], probs[:, P:T], v(0), start=True, stop=False)
        return pe.matmul(out[:, P:T], probs[:, T:384], v(1), start=False, stop=True)

    def a_turn(nxt, cur, prev):
        if nxt:
            n, kv, k = nxt[0], nxt[1], nxt[1] % 2
            pe.wait_ge(m.s_a_q, n + 1)
            pieces(lambda rb: m.g[:, k, P * rb:P * rb + P], lambda rb: m.a_qs[:, k, rb], RB, m.s_a_qtp)
        if cur:
            t, kvc, kc = cur[0], cur[1], cur[1] % 2
            pe.wait_ge(m.s_a_p, 2 * t + 2)
            pieces(lambda a: m.u[:, kc, P * a:P * a + P], lambda a: m.a_lg[:, kc, P * a:P * a + P], 3, m.s_a_ptp)
        if prev:
            pt, kp = prev[0], prev[1] % 2
            pe.wait_ge(m.s_a_ogr, pt + 1)
            pe.wait_ge(m.s_a_done, pt + 1)
            pieces(lambda rb: m.t[:, kp, T + P * rb:T + P * rb + P], lambda rb: m.a_og[:, rb], RB, m.s_a_ogt)
        if nxt:
            pe.wait_ge(m.s_a_qtc, n + 1)
            pe.matmul(m.g[:, 2 + k, 0:P], m.a_qt[:, k, 0:P], m.a_kt[:, kv, 0:P], start=True, stop=True)
            pe.matmul(m.g[:, 2 + k, P:384], m.a_qt[:, k, P:T], m.a_kt[:, kv, :], start=True, stop=True).then_inc(m.s_a_s, 1)
        if cur:
            pe.wait_ge(m.s_a_ptc, t + 1)
            v = 2560 + HD * kvc
            attend(m.a_pt[:, kc], lambda s: m.pa[:, s, v:v + HD], m.t[:, kc]).then_inc(m.s_a_o, 1)

    heads_three_deep(lane, {}, a_turn, NH, GROUP)
    pe.wait_ge(m.s_a_done, NH + 2)

    def norm_and_embed(name_out, name_ple, layer):
        gemm(name_out)
        pe.wait_ge(m.s_ple_landed, 32 * (layer + 1))
        blocks(bank_for_columns(), lambda kt, rb: m.ple_p[:, rb, P * kt:P * kt + P])

        def embed(u):
            pe.wait_ge(m.s_ple_free, 4 * layer + u + 1)
            for rb in range(RB):
                for k in range(2):
                    ins = pe.matmul(m.u[:, rb, :], m.ple_pt[:, k, P * rb:P * rb + P], m.ple_w[:, k, bass.ds(512 * u, 512)],
                                    start=k == 0, stop=k == 1)
            ins.then_inc(m.s_ple_full, 1)

        gemm(name_ple, embed, arriving(m.res, 8, 2))

    norm_and_embed("a_out", "ple0", 0)
    gemm("b_kvq", None, arriving(m.res, 4, 1))

    kvq = PLAN["b_kvq"]

    def scores_aside(b):
        if b == KEYS_AT:
            for k in range(2):
                pe.wait_ge(m.s_g_free[k], (kvq.s0 + kvq.units) // 2 + 1)
            columns_split()
            keys(m.pb, 0, m.t).then_inc(m.s_b_k_t, 1)
        t = b - DOTS_AT
        if 0 <= t < B_PAIRS:
            pe.wait_ge(m.s_b_qtc, t + 1)
            if t:
                pe.wait_ge(m.s_b_zc, 4 * t)
            for hh, bank in enumerate((m.t[:, 1], m.u[:, 1])):
                kv, q = (2 * t + hh) // GROUP, m.b_qt[:, t % 2, T * hh:T * hh + T]
                pe.matmul(bank[:, 0:T], m.b_kt[:, kv, 0:P], q, start=True, stop=True)
                ins = pe.matmul(bank[:, T:384], m.b_kt[:, kv, P:T], q[:, P:T], start=True, stop=True)
            ins.then_inc(m.s_b_z, 1)
        t = b - DOTS_AT + 1
        if 0 <= t < B_PAIRS:
            if t == 0:
                pe.wait_ge(m.s_b_k_copied, 1)
            pieces(lambda a: m.t[:, 0, P * a:P * a + P],
                   lambda a: m.pb[:, a % 2, 1024 + HD * (2 * t + a // 2):1024 + HD * (2 * t + a // 2) + HD], 4, m.s_b_qtp)

    gemm("b_gate", aside=scores_aside)
    gate = PLAN["b_gate"]
    for k in range(2):
        pe.wait_ge(m.s_g_free[k], (gate.s0 + gate.units) // 2 + 1)

    def later_sums(c):
        pe.wait_ge(m.s_b_spr, c + 1)
        if c:
            pe.wait_ge(m.s_b_a1, c)
        for n in (0, 2):
            pe.matmul(m.g[:, n], m.gt, m.b_sp[:, c, n], start=True, stop=True)
        pe.matmul(m.g[:, 1], m.gt, m.b_sp[:, c, 1], start=True, stop=False)
        pe.matmul(m.g[:, 1], m.ones, m.b_sp[:, c, 2], start=False, stop=True).then_inc(m.s_b_sfx, 1)

    def attend_group(c):
        pe.wait_ge(m.s_b_w, c + 1)
        if c:
            pe.wait_ge(m.s_b_ogr, c)
        v = [m.pb[:, s, 512 + HD * c:512 + HD * c + HD] for s in range(RB)]
        for hh in range(GROUP):
            h = slice(HD * hh, HD * hh + HD)
            pe.matmul(m.u[:, 0, h], m.b_e[:, c, 0, h], v[0], start=True, stop=True)
            pe.matmul(m.u[:, 1, h], m.b_e[:, c, 1, h], v[0], start=True, stop=False)
            ins = pe.matmul(m.u[:, 1, h], m.b_e[:, c, 2, h], v[1], start=False, stop=True)
        ins.then_inc(m.s_b_o, 1)

    def group_columns(c):
        pe.wait_ge(m.s_b_ogr, c + 1)
        if c:
            pe.wait_ge(m.s_b_done, c)
        pieces(lambda a: m.t[:, a // 4, P * (a % 4):P * (a % 4) + P],
               lambda a: m.b_og[:, c % 2, a % 2, HD * (a // 2):HD * (a // 2) + HD], 2 * GROUP, m.s_b_ogt)

    later_sums(0)
    later_sums(1)
    attend_group(0)
    later_sums(2)
    group_columns(0)
    attend_group(1)
    later_sums(3)
    for c in range(1, NKV):
        group_columns(c)
        if c + 1 < NKV:
            attend_group(c + 1)
    pe.wait_ge(m.s_b_done, NKV)
    norm_and_embed("b_out", "ple1", 1)
    gemm("c_hq", None, arriving(m.c_h, 4, 1))
    for name in ("c_f", "c_hi", "c_hg", "c_mla"):
        gemm(name)
    pe.wait_ge(m.s_y_ready, lane.n["y"] + 1)
    columns(m.pm, 3, 1)
    columns_split()
    for name, x0 in (("uq", 8), ("ukv", 12)):
        st = PLAN[name]
        for j in range(4):
            pe.wait_ge(m.s_g_free[j % 2], (st.s0 + j) // 2 + 1)
            quarter(st, st.v0, st.g0, j, j % 2, x0, True, True)
    pe.wait_ge(m.s_m_ready, 1)
    pieces(lambda rb: m.t[:, 0, P * rb:P * rb + P], lambda rb: m.m_krd[:, rb], RB, m.s_m_krt_t)
    pe.wait_ge(m.s_m_krt_c, 1)
    for h in range(MH):
        for rb in range(RB):
            c = T * (h % 2) + P * rb
            ins = pe.transpose(m.g[:, h // 2, c:c + P], m.mkv[:, rb, (NOPE + VD) * h:(NOPE + VD) * h + NOPE], m.ident)
        if h % 2:
            ins.then_inc(m.s_m_ktp, 1)
    pe.wait_ge(m.s_m_ktc, 4)

    def m_turn(nxt, cur, prev):
        if nxt:
            n, k, _ = nxt
            pe.wait_ge(m.s_m_q, n + 1)
            pieces(lambda a: m.g[:, k, P * a:P * a + P], lambda a: m.m_qs[:, k, a % 2, P * (a // 2):P * (a // 2) + P], 4, m.s_m_qtp)
        if cur:
            t, kc, _ = cur
            pe.wait_ge(m.s_m_p, 2 * t + 2)
            pieces(lambda a: m.u[:, kc, P * a:P * a + P], lambda a: m.m_lg[:, kc, a // 2, P * (a % 2):P * (a % 2) + P], 4, m.s_m_ptp)
        if prev:
            pt, kp, _ = prev
            pe.wait_ge(m.s_m_ogr, pt + 1)
            pe.wait_ge(m.s_m_done, pt + 1)
            pieces(lambda rb: m.t[:, kp, T + P * rb:T + P * rb + P], lambda rb: m.m_og[:, rb], RB, m.s_m_ogt)
        if nxt:
            pe.wait_ge(m.s_m_qtc, n + 1)
            keys_t = m.m_ktt[:, bass.ds(n, 1), :].rearrange("p h t -> p (h t)")
            for rb in range(RB):
                rows_, out = slice(P * rb, P * rb + P), m.g[:, 2 + k, T * rb:T * rb + T]
                pe.matmul(out, m.m_qt[:, k, 0, rows_], keys_t, start=True, stop=False)
                ins = pe.matmul(out, m.m_qt[:, k, 1, rows_], m.m_krt[:], start=False, stop=True)
            ins.then_inc(m.s_m_s, 1)
        if cur:
            pe.wait_ge(m.s_m_ptc, t + 1)
            for rb in range(RB):
                for s in range(RB):
                    ins = pe.matmul(m.t[:, kc, P * rb:P * rb + P], m.m_pt[:, kc, rb, P * s:P * s + P],
                                    m.mkv[:, s, bass.ds((NOPE + VD) * t + NOPE, VD)], start=s == 0, stop=s == 1)
            ins.then_inc(m.s_m_o, 1)

    heads_three_deep(lane, {}, m_turn, MH, 2)
    pe.wait_ge(m.s_m_done, MH + 2)
    pe.wait_ge(m.s_h_consts, 48)

    def spans(k, group):
        for dr in range(2):
            for blk, bank in enumerate(((m.g[:, 2], m.g[:, 3]), (m.u[:, 0], m.u[:, 1]))[dr]):
                lf = m.h_lf[:, k, dr, blk, :]
                if group:
                    ins = pe.matmul(bank, lf, m.h_md[:, dr, 5:9, :].rearrange("p l t -> p (l t)"), start=True, stop=True)
                elif blk == 0:
                    ins = pe.matmul(bank, lf, m.h_md[:, dr, 0:4, :].rearrange("p l t -> p (l t)"), start=True, stop=True)
                else:
                    pe.matmul(bank[:, 0:P], lf, m.h_md[:, dr, 4, :], start=True, stop=True)
                    ins = pe.matmul(bank[:, P:512], lf, m.h_md[:, dr, 1:4, :].rearrange("p l t -> p (l t)"), start=True, stop=True)
        ins.then_inc(m.s_h_d, 1)

    def block_products(group, levels):
        for blk in range(RB):
            b = slice(P * blk, P * blk + P)
            for n, l in enumerate(levels):
                ins = pe.matmul(m.t[:, blk, P * n:P * n + P], m.h_kq[:, group, 0, l, b], m.h_kq[:, group, 1, l, b], start=True, stop=True)
        ins.then_inc(m.s_h_am, 1)

    def h_turn(nxt, cur, prev):
        if nxt:
            n, k, _ = nxt
            pe.wait_ge(m.s_h_q, 5 * n + 3)
            if cur:
                pe.wait_ge(m.s_h_qc, cur[0] + 1)
                pe.wait_ge(m.s_h_kc, cur[0] + 1)
            if prev:
                pe.wait_ge(m.s_h_off, prev[0] + 1)
                pe.wait_ge(m.s_h_dg, prev[0] + 1)
            for rb in range(RB):
                pe.transpose(m.g[:, 0, P * rb:P * rb + P], m.h_qs[:, k, rb], m.ident)
            pieces(lambda a: m.g[:, 1, P * a:P * a + P], lambda a: m.h_fs[:, k, a // 2, a % 2], 4, m.s_h_tr)
            pe.wait_ge(m.s_h_q, 5 * n + 5)
            if cur:
                pe.wait_ge(m.s_h_ex, 8 * cur[0] + 8)
            spans(k, 0)
        if prev:
            pe.wait_ge(m.s_h_red, prev[0] + 1)
            pe.wait_ge(m.s_h_off, prev[0] + 1)
            for blk in range(RB):
                for s in range(RB):
                    ins = pe.matmul(m.t[:, 0, P * blk:P * blk + P], m.h_at[:, 2 * s + blk, :], m.pc[:, s, bass.ds(3072 + HD * prev[0], HD)],
                                    start=s == 0, stop=s == 1)
            ins.then_inc(m.s_h_o, 1)
        if cur:
            t, kc, _ = cur
            pe.wait_ge(m.s_h_mul, 2 * t + 3)
            if nxt:
                pe.wait_ge(m.s_h_qc, n + 1)
            if prev:
                pe.wait_ge(m.s_h_oc, prev[0] + 1)
            pe.matmul(m.g[:, 0, T:T + P], m.h_kq[:, 0, 0, 0, 0:P], m.h_kq[:, 0, 1, 0, P:T], start=True, stop=True)
            pe.matmul(m.g[:, 0, T + P:2 * T], m.h_kq[:, 0, 0, 0, P:T], m.h_kq[:, 0, 1, 0, 0:P], start=True, stop=True)
            block_products(0, range(1, 4))
        if nxt:
            pe.wait_ge(m.s_h_ex, 8 * n + 4)
            spans(k, 1)
        if cur:
            pe.wait_ge(m.s_h_mul, 2 * t + 4)
            pe.wait_ge(m.s_h_msk, t + 1)
            block_products(1, range(4))
            if nxt:
                pe.wait_ge(m.s_h_kc, n + 1)
            for blk in range(RB):
                b = slice(P * blk, P * blk + P)
                ins = pe.matmul(m.g[:, 1, b], m.h_ks[:, kc, b], m.h_qt[:, kc, b], start=True, stop=True)
            ins.then_inc(m.s_h_am, 1)

    heads_three_deep(lane, {}, h_turn, HH, 2)
    pe.wait_ge(m.s_y_ready, lane.n["y"] + 1)
    columns(m.pc, 4, 1)
    columns_split()
    gemm("c_out")
    mlp = PLAN["mlp"]
    first = arriving(m.mix, 4, 1)
    t0 = lane.n["T"] + 8

    def hidden_columns(q, k):
        pe.wait_ge(m.s_g_free[k % 2], mlp.s0 // 2 + 4 * q + k // 2 + 2)
        for half in range(2):
            b = (t0 + half) % 2
            pe.wait_ge(m.s_t_free[b], (t0 + half) // 2 + 4 * q + k + 1)
            blocks(b, lambda kt, rb: m.ur[:, k % 2, rb, T * half + P * kt:T * half + P * kt + P])

    def hidden_quarter(q, first=None):
        for k in range(8):
            xs = (m.xh, m.xl) if k < 4 else (m.uh, m.ul)
            if first and k == 0:
                first(mlp)
            elif k == 4:
                pe.wait_ge(m.s_g_free[0], mlp.s0 // 2 + 4 * q + 3)
                for j in range(4):
                    if j == 2:
                        hidden_columns(q, 3)
                    for half in range(2):
                        pe.wait_ge(m.s_t_free[(t0 + half) % 2], (t0 + half) // 2 + 4 * q + j + 2)
                    quarter(mlp, mlp.v0 + 8 * q + 4, mlp.g0 + 8 * q + 4, j, 0, 4 * j, j == 0, j == 3, m.uh, m.ul)
            else:
                unit(mlp, mlp.v0 + 8 * q + k, mlp.g0 + 8 * q + k, mlp.s0 // 2 + 4 * q + k // 2, k % 2, *xs)
            if 1 <= k <= 3:
                hidden_columns(q, k - 1)

    hidden_quarter(0, first)
    lane.loop(3, {}, hidden_quarter, 1)


def shape_constants():
    import numpy as np

    i = np.arange(P)
    s, t = i[:, None], i[None, :]
    const = np.concatenate([np.eye(P), np.ones((P, P)), np.where(t <= s, 0.0, NEG), s < t, s > t], axis=1)

    def inverse(base, half):
        return 1.0 / np.float32(base) ** (np.arange(half, dtype=np.float32) / np.float32(half))

    rates = np.tile(np.concatenate([inverse(500000.0, ROT_A), inverse(500000.0, ROT_I), inverse(10000.0, ROT_M)]), (P, 1))
    tau, spans = s, np.zeros((P, 2, 9, P))

    def span(mid, right):
        fwd = np.where(right, (mid <= tau) & (tau <= t), (t < tau) & (tau < mid))
        bwd = np.where(right, (mid <= tau) & (tau < t), (t <= tau) & (tau < mid))
        return fwd, bwd

    def level(l):
        half = P >> l
        return span(t // (2 * half) * (2 * half) + half, t % (2 * half) >= half)

    order = [span(P, np.zeros((1, P), bool))] + [level(l) for l in range(1, 4)]
    order += [span(0, np.ones((1, P), bool))] + [level(l) for l in range(4, LEVELS)]
    for n, pair in enumerate(order):
        for dr in range(2):
            spans[:, dr, n] = pair[dr]
    masks = [(s // (P >> l) // 2 == t // (P >> l) // 2) & (s // (P >> l) != t // (P >> l)) for l in range(1, LEVELS)]
    masks = np.stack(masks + [s == t], axis=1)
    out = {"consts": const, "rates": rates, "spans": spans.reshape(P, -1), "level_masks": masks.reshape(P, -1)}
    return {k: np.ascontiguousarray(v, dtype=np.float32) for k, v in out.items()}


def program(nc, arrays):
    import numpy as np

    a = {}
    for name, x in arrays.items():
        a[name] = nc.dram_tensor(f"in_{name}", x.shape, mybir.dt.from_np(np.dtype(x.dtype)), kind="ExternalInput").ap()
    out = nc.dram_tensor("out", (1, T, D), F32, kind="ExternalOutput").ap()
    d = Names()
    d.x = a["x"][0]
    d.p = a["p"][:, 0]
    d.positions = a["positions"]
    d.positions_2 = a["positions_2"]
    d.w_in_a = a["w_in_a"][0]
    d.w_o_a = a["w_o_a"][0]
    d.w_kv_b = a["w_kv_b"]
    d.w_in_b = a["w_in_b"][0]
    d.w_o_b = a["w_o_b"][0]
    d.ln_g = a["ln_g"]
    d.ln_b = a["ln_b"]
    d.w_ple = a["w_ple"]
    d.w_g0 = a["w_ple_gate"][0]
    d.w_g1 = a["w_ple_gate"][1]
    d.c = a["c_2"]
    d.w_mod = a["w_mod_2"][0]
    d.b_mod = a["b_mod_2"][0]
    d.pre_mix_g = a["pre_mix_g_2"][0]
    d.post_mix_g = a["post_mix_g_2"][0]
    d.pre_mlp_g = a["pre_mlp_g_2"][0]
    d.post_mlp_g = a["post_mlp_g_2"][0]
    d.w_in_c = a["w_in_2"][0]
    d.q_norm_g = a["q_norm_g_2"][0]
    d.kv_norm_g = a["kv_norm_g_2"][0]
    d.w_uq = a["w_uq_2"][0]
    d.w_ukv = a["w_ukv_2"][0]
    d.hgrn_g = a["hgrn_norm_g_2"][0]
    d.lb_f = a["hgrn_lb_logits_fwd_2"]
    d.lb_b = a["hgrn_lb_logits_bwd_2"]
    d.w_out = a["w_out_2"][0]
    d.w_up = a["w_up_2"][0]
    d.w_down = a["w_down_2"][0]
    d.consts = a["consts"]
    d.rates = a["rates"]
    d.spans = a["spans"]
    d.level_masks = a["level_masks"]
    build(nc, d, out[0])


def kernel(**inputs):
    import concourse.bacc as bacc
    import numpy as np
    from concourse.bass_utils import run_bass_kernel_spmd

    arrays = {k: np.ascontiguousarray(v) for k, v in inputs.items()}
    arrays.update(shape_constants())
    nc = bacc.Bacc("TRN2", target_bir_lowering=False, num_devices=1)
    program(nc, arrays)
    r = run_bass_kernel_spmd(nc, [{f"in_{k}": v for k, v in arrays.items()}], core_ids=[0])
    return r.results[0]["out"]
```

```python
from collections import defaultdict, namedtuple
from contextlib import ExitStack

import concourse.bass as bass
from concourse import mybir

F32 = mybir.dt.float32
F32R = mybir.dt.float32r
I32 = mybir.dt.int32
ACT = mybir.ActivationFunctionType
ALU = mybir.AluOpType
AXX = mybir.AxisListType.X

P = 128
RB = 2
T = RB * P
D = 2048
KT = D // P
HD = 128
NH = 16
NKV = 4
GROUP = NH // NKV
N_SEL = T // 4
IDX_H, IDX_D = 16, 64
ROT_A, ROT_I, ROT_M = 16, 8, 32
NROT = ROT_A + ROT_I + ROT_M
ALPHA = 4.0 ** 0.25
LN_EPS, RMS_EPS = 1e-5, 1e-6
NEG = -1e30
TAKEN = -3e38
MH, NOPE, ROPE, VD = 8, 128, 64, 128
QRANK, KVRANK = 512, 256
HH = 8
LEVELS = 8
WORDS = 18432
TWO_PI_HI, TWO_PI_MID, TWO_PI_LO = 6.28125, 1.9350051879882812e-03, 3.0199159819545e-07
ROUND = 12582912.0

KEYS_AT, DOTS_AT = 3, 6
IDX_PAIRS, PAIRS = IDX_H // 2, NH // 2
BEST_AT = DOTS_AT + IDX_PAIRS
ROUNDS = N_SEL // 8

C_IDENT, C_ONES, C_TRI, C_LT, C_GT, C_ROT = 0, 128, 256, 384, 512, 640
NCONST = C_ROT

STAGES = [
    ("a_idx", 4, True, 4, 276), ("a_qkv", 6, True, 4, 512), ("a_gate", 4, True, 4, 512),
    ("a_out", 4, True, 4, 512), ("ple0", 4, False, 4, 512),
    ("b_kvq", 6, True, 4, 512), ("b_gate", 4, True, 4, 512), ("b_out", 4, True, 4, 512), ("ple1", 4, False, 4, 512),
    ("c_hq", 2, True, 4, 512), ("c_f", 4, True, 4, 512), ("c_hi", 2, True, 4, 512), ("c_hg", 2, True, 4, 512),
    ("c_mla", 2, True, 4, 416), ("uq", 1, False, 4, 384), ("ukv", 1, False, 2, 512),
    ("c_out", 4, True, 4, 512), ("mlp", 32, False, 4, 512),
]


Stage = namedtuple("Stage", "name units mods kq width v0 g0 s0 m0 next per")


class Names:
    pass


def plan():
    out, v, g, s, m = {}, 0, 0, 0, 0
    for n, (name, units, mods, kq, width) in enumerate(STAGES):
        nxt = STAGES[n + 1][0] if n + 1 < len(STAGES) else None
        out[name] = Stage(name=name, units=units, mods=mods, kq=kq, width=width, v0=v, g0=g, s0=s, m0=m,
                                    next=nxt, per=3 if mods else 2)
        v += units + (units // 2 if mods else 0)
        m += units // 2 if mods else 0
        g += units
        s += 4 if units == 1 else units
    return out


PLAN = plan()


def v_of(st, i, k):
    return st.v0 + st.per * i + (0, 1, st.per)[k]


def v_mod(st, i):
    return st.v0 + st.per * i + 2


class Lane:

    def __init__(self, eng, step):
        self.eng, self.step = eng, step
        self.base, self.n = {}, defaultdict(int)

    def at(self, key="step"):
        return self.base.get(key, 0) + self.n[key]

    def did(self, ins):
        ins.then_inc(self.step, 1)
        self.n["step"] += 1

    def sync(self):
        self.eng.wait_ge(self.step, self.at())

    def link(self, ins):
        self.did(ins)
        self.sync()

    def loop(self, count, per, body, first=0):
        if count == 1:
            body(first)
            return
        if count <= 0:
            return
        start = {k: self.at(k) for k in set(per) | set(self.n)}
        with self.eng.Fori(0, count) as i:
            self.base = {k: start[k] + i * per[k] if per.get(k) else start[k] for k in start}
            self.n = defaultdict(int)
            body(i + first if first else i)
            got = {k: n for k, n in self.n.items() if n}
            assert got == {k: n for k, n in per.items() if n}, f"a turn counts {got}"
        self.base = {}
        self.n = defaultdict(int, {k: start[k] + count * per.get(k, 0) for k in start})


def heads_three_deep(lane, per, turn, count, unroll):
    def head(i, j):
        return unroll * i + j, j % unroll, i + j // unroll

    def three(i, j):
        return [head(i, j + 2 - back) for back in range(3)]

    turn(head(0, 0), None, None)
    turn(head(0, 1), head(0, 0), None)
    turns = (count - 2) // unroll

    def body(i):
        for j in range(unroll):
            turn(*three(i, j))

    lane.loop(turns, per, body)
    for j in range(unroll * turns, count):
        turn(*[head(0, j + 2 - back) if j + 2 - back < count else None for back in range(3)])


def build(nc, d, out):
    ctx = ExitStack()
    with ctx:
        m = memory(nc, ctx, d, out)
        block = ctx.enter_context(nc.Block())

        @block.sync
        def _(eng):
            sync_program(nc, eng, m, d, out)

        @block.gpsimd
        def _(eng):
            pool_program(nc, eng, m, d)

        @block.scalar
        def _(eng):
            scalar_program(nc, eng, m, d)

        @block.vector
        def _(eng):
            vector_program(nc, eng, m, d)

        @block.tensor
        def _(eng):
            tensor_program(nc, eng, m, d)


def memory(nc, ctx, d, out):
    m = Names()

    def sb(name, shape, dt=F32):
        return ctx.enter_context(nc.sbuf_tensor(name, shape, dt))

    def ps(name, shape):
        return ctx.enter_context(nc.psum_tensor(name, shape, F32))

    def sem(name):
        return ctx.enter_context(nc.semaphore(name))

    arena = nc.alloc_sbuf_tensor("arena", [P, WORDS], F32)
    base = nc.lookup_mloc(arena).addr

    def at(name, word, shape, dt=F32):
        n = 1
        for x in shape[1:]:
            n *= x
        assert word + n <= WORDS, (name, word + n)
        return nc.alloc_sbuf_tensor_at(name, shape, dt, offset=base + 4 * word)

    raw_words = 4 * 4 * 512
    raw_arena = nc.alloc_sbuf_tensor("raw", [P, 4, 4, 512], F32)
    raw_base = nc.lookup_mloc(raw_arena).addr
    m.raw = raw_arena

    def at_raw(name, word, shape, dt=F32):
        n = 1
        for x in shape[1:]:
            n *= x
        assert word + n <= raw_words, (name, word + n)
        return nc.alloc_sbuf_tensor_at(name, shape, dt, offset=raw_base + 4 * word)

    m.hi, m.lo = sb("w_high", [P, 4, 4, 512], F32R), sb("w_low", [P, 4, 4, 512], F32R)
    m.xh, m.xl = sb("x_high", [P, KT, T], F32R), sb("x_low", [P, KT, T], F32R)
    m.const = sb("const", [P, NCONST])
    m.ident, m.ones = m.const[:, C_IDENT:C_IDENT + P], m.const[:, C_ONES:C_ONES + P]
    m.tri, m.lt, m.gt = (m.const[:, c:c + P] for c in (C_TRI, C_LT, C_GT))
    m.acc = sb("mod_sum", [P, 512])
    m.ct = sb("cond_columns", [P, KT])
    m.cs = sb("cos_sin", [P, 2, RB, NROT])
    m.st = sb("stats", [P, RB, 4, 6])
    m.mv = sb("mean_var", [P, 2 * RB, 2])
    m.rstd = sb("rstd", [P, 2 * RB])
    m.msq = sb("mean_square", [P, 2 * RB])
    m.x_sq = sb("x_square_sums", [P, RB, 4])
    m.brow = sb("mod_bias", [1, 512])
    m.dummy = sb("credit_word", [P, 1])

    m.res = at("residual", 0, [P, RB, D])
    m.posi = at("positions_i", 4096, [P, 2 * RB], I32)
    m.posf = at("positions_f", 4104, [P, 2 * RB])
    m.ang = at("angles", 4112, [P, RB, NROT])
    m.turns = at("angle_turns", 4112 + 2 * NROT, [P, RB, NROT])
    m.crow = at("cond_rows", 4112 + 4 * NROT, [KT, P])
    m.rot = at("rotary_rates", 4112 + 4 * NROT + P, [P, NROT])
    m.pa = at("proj_a", 4096, [P, RB, 6224])
    m.a_ikt = at("a_index_keys_t", 0, [P, T])
    m.a_ikd = at("a_index_keys_twice", 256, [P, RB, 2, IDX_D])
    m.a_bias = at("a_bias", 1024, [P, 384])
    m.a_bias0 = at("a_causal_bias", 1408, [P, 384])
    m.a_score = at("a_index_score", 1792, [P, 384])
    m.a_top = at("a_top8", 2176, [P, 2, 8])
    m.a_rope = at("a_rope", 2192, [P, 2, 20 * 2 * ROT_A])
    m.a_iqs = at("a_index_q", 2192, [P, 2, RB, P])
    m.a_iqt = at("a_index_q_t", 2704, [P, 2, T])
    m.a_iws = at("a_index_w", 16544, [P, 2, RB, 2])
    m.a_rl = at("a_index_relu", 16552, [P, 2, 2, 384])
    m.a_kt = at("a_keys_t", 0, [P, NKV, T])
    m.a_z11 = at("a_scores_11", 1792, [P, NH * HD])
    m.a_qt = at("a_q_t", 16544, [P, 2, 2 * T])
    m.a_nm = at("a_neg_max", 17568, [P, NKV, RB, GROUP])
    m.a_sum = at("a_sum", 17600, [P, NKV, RB, GROUP])
    m.a_rs = at("a_inverse_sum", 17632, [P, NKV, RB, GROUP])
    m.row_g = at("row_g", 4096, [P, D])
    m.row_b = at("row_b", 6144, [P, D])
    m.ple_w = at("ple_w", 8192, [P, 2, D])
    m.ple_p = at("ple_p", 12288, [P, RB, 256])
    m.ple_pt = at("ple_p_t", 12800, [P, 2, T])
    m.ple_s = at("ple_gate", 13312, [P, 2, RB, 512])
    m.pb = at("proj_b", 4096, [P, RB, 5120])
    m.b_kt = at("b_keys_t", 14336, [P, NKV, T])
    m.b_z11 = at("b_scores_11", 15360, [P, NH * HD])
    m.b_qt = at("b_q_t", 17408, [P, 2, 2 * T])
    m.c_g1 = at("c_row_gain", 4096, [P, D])
    m.c_sc = at("c_row_scale", 6144, [P, D])
    m.c_sh = at("c_row_shift", 15360, [P, D])
    m.c_h = at("c_normed", 10240, [P, RB, D])
    m.pc = at("proj_c", 0, [P, RB, 5120])
    m.pm = at("proj_mla", 10240, [P, RB, 832])
    m.m_rg = at("m_norm_rows", 11904, [P, QRANK + KVRANK])
    m.m_rope = at("m_rope", 12672, [P, 2, 512])
    m.m_krd = m.acc[:, 0:RB * P].rearrange("p (r e) -> p r e", r=RB)
    m.mq = at("mla_q", 11264, [P, RB, 1536])
    m.mkv = at("mla_kv", 14336, [P, RB, 2048])
    m.m_rope2 = at_raw("m_rope2", 0, [P, 2, 512])
    m.m_qs = at_raw("m_q", 1024, [P, 2, RB, 256])
    m.m_qt = at_raw("m_q_t", 2560, [P, 2, 2, T])
    m.m_krt = at_raw("m_k_rope_t", 4096, [P, T])
    m.m_lg = at_raw("m_logits", 4352, [P, 2, RB, T])
    m.m_pt = at_raw("m_probs_t", 5376, [P, 2, RB, T])
    m.m_og = at_raw("m_out", 6400, [P, RB, P])
    m.m_nm = at_raw("m_neg_max", 6656, [P, 2, RB])
    m.m_sum = at_raw("m_sum", 6664, [P, 2, RB])
    m.m_rs = at_raw("m_inverse_sum", 6672, [P, 2, RB])
    def at_ring(ring):
        start = nc.lookup_mloc(ring).addr

        def place(name, word, shape):
            n = 1
            for x in shape[1:]:
                n *= x
            assert word + n <= raw_words, (name, word + n)
            return nc.alloc_sbuf_tensor_at(name, shape, F32, offset=start + 4 * word)

        return place

    at_hi, at_lo = at_ring(m.hi), at_ring(m.lo)
    m.a_lg = at_hi("a_logits", 0, [P, NKV, 3 * GROUP * HD])
    m.a_pt = at_lo("a_probs_t", 3072, [P, 2, 3, GROUP * HD])
    m.a_og = at_lo("a_out_gated", 6144, [P, 2, RB, GROUP * HD])
    m.b_e = at_hi("b_exp", 0, [P, NKV, 3, GROUP * HD])
    m.b_sp = at_lo("b_softplus", 0, [P, NKV, 3, GROUP * HD])
    m.b_og = at_lo("b_out_gated", 6144, [P, 2, RB, GROUP * HD])
    m.h_l0 = at("h_bound_logits", 14336, [P, 2, 2, 1024])
    m.h_t = at("h_one_minus", 12288, [P, RB, 1024])
    m.h_md = at_hi("h_spans", 0, [P, 2, 9, P])
    m.h_e = at_hi("h_decay", 2304, [P, 2, 2, 4, T])
    m.m_ktt = at_hi("m_keys_t", 2304, [P, MH, T])
    m.h_kt = at_hi("h_k_t", 6400, [P, 2, 2, T])
    m.h_ks = at_hi("h_k_sum", 7424, [P, 2, T])
    m.h_lfa = at_lo("h_log_f_all", 0, [P, RB, 2048])
    m.h_mask = at_lo("h_level_masks", 4096, [P, LEVELS, P])
    m.h_qt = at_lo("h_q_t", 5120, [P, 2, T])
    m.h_at = at_lo("h_weights_t", 5632, [P, 4, P])
    m.h_fs = at_lo("h_f", 6144, [P, 2, 2, RB, P])
    m.h_qs = at_lo("h_q", 7168, [P, 2, RB, P])
    m.h_ng = at_lo("h_norm_g", 7680, [P, P])
    m.h_sq = at_lo("h_squares", 7808, [P, RB, P])
    m.h_kq = at("h_keys_queries", 10240, [P, 2, 2, 4, T])
    m.h_tm = at("h_masked", 14336, [P, 2, LEVELS, P])
    m.h_lf = at("h_log_f", 16384, [P, 2, 2, RB, P])
    m.h_ms = at("h_mean_sq", 17408, [P, RB, HH])
    m.h_r = at("h_rstd", 17424, [P, RB, HH])
    m.mix = at("mix", 4096, [P, RB, D])
    m.x_ga = at("x_row_gate", 8192, [P, D])
    m.x_pg = at("x_row_post", 10240, [P, D])
    m.x_g1 = at("x_row_gain", 12288, [P, D])
    m.x_sc = at("x_row_scale", 14336, [P, D])
    m.x_sh = at("x_row_shift", 16384, [P, D])
    m.y = at("mlp_sum", 4096, [P, RB, D])
    m.uh = at("u_high", 8192, [P, KT, T], F32R)
    m.ul = at("u_low", 12288, [P, KT, T], F32R)
    m.ur = at("u_rows", 16384, [P, 2, RB, 512])
    m.z_gm = at_raw("z_row_gate", 0, [P, D])
    m.z_pg = at_raw("z_row_post", 2048, [P, D])

    m.g = ps("products", [P, 4, 512])
    m.t = ps("transposed", [P, 2, 512])
    m.u = ps("aside", [P, 2, 512])
    m.pairs = [m.u, m.t]

    m.mod_d = nc.dram_tensor("mod_row", (6 * D,), F32).ap()
    m.res_d = nc.dram_tensor("residual_kept", (T, D), F32).ap()

    m.s_landed = [sem(f"quarter_landed_{j}") for j in range(4)]
    m.s_raw_used = sem("raw_used")
    m.s_w_high = sem("w_high")
    m.s_w_used = sem("w_used")
    m.s_x_high_ready = sem("x_high_ready")
    m.s_y_ready = sem("y_ready")
    m.s_const_landed = sem("const_landed")
    m.s_x_landed = sem("x_landed")
    m.s_pos_landed = sem("pos_landed")
    m.s_rows_landed = sem("rows_landed")
    m.s_rows2_landed = sem("rows2_landed")
    m.s_gain_rows_landed = sem("gain_rows_landed")
    m.s_x_scale = sem("x_scale")
    m.s_x_gains = sem("x_gains")
    m.s_ple_landed = sem("ple_landed")
    m.s_res_stored = sem("res_stored")
    m.s_out_stored = sem("out_stored")
    m.s_mod_summed = sem("mod_summed")
    m.s_mod_row = sem("mod_row")
    m.s_brow_landed = sem("brow_landed")
    m.s_mod_stored = sem("mod_stored")
    m.s_pool_step = sem("pool_step")
    m.s_act_step = sem("act_step")
    m.s_dve_step = sem("dve_step")
    m.s_pe_step = sem("pe_step")
    m.s_angles_ready = sem("angles_ready")
    m.s_sin_ready = sem("sin_ready")
    m.s_var_ready = sem("var_ready")
    m.s_std_ready = sem("std_ready")
    m.s_ple_full = sem("ple_full")
    m.s_ple_free = sem("ple_free")
    m.s_x4_ready = sem("x4_ready")
    m.s_mlp_done = sem("mlp_done")
    m.s_res2_landed = sem("res2_landed")
    m.s_a_ready = sem("a_ready")
    m.s_a_k_t = sem("a_k_t")
    m.s_a_ktp = sem("a_ktp")
    m.s_a_k_copied = sem("a_k_copied")
    m.s_a_iq = sem("a_iq")
    m.s_a_iqt = sem("a_iqt")
    m.s_a_iqc = sem("a_iqc")
    m.s_a_dots = sem("a_dots")
    m.s_a_relu = sem("a_relu")
    m.s_a_idx_done = sem("a_idx_done")
    m.s_a_roped = sem("a_roped")
    m.s_a_qtp = sem("a_qtp")
    m.s_a_qtc = sem("a_qtc")
    m.s_a_z = sem("a_z")
    m.s_a_zc = sem("a_z_copied")
    m.s_a_nmax = sem("a_nmax")
    m.s_a_p = sem("a_p")
    m.s_a_ptp = sem("a_ptp")
    m.s_a_ptc = sem("a_ptc")
    m.s_a_o = sem("a_o")
    m.s_a_ogr = sem("a_ogr")
    m.s_a_ogt = sem("a_ogt")
    m.s_a_xh = sem("a_xh")
    m.s_a_done = sem("a_done")
    m.s_b_k_t = sem("b_k_t")
    m.s_b_k_copied = sem("b_k_copied")
    m.s_b_qtp = sem("b_qtp")
    m.s_b_qtc = sem("b_qtc")
    m.s_b_z = sem("b_z")
    m.s_b_zc = sem("b_z_copied")
    m.s_b_abs = sem("b_abs")
    m.s_b_l = sem("b_l")
    m.s_b_spr = sem("b_softplus_ready")
    m.s_b_sfx = sem("b_sfx")
    m.s_b_a1 = sem("b_a1")
    m.s_b_ex = sem("b_ex")
    m.s_b_w = sem("b_w")
    m.s_b_o = sem("b_o")
    m.s_b_ogr = sem("b_ogr")
    m.s_b_ogt = sem("b_ogt")
    m.s_b_xh = sem("b_xh")
    m.s_b_done = sem("b_done")
    m.s_m_ready = sem("m_ready")
    m.s_m_krt_t = sem("m_krt_t")
    m.s_m_krt_c = sem("m_krt_c")
    m.s_m_q = sem("m_q")
    m.s_m_qtp = sem("m_qtp")
    m.s_m_qtc = sem("m_qtc")
    m.s_m_s = sem("m_s")
    m.s_m_nmax = sem("m_nmax")
    m.s_m_p = sem("m_p")
    m.s_m_ptp = sem("m_ptp")
    m.s_m_ptc = sem("m_ptc")
    m.s_m_o = sem("m_o")
    m.s_m_ogr = sem("m_ogr")
    m.s_m_ogt = sem("m_ogt")
    m.s_m_xh = sem("m_xh")
    m.s_m_done = sem("m_done")
    m.s_m_qkv = sem("m_qkv")
    m.s_m_ktp = sem("m_ktp")
    m.s_m_ktc = sem("m_ktc")
    m.s_h_lb = sem("h_lb")
    m.s_h_lbs = sem("h_lbs")
    m.s_h_fr = sem("h_fr")
    m.s_h_rows = sem("h_rows")
    m.s_h_consts = sem("h_consts")
    m.s_h_q = sem("h_q")
    m.s_h_logf = sem("h_logf")
    m.s_h_tr = sem("h_tr")
    m.s_h_qc = sem("h_qc")
    m.s_h_kc = sem("h_kc")
    m.s_h_k1 = sem("h_keys")
    m.s_h_ms = sem("h_squares_summed")
    m.s_x_sq = sem("x_squares")
    m.s_x_added = sem("x_added")
    m.s_h_d = sem("h_d")
    m.s_h_ex = sem("h_ex")
    m.s_h_mul = sem("h_mul")
    m.s_h_am = sem("h_am")
    m.s_h_dg = sem("h_dg")
    m.s_h_gain = sem("h_gain")
    m.s_h_msk = sem("h_msk")
    m.s_h_off = sem("h_off")
    m.s_h_red = sem("h_red")
    m.s_h_o = sem("h_o")
    m.s_h_oc = sem("h_oc")
    m.s_h_ms1 = sem("h_ms1")
    m.s_h_std = sem("h_std")
    m.s_g_free = [sem(f"product_free_{b}") for b in range(2)]
    m.s_t_full = [sem(f"transposed_full_{b}") for b in range(2)]
    m.s_t_free = [sem(f"transposed_free_{b}") for b in range(2)]
    return m


def gemm_turns(lane, st, per, turn, tail, straight=False):
    n = st.units // 2
    if straight:
        for i in range(n - 1):
            turn(i)
    else:
        lane.loop(n - 1, per, turn)
    tail(n - 1)


def rows(ap, n):
    return ap.rearrange("(o n) -> o n", o=1).broadcast_to((P, n))


def scores(m, c):
    w = GROUP * HD
    return m.pb[:, :, 1024 + w * c:1024 + w * c + w], m.b_z11[:, w * c:w * c + w]


def logits(m, c):
    w = GROUP * HD
    return (m.a_lg[:, c, 0:w].rearrange("p (h t) -> p h t", h=GROUP),
            m.a_lg[:, c, w:3 * w].rearrange("p (h b t) -> p h b t", h=GROUP, b=RB))


def sync_program(nc, sp, m, d, out):
    lane = Lane(sp, m.s_pe_step)

    def load(st, v, src):
        for j in range(4):
            sp.wait_ge(m.s_raw_used, 4 * v + j + 1)
            sp.dma_start(m.raw[:, j, 0:st.kq, 0:st.width], src(j)).then_inc(m.s_landed[j], 16)

    def tiles(w, j, col, width, row=0):
        return w.rearrange("(k p) n -> p k n", p=P)[:, row + 4 * j:row + 4 * j + 4, bass.ds(col, width)]

    def source(name, u):
        col = {"a_qkv": 0, "a_gate": 3072, "a_idx": 5120, "b_gate": 2048, "c_hq": 832, "c_f": 1856,
               "c_hi": 3904, "c_hg": 4928}.get(name, 0)
        width = PLAN[name].width
        if name == "b_kvq":
            w, c = (d.w_kv_b, 512 * u) if isinstance(u, int) and u < 2 else (d.w_in_b, 512 * (u - 2))
        elif name == "uq":
            return lambda j: d.w_uq.rearrange("(k p) n -> p k n", p=P)[:, :, 384 * j:384 * j + 384]
        elif name == "ukv":
            return lambda j: d.w_ukv.rearrange("(k p) n -> p k n", p=P)[:, :, 512 * j:512 * j + 512]
        else:
            w = {"a": d.w_in_a, "b": d.w_in_b, "c": d.w_in_c}.get(name[0])
            w = {"a_out": d.w_o_a, "b_out": d.w_o_b, "c_out": d.w_out, "ple0": d.w_g0, "ple1": d.w_g1}.get(name, w)
            c = col + width * u
        c = sp.snap(c) if not isinstance(c, int) else c
        return lambda j: tiles(w, j, c, width)

    def load_unit(name, i, k):
        st = PLAN[name]
        load(st, v_of(st, i, k), source(name, 2 * i + k))

    def load_mod(name, i):
        st = PLAN[name]
        c = 512 * (st.m0 + i)
        c = sp.snap(c) if not isinstance(c, int) else c
        load(PLAN["a_qkv"], v_mod(st, i), lambda j: tiles(d.w_mod, j, c, 512))

    def gemm(name, before_tail=None, next_too=True):
        st = PLAN[name]

        def turn(i):
            load_unit(name, i, 1)
            if st.mods:
                load_mod(name, i)
            load_unit(name, i, 2)

        def tail(i):
            if before_tail:
                before_tail()
            load_unit(name, i, 1)
            if st.mods:
                load_mod(name, i)
            if next_too:
                load_unit(st.next, 0, 0)

        n = st.units // 2
        if name == "b_kvq":
            for i in range(n - 1):
                turn(i)
        else:
            lane.loop(n - 1, {}, turn)
        tail(n - 1)

    def bring(tile, src, s):
        sp.dma_start(tile, src).then_inc(s, 16)

    tokens = "(r p) n -> p r n"
    bring(m.const[:], d.consts, m.s_const_landed)
    bring(m.crow[:], d.c.rearrange("o (k p) -> (o k) p", p=P), m.s_const_landed)
    bring(m.res[:], d.x.rearrange(tokens, p=P), m.s_x_landed)
    with nc.allow_non_contiguous_dma(reason="512 positions"):
        bring(m.posi[:, 0:RB], d.positions.rearrange("o (r p) -> p (o r)", p=P), m.s_pos_landed)
        bring(m.posi[:, RB:2 * RB], d.positions_2.rearrange("o (r p) -> p (o r)", p=P), m.s_pos_landed)
    bring(m.rot[:], d.rates, m.s_pos_landed)
    load_unit("a_idx", 0, 0)
    for name in ("a_idx", "a_qkv", "a_gate"):
        gemm(name)

    def norm_rows(layer):
        def go():
            if layer:
                sp.wait_ge(m.s_b_done, NKV)
            bring(m.row_g[:], rows(d.ln_g[layer], D), m.s_rows_landed)
            bring(m.row_b[:], rows(d.ln_b[layer], D), m.s_rows_landed)
            bring(m.ple_w[:], d.w_ple[layer].rearrange("(k p) n -> p k n", p=P), m.s_ple_landed)
            bring(m.ple_p[:], d.p[layer].rearrange(tokens, p=P), m.s_ple_landed)
        return go

    sp.wait_ge(m.s_a_done, NKV)
    bring(m.res[:], d.x.rearrange(tokens, p=P), m.s_x_landed)
    gemm("a_out", norm_rows(0))
    gemm("ple0")
    gemm("b_kvq")
    gemm("b_gate")
    gemm("b_out", norm_rows(1))

    def c_rows():
        sp.wait_ge(m.s_y_ready, 20)
        bring(m.c_g1[:], rows(d.pre_mix_g, D), m.s_rows2_landed)
        sp.wait_ge(m.s_mod_stored, 16 * 9)
        bring(m.c_sh[:], rows(m.mod_d[0:D], D), m.s_rows2_landed)
        bring(m.c_sc[:], rows(m.mod_d[D:2 * D], D), m.s_rows2_landed)

    gemm("ple1", c_rows)
    sp.wait_ge(m.s_x4_ready, 4)
    bring(m.res_d.rearrange(tokens, p=P), m.res[:], m.s_res_stored)
    gemm("c_hq")
    gemm("c_f")
    sp.wait_ge(m.s_w_used, 4 * PLAN["c_f"].g0 + 4)
    for dr, lb in enumerate((d.lb_f, d.lb_b)):
        for slot in range(2):
            bring(m.h_l0[:, dr, slot, :], rows(lb[slot], 1024), m.s_h_rows)
    gemm("c_hi")
    gemm("c_hg")
    sp.wait_ge(m.s_h_fr, 2)
    bring(m.m_rg[:, 0:QRANK], rows(d.q_norm_g, QRANK), m.s_rows2_landed)
    bring(m.m_rg[:, QRANK:], rows(d.kv_norm_g, KVRANK), m.s_rows2_landed)
    gemm("c_mla")
    load_unit("ukv", 0, 0)
    sp.wait_ge(m.s_w_used, 4 * PLAN["ukv"].g0 + 8)
    bring(m.h_md[:], d.spans.rearrange("p (a b c) -> p a b c", a=2, b=9), m.s_h_consts)
    bring(m.h_mask[:], d.level_masks.rearrange("p (a b) -> p a b", a=LEVELS), m.s_h_consts)
    bring(m.h_ng[:], rows(d.hgrn_g, P), m.s_h_consts)
    sp.wait_ge(m.s_m_done, MH + 2)
    load_unit("c_out", 0, 0)

    def x_rows():
        for b in range(2):
            sp.wait_ge(m.s_t_free[b], 26)
        sp.wait_ge(m.s_mod_stored, 16 * 21)
        bring(m.x_ga[:], rows(m.mod_d[2 * D:3 * D], D), m.s_gain_rows_landed)
        bring(m.x_pg[:], rows(d.post_mix_g, D), m.s_gain_rows_landed)
        bring(m.x_g1[:], rows(d.pre_mlp_g, D), m.s_gain_rows_landed)
        bring(m.x_sc[:], rows(m.mod_d[4 * D:5 * D], D), m.s_gain_rows_landed)
        sp.wait_ge(m.s_res_stored, 16)
        bring(m.res[:], m.res_d.rearrange(tokens, p=P), m.s_res2_landed)
        bring(m.x_sh[:], rows(m.mod_d[3 * D:4 * D], D), m.s_rows2_landed)

    gemm("c_out", next_too=False)
    x_rows()
    mlp = PLAN["mlp"]

    def mlp_load(q, k):
        if k < 4:
            c = 2048 * q + 512 * k
            c = sp.snap(c) if not isinstance(c, int) else c
            load(mlp, mlp.v0 + 8 * q + k, lambda j: tiles(d.w_up, j, c, 512))
        else:
            if isinstance(q, int):
                load(mlp, mlp.v0 + 8 * q + k,
                     lambda j: tiles(d.w_down, j, 512 * (k - 4), 512, row=KT * q))
            else:
                off = sp.snap(2048 * q)
                w = d.w_down[bass.ds(off, 2048), :]
                load(mlp, mlp.v0 + 8 * q + k, lambda j: tiles(w, j, 512 * (k - 4), 512))

    lane.loop(4, {}, lambda q: [mlp_load(q, k) for k in range(8)])
    sp.wait_ge(m.s_raw_used, 4 * (mlp.v0 + 32) + 1)
    sp.wait_ge(m.s_mod_stored, 16 * 25)
    bring(m.z_gm[:], rows(m.mod_d[5 * D:6 * D], D), m.s_rows2_landed)
    sp.wait_ge(m.s_raw_used, 4 * (mlp.v0 + 32) + 2)
    bring(m.z_pg[:], rows(d.post_mlp_g, D), m.s_rows2_landed)
    for c in range(4):
        sp.wait_ge(m.s_mlp_done, RB * c + RB)
        bring(out.rearrange(tokens, p=P)[:, :, 512 * c:512 * c + 512], m.res[:, :, 512 * c:512 * c + 512], m.s_out_stored)
    sp.wait_ge(m.s_out_stored, 64)


def pool_program(nc, pool, m, d):
    lane = Lane(pool, m.s_pool_step)
    credits = [(m.s_raw_used, 4), (m.s_w_used, 4), (m.s_mod_summed, 1), (m.s_mod_stored, 16), (m.s_h_d, 4), (m.s_h_mul, 2),
               (m.s_m_done, 2), (m.s_m_qtp, 2), (m.s_a_idx_done, 2), (m.s_ple_free, 1)]
    credits += [(s, 1) for s in m.s_g_free + m.s_t_free]
    for n, (s, k) in enumerate(credits):
        if n:
            pool.wait_ge(credits[n - 1][0], 1)
        nc.gpsimd.memset(m.dummy[:], 0.0).then_inc(s, k)

    pool.wait_ge(m.s_a_ready, 1)
    nc.gpsimd.tensor_copy(m.a_ikd[:, :, 0, :], m.pa[:, :, 6144:6208]).then_inc(m.s_a_k_t, 1)
    nc.gpsimd.tensor_copy(m.a_ikd[:, :, 1, :], m.pa[:, :, 6144:6208]).then_inc(m.s_a_k_t, 1)

    def index_pair(i):
        for k in range(2):
            t = 2 * i + k
            pool.wait_ge(m.s_a_idx_done, t + 1)
            nc.gpsimd.tensor_copy(m.a_iws[:, k], m.pa[:, :, bass.ds(6208 + 2 * t, 2)]).then_inc(m.s_a_iq, 1)
            nc.gpsimd.tensor_copy(m.a_iqs[:, k], m.pa[:, :, bass.ds(5120 + P * t, P)]).then_inc(m.s_a_iq, 1)

    lane.loop(4, {}, index_pair)

    pool.wait_ge(m.s_m_ready, 1)
    nc.gpsimd.memset(m.m_qs[:], 0.0).then_inc(m.s_m_qkv, 1)
    pool.wait_ge(m.s_m_qkv, 1)

    def m_heads(i):
        for k in range(2):
            t = 2 * i + k
            pool.wait_ge(m.s_m_qtp, t + 1)
            nc.gpsimd.tensor_copy(m.m_qs[:, k, :, 0:NOPE + ROPE], m.mq[:, :, bass.ds((NOPE + ROPE) * t, NOPE + ROPE)]).then_inc(m.s_m_q, 1)

    lane.loop(MH // 2, {}, m_heads)
    pool.wait_ge(m.s_h_logf, RB)
    pool.wait_ge(m.s_w_used, 4 * PLAN["ukv"].g0 + 8)

    def h_heads(i):
        for k in range(2):
            t = 2 * i + k
            pool.wait_ge(m.s_h_d, 2 * t + 2)
            nc.gpsimd.tensor_copy(m.h_qs[:, k], m.pc[:, :, bass.ds(HD * t, HD)]).then_inc(m.s_h_q, 1)
            for dr in range(2):
                nc.gpsimd.tensor_copy(m.h_fs[:, k, dr], m.pc[:, :, bass.ds(1024 * (dr + 1) + HD * t, HD)]).then_inc(m.s_h_q, 1)
            pool.wait_ge(m.s_m_done, MH + 2)
            for dr in range(2):
                nc.gpsimd.tensor_copy(m.h_lf[:, k, dr], m.h_lfa[:, :, bass.ds(1024 * dr + HD * t, HD)]).then_inc(m.s_h_q, 1)

    lane.loop(HH // 2, {}, h_heads)
    pool.wait_ge(m.s_h_consts, 48)
    for rb in range(RB):
        gate = m.pc[:, rb, 4096:5120].rearrange("p (h e) -> p h e", h=HH)
        nc.gpsimd.tensor_tensor(gate, gate, m.h_ng[:].unsqueeze(1).broadcast_to((P, HH, HD)), ALU.mult).then_inc(m.s_h_gain, 1)
    pool.wait_ge(m.s_gain_rows_landed, 64)
    nc.gpsimd.tensor_tensor(m.x_pg[:], m.x_pg[:], m.x_ga[:], ALU.mult).then_inc(m.s_x_gains, 1)
    pool.wait_ge(m.s_x_scale, 1)
    nc.gpsimd.tensor_tensor(m.x_g1[:], m.x_g1[:], m.x_sc[:], ALU.mult).then_inc(m.s_x_gains, 1)


def scalar_program(nc, act, m, d):
    lane = Lane(act, m.s_act_step)

    def high(st, v, g, js=range(4), aside=None):
        for j in js:
            act.wait_ge(m.s_landed[j], 16 * v + 16)
            act.wait_ge(m.s_w_used, 4 * g + j + 1)
            act.activation(m.hi[:, j, 0:st.kq, 0:st.width], m.raw[:, j, 0:st.kq, 0:st.width], ACT.Copy).then_inc(m.s_w_high, 1)
            if aside:
                aside(j)

    def high_unit(name, i, k, js=range(4), aside=None):
        st = PLAN[name]
        high(st, v_of(st, i, k), st.g0 + 2 * i + k, js, aside)

    def product(st, i, k):
        act.wait_ge(m.s_w_used, 4 * (st.g0 + 2 * i + k) + 8)
        return m.g[:, 2 * k:2 * k + 2, 0:st.width]

    def mod_io(st, i):
        n = st.m0 + i
        act.wait_ge(m.s_mod_row, n + 1)
        act.dma_start(m.mod_d[bass.ds(512 * n, 512)].rearrange("(o n) -> o n", o=1), m.acc[0:1, :]).then_inc(m.s_mod_stored, 16)
        if not (isinstance(n, int) and n == 23):
            act.dma_start(m.brow[:], d.b_mod[bass.ds(512 * n + 512, 512)].rearrange("(o n) -> o n", o=1)).then_inc(m.s_brow_landed, 16)

    def gemm(name, take, next_too=True, per={}, late=0, aside=None):
        st = PLAN[name]

        def by(u):
            return aside and (lambda j: aside(4 * u + j))

        def turn(i):
            high_unit(name, i, 1, aside=by(2 * i))
            take(st, i, 0)
            high_unit(name, i, 2, aside=by(2 * i + 1))
            take(st, i, 1)
            if st.mods:
                mod_io(st, i)

        def tail(i):
            high_unit(name, i, 1, aside=by(2 * i))
            take(st, i, 0)
            if next_too:
                high_unit(st.next, 0, 0, range(min(3, 4 - late)), by(2 * i + 1))
            if aside and late:
                for j in range(min(3, 4 - late), 4):
                    aside(4 * (2 * i + 1) + j)
            take(st, i, 1)
            if next_too and not late:
                high_unit(st.next, 0, 0, [3], by(2 * i + 1))
            if st.mods:
                mod_io(st, i)

        gemm_turns(lane, st, per, turn, tail, aside)

    def keep(tile, col, func=ACT.Copy):
        def take(st, i, k):
            src = product(st, i, k)
            act.activation(tile[:, :, bass.ds(col + st.width * (2 * i + k), st.width)], src, func).then_inc(m.s_g_free[k], 1)
        return take

    def nothing(st, i, k):
        pass

    def high_columns(k0, uses):
        for q in range(uses):
            n = lane.n["T"]
            act.wait_ge(m.s_t_full[n % 2], n // 2 + 1)
            act.activation(m.xh[:, k0 + 2 * q:k0 + 2 * q + 2, :], m.t[:, n % 2, :].rearrange("p (k t) -> p k t", k=2), ACT.Copy)\
               .then_inc(m.s_x_high_ready, 1)
            lane.n["T"] += 1

    def std(n, columns=RB):
        act.wait_ge(m.s_var_ready, n)
        act.activation(m.rstd[:, 0:columns], m.msq[:, 0:columns], ACT.Sqrt).then_inc(m.s_std_ready, 1)

    act.dma_start(m.brow[:], d.b_mod[0:512].rearrange("(o n) -> o n", o=1)).then_inc(m.s_brow_landed, 16)
    act.wait_ge(m.s_t_full[0], 1)
    act.activation(m.ct[:], m.t[:, 0, 0:KT], ACT.Silu).then_inc(m.s_t_free[0], 1)
    lane.n["T"] += 1
    for c in range(4):
        high_columns(4 * c, 2)
        high_unit("a_idx", 0, 0, [c])
    act.wait_ge(m.s_angles_ready, 1)
    act.activation(m.cs[:, 0], m.turns[:], ACT.Sin).then_inc(m.s_sin_ready, 1)
    act.activation(m.cs[:, 1], m.ang[:], ACT.Sin).then_inc(m.s_sin_ready, 1)
    act.wait_ge(m.s_sin_ready, 2)
    gemm("a_idx", keep(m.pa, 5120))

    def index_aside(b):
        if b == KEYS_AT:
            act.wait_ge(m.s_a_ktp, 1)
            act.activation(m.a_ikt[:], m.u[:, 1, 0:T], ACT.Copy).then_inc(m.s_a_k_copied, 1)
        t = b - DOTS_AT
        if 0 <= t < IDX_PAIRS:
            for hh, bank in enumerate((m.t[:, 1, 0:384], m.u[:, 1, 0:384])):
                act.wait_ge(m.s_a_dots, t + 1)
                act.activation(m.a_rl[:, t % 2, hh], bank, ACT.Relu, scale=IDX_D ** -0.5 * IDX_H ** -0.5).then_inc(m.s_a_relu, 1)
        t = b - DOTS_AT + 1
        if 0 <= t < IDX_PAIRS:
            act.wait_ge(m.s_a_iqt, t + 1)
            act.activation(m.a_iqt[:, t % 2], m.t[:, 0, 0:T], ACT.Copy).then_inc(m.s_a_iqc, 1)

    gemm("a_qkv", keep(m.pa, 0), aside=index_aside)

    def a_scores_aside(b):
        if b == KEYS_AT:
            act.wait_ge(m.s_a_ktp, 2)
            act.activation(m.a_kt[:].rearrange("p (a k) t -> p a (k t)", a=2), m.t[:], ACT.Copy).then_inc(m.s_a_k_copied, 1)
        t = b - DOTS_AT
        if 0 <= t < PAIRS:
            act.wait_ge(m.s_a_z, t + 1)
            for hh, bank in enumerate((m.t[:, 1], m.u[:, 1])):
                h = HD * (2 * t + hh)
                act.activation(m.pa[:, :, h:h + HD], bank[:, 0:T].rearrange("p (r e) -> p r e", r=RB), ACT.Copy, scale=HD ** -0.5)\
                   .then_inc(m.s_a_zc, 1)
                act.activation(m.a_z11[:, h:h + HD], bank[:, T:384], ACT.Copy, scale=HD ** -0.5).then_inc(m.s_a_zc, 1)
        t = b - DOTS_AT + 1
        if 0 <= t < PAIRS:
            act.wait_ge(m.s_a_qtp, t + 1)
            act.activation(m.a_qt[:, t % 2], m.t[:, 0, :], ACT.Copy).then_inc(m.s_a_qtc, 1)

    gemm("a_gate", keep(m.pa, 3072, ACT.Silu), late=4, aside=a_scores_aside)

    def head_high(bank, h):
        return act.activation(m.xh[:, bass.ds(h, 1), :].rearrange("p k t -> p (k t)"), m.t[:, bank, T:2 * T], ACT.Copy)

    def group_high(c, transposed, done):
        act.wait_ge(transposed, c + 1)
        act.activation(m.xh[:, GROUP * c:GROUP * c + GROUP, :].rearrange("p (a k) t -> p a (k t)", a=2), m.pairs[c % 2][:], ACT.Copy).then_inc(done, 1)

    def exps(c):
        act.wait_ge(m.s_a_nmax, c + 1)
        lg0, lg1 = logits(m, c)
        for hh in range(GROUP):
            for rb, x in enumerate((lg0[:, hh], lg1[:, hh].rearrange("p b t -> p (b t)"))):
                act.activation(x, x, ACT.Exp, bias=m.a_nm[:, c, rb, hh:hh + 1], accum_out=m.a_sum[:, c, rb, hh:hh + 1]).then_inc(m.s_a_p, 1)

    def probs_copied(c):
        act.wait_ge(m.s_a_ptp, c + 1)
        if c >= 2:
            act.wait_ge(m.s_a_o, c - 1)
        act.activation(m.a_pt[:, c % 2], m.g[:, 0:3, :], ACT.Copy).then_inc(m.s_a_ptc, 1)

    def a_out_high(j):
        act.wait_ge(m.s_a_ptp, min(j + 2, NKV))
        high_unit("a_out", 0, 0, [j])

    exps(0)
    exps(1)
    probs_copied(0)
    exps(2)
    probs_copied(1)
    exps(3)
    probs_copied(2)
    group_high(0, m.s_a_ogt, m.s_a_xh)
    probs_copied(3)
    group_high(1, m.s_a_ogt, m.s_a_xh)
    a_out_high(0)
    group_high(2, m.s_a_ogt, m.s_a_xh)
    a_out_high(1)
    group_high(3, m.s_a_ogt, m.s_a_xh)
    a_out_high(2)
    a_out_high(3)

    def norm_and_embed(name_out, name_ple, layer):
        gemm(name_out, nothing, late=2)
        n = lane.n["T"]
        act.wait_ge(m.s_t_full[n % 2], n // 2 + 1)
        act.activation(m.ple_pt[:], m.t[:, n % 2, :].rearrange("p (k t) -> p k t", k=2), ACT.Copy).then_inc(m.s_t_free[n % 2], 1)
        lane.n["T"] += 1
        std(layer + 1)
        high_unit(name_ple, 0, 0, [2])
        high_columns(0, 2)
        high_unit(name_ple, 0, 0, [3])
        high_columns(4, 6)

        def gate(st, i, k):
            src = product(st, i, k)
            act.activation(m.ple_s[:, k], src, ACT.Sigmoid).then_inc(m.s_g_free[k], 1)

        gemm(name_ple, gate)

    norm_and_embed("a_out", "ple0", 0)
    high_columns(0, 8)
    gemm("b_kvq", keep(m.pb, 0))

    def scores_aside(b):
        if b == KEYS_AT:
            act.wait_ge(m.s_b_k_t, 1)
            act.activation(m.b_kt[:].rearrange("p (a k) t -> p a (k t)", a=2), m.t[:], ACT.Copy).then_inc(m.s_b_k_copied, 1)
        t = b - DOTS_AT
        if 0 <= t < PAIRS:
            act.wait_ge(m.s_b_z, t + 1)
            for hh, bank in enumerate((m.t[:, 1], m.u[:, 1])):
                h = HD * (2 * t + hh)
                act.activation(m.pb[:, :, 1024 + h:1024 + h + HD], bank[:, 0:T].rearrange("p (r e) -> p r e", r=RB), ACT.Copy, scale=HD ** -0.5)\
                   .then_inc(m.s_b_zc, 1)
                act.activation(m.b_z11[:, h:h + HD], bank[:, T:384], ACT.Copy, scale=HD ** -0.5).then_inc(m.s_b_zc, 1)
        t = b - DOTS_AT + 1
        if 0 <= t < PAIRS:
            act.wait_ge(m.s_b_qtp, t + 1)
            act.activation(m.b_qt[:, t % 2], m.t[:, 0, :], ACT.Copy).then_inc(m.s_b_qtc, 1)

    gemm("b_gate", keep(m.pb, 3072, ACT.Silu), late=4, aside=scores_aside)

    def exps_of_magnitudes(cs):
        for c in cs:
            act.wait_ge(m.s_b_abs, 2 * c + 2)
            lane.did(act.activation(m.b_e[:, c], m.b_e[:, c], ACT.Exp))
        lane.sync()

    def logs(cs):
        for c in cs:
            act.activation(m.b_e[:, c], m.b_e[:, c], ACT.Ln, bias=1.0).then_inc(m.s_b_l, 1)

    def weights(c):
        act.wait_ge(m.s_b_a1, c + 1)
        act.activation(m.b_e[:, c], m.b_e[:, c], ACT.Exp).then_inc(m.s_b_ex, 1)

    def next_high(j):
        act.wait_ge(m.s_b_o, min(j + 2, NKV))
        high_unit("b_out", 0, 0, [j])

    exps_of_magnitudes((0, 1))
    logs((0, 1))
    exps_of_magnitudes((2, 3))
    logs((2, 3))
    weights(0)
    weights(1)
    group_high(0, m.s_b_ogt, m.s_b_xh)
    weights(2)
    group_high(1, m.s_b_ogt, m.s_b_xh)
    weights(3)
    next_high(0)
    group_high(2, m.s_b_ogt, m.s_b_xh)
    next_high(1)
    group_high(3, m.s_b_ogt, m.s_b_xh)
    next_high(2)
    next_high(3)
    norm_and_embed("b_out", "ple1", 1)
    std(3)
    high_columns(0, 8)
    act.wait_ge(m.s_res_stored, 16)
    gemm("c_hq", keep(m.pc, 0))
    gemm("c_f", keep(m.pc, 1024, ACT.Sigmoid))
    def bounds(dr):
        act.wait_ge(m.s_h_lb, dr + 1)
        act.activation(m.h_l0[:, dr, 0], m.h_l0[:, dr, 0], ACT.Sigmoid).then_inc(m.s_h_lbs, 1)

    gemm("c_hi", keep(m.pc, 3072))
    bounds(0)
    gemm("c_hg", keep(m.pc, 4096, ACT.Silu))
    bounds(1)
    gemm("c_mla", keep(m.pm, 0), late=2)
    std(4, 2 * RB)
    high_unit("uq", 0, 0, [2])
    high_columns(8, 3)
    high_unit("uq", 0, 0, [3])
    uq, ukv = PLAN["uq"], PLAN["ukv"]
    for j in range(4):
        high(ukv, ukv.v0, ukv.g0, [j])
        act.wait_ge(m.s_w_used, 4 * uq.g0 + 4 + j + 1)
        act.activation(m.mq[:, :, 384 * j:384 * j + 384], m.g[:, 2 * (j % 2):2 * (j % 2) + 2, 0:384], ACT.Copy).then_inc(m.s_g_free[j % 2], 1)
    act.wait_ge(m.s_h_fr, 2)
    for j in range(4):
        act.wait_ge(m.s_w_used, 4 * ukv.g0 + 4 + j + 1)
        act.activation(m.mkv[:, :, 512 * j:512 * j + 512], m.g[:, 2 * (j % 2):2 * (j % 2) + 2, :], ACT.Copy).then_inc(m.s_g_free[j % 2], 1)
        if 1 <= j <= 2:
            act.activation(m.h_lfa[:, j - 1], m.pc[:, j - 1, 1024:3072], ACT.Ln).then_inc(m.s_h_logf, 1)
    act.wait_ge(m.s_m_krt_t, 1)
    act.activation(m.m_krt[:], m.t[:, 0, 0:T], ACT.Copy).then_inc(m.s_m_krt_c, 1)
    mscale = (NOPE + ROPE) ** -0.5

    for c in range(4):
        act.wait_ge(m.s_m_ktp, c + 1)
        act.activation(m.m_ktt[:, 2 * c:2 * c + 2, :], m.g[:, c, :].rearrange("p (h t) -> p h t", h=2), ACT.Copy).then_inc(m.s_m_ktc, 1)

    def m_turn(nxt, cur, prev):
        if nxt:
            n, k, _ = nxt
            act.wait_ge(m.s_m_qtp, n + 3)
            act.activation(m.m_qt[:, k].rearrange("p a t -> p (a t)"), m.g[:, k, :], ACT.Copy).then_inc(m.s_m_qtc, 1)
        if cur:
            t, kc, _ = cur
            act.wait_ge(m.s_m_ptp, t + 1)
            act.activation(m.m_pt[:, kc].rearrange("p a t -> p (a t)"), m.u[:, kc, :], ACT.Copy).then_inc(m.s_m_ptc, 1)
        if prev:
            act.wait_ge(m.s_m_ogt, prev[0] + 1)
            head_high(prev[1], prev[0]).then_inc(m.s_m_xh, 1)
        if nxt:
            act.wait_ge(m.s_m_nmax, n + 1)
            for rb in range(RB):
                act.activation(m.m_lg[:, k, rb], m.g[:, 2 + k, T * rb:T * rb + T], ACT.Exp, scale=mscale, bias=m.m_nm[:, k, rb:rb + 1],
                               accum_out=m.m_sum[:, k, rb:rb + 1]).then_inc(m.s_m_p, 1)

    heads_three_deep(lane, {}, m_turn, MH, 2)
    span_banks = [m.g[:, 2], m.g[:, 3], m.u[:, 0], m.u[:, 1]]

    def decays(n, group, banks=range(4)):
        act.wait_ge(m.s_h_mul, 2 * n + group + 1)
        act.wait_ge(m.s_h_d, 2 * n + group + 5)
        for b in banks:
            act.activation(m.h_e[:, group, b // 2, :, P * (b % 2):P * (b % 2) + P], span_banks[b].rearrange("p (l t) -> p l t", l=4), ACT.Exp)\
               .then_inc(m.s_h_ex, 1)

    def h_turn(nxt, cur, prev):
        if nxt:
            n, k, _ = nxt
            act.wait_ge(m.s_h_tr, n + 1)
            act.activation(m.h_qt[:, k], m.g[:, 0, 0:T], ACT.Copy).then_inc(m.s_h_qc, 1)
            act.activation(m.h_kt[:, k].rearrange("p a t -> p (a t)"), m.g[:, 1, :], ACT.Identity, scale=-1.0, bias=1.0).then_inc(m.s_h_k1, 1)
            decays(n, 0, (0, 1))
        if prev:
            act.wait_ge(m.s_h_o, prev[0] + 1)
            act.activation(m.pc[:, :, bass.ds(HD * prev[0], HD)], m.t[:, 0, 0:T].rearrange("p (r e) -> p r e", r=2), ACT.Copy).then_inc(m.s_h_oc, 1)
        if nxt:
            decays(n, 0, (2, 3))
        if cur:
            act.wait_ge(m.s_h_am, 3 * cur[0] + 1)
            act.activation(m.h_at[:, 1:3, :], m.g[:, 0, T:2 * T].rearrange("p (a t) -> p a t", a=2), ACT.Copy).then_inc(m.s_h_off, 1)
        if nxt:
            decays(n, 1)
        if prev:
            act.wait_ge(m.s_h_oc, prev[0] + 1)
            lane.sync()
            for rb in range(RB):
                lane.did(act.activation(m.h_sq[:, rb], m.pc[:, rb, bass.ds(HD * prev[0], HD)], ACT.Square,
                                        accum_out=m.h_ms[:, rb, bass.ds(prev[0], 1)]))

    heads_three_deep(lane, {"step": 4}, h_turn, HH, 2)
    lane.sync()
    act.activation(m.h_sq[:, 0, 0:1], m.h_sq[:, 0, 0:1], ACT.Copy).then_inc(m.s_h_ms, 1)
    act.wait_ge(m.s_h_ms1, 1)
    act.activation(m.h_r[:], m.h_ms[:], ACT.Sqrt).then_inc(m.s_h_std, 1)
    act.wait_ge(m.s_h_mul, 2 * HH + 2)
    high_unit("c_out", 0, 0, [0, 1])
    high_columns(8, 4)
    high_unit("c_out", 0, 0, [2, 3])
    def scale_plus_one(st, i, k):
        if 2 * i + k == 3:
            act.wait_ge(m.s_gain_rows_landed, 64)
            act.activation(m.x_sc[:], m.x_sc[:], ACT.Identity, bias=1.0).then_inc(m.s_x_scale, 1)

    gemm("c_out", scale_plus_one, late=4)
    std(5)
    for c in range(4):
        act.wait_ge(m.s_x_added, c + 1)
        for rb in range(RB):
            act.activation(m.mix[:, rb, 512 * c:512 * c + 512], m.res[:, rb, 512 * c:512 * c + 512], ACT.Square, accum_out=m.x_sq[:, rb, c:c + 1]).then_inc(m.s_x_sq, 1)
        if c < 2:
            high_unit("mlp", 0, 0, [c])
    std(6)
    high_unit("mlp", 0, 0, [2])
    high_columns(0, 2)
    high_unit("mlp", 0, 0, [3])
    high_columns(4, 6)
    mlp = PLAN["mlp"]

    def mlp_high(q, k, js=range(4)):
        high(mlp, mlp.v0 + 8 * q + k, mlp.g0 + 8 * q + k, js)

    def squares(q, k):
        act.wait_ge(m.s_w_used, 4 * (mlp.g0 + 8 * q + k) + 8)
        lane.did(act.activation(m.ur[:, k % 2], m.g[:, 2 * (k % 2):2 * (k % 2) + 2, :], ACT.Relu))
        act.wait_ge(m.s_act_step, lane.at())
        act.activation(m.ur[:, k % 2], m.ur[:, k % 2], ACT.Square).then_inc(m.s_g_free[k % 2], 1)

    def u_high(q, k):
        for half in range(2):
            b = (mlp_t0 + half) % 2
            act.wait_ge(m.s_t_full[b], (mlp_t0 + half) // 2 + 4 * q + k + 1)
            act.activation(m.uh[:, 4 * k + 2 * half:4 * k + 2 * half + 2, :], m.t[:, b, :].rearrange("p (k t) -> p k t", k=2), ACT.Copy)\
               .then_inc(m.s_x_high_ready, 1)

    mlp_t0 = lane.n["T"]

    def quarter(q, last):
        for k in range(8):
            if k == 4:
                mlp_high(q, 5, (0, 1))
                u_high(q, 3)
                mlp_high(q, 5, (2, 3))
            elif k < 7 or not last:
                mlp_high(q, k + 1)
            if k < 4:
                squares(q, k)
            if 1 <= k <= 3:
                u_high(q, k - 1)

    lane.loop(3, {"step": 4}, lambda q: quarter(q, False))
    quarter(3, True)
    std(7)


def vector_program(nc, dve, m, d):
    lane = Lane(dve, m.s_dve_step)
    stt = dve.scalar_tensor_tensor

    def low(st, v, g, js=range(4), aside=None):
        for j in js:
            dve.wait_ge(m.s_w_high, 4 * g + j + 1)
            s = (slice(None), j, slice(0, st.kq), slice(0, st.width))
            dve.tensor_tensor(m.lo[s], m.raw[s], m.hi[s].bitcast(F32), ALU.subtract).then_inc(m.s_raw_used, 1)
            if aside:
                aside(j)

    def low_unit(name, i, k, js=range(4), aside=None):
        st = PLAN[name]
        low(st, v_of(st, i, k), st.g0 + 2 * i + k, js, aside)

    def mod_piece(st, i):
        n, v = st.m0 + i, v_mod(st, i)
        dve.wait_ge(m.s_mod_summed, n + 1)
        dve.wait_ge(m.s_mod_stored, 16 * n + 16)
        for j in range(4):
            dve.wait_ge(m.s_landed[j], 16 * v + 16)
            for kk in range(4):
                c = 4 * j + kk
                if c == 0:
                    ins = dve.tensor_scalar(m.acc[:], m.raw[:, j, kk, :], m.ct[:, c:c + 1], None, ALU.mult)
                else:
                    ins = stt(m.acc[:], m.raw[:, j, kk, :], m.ct[:, c:c + 1], m.acc[:], ALU.mult, ALU.add)
                if kk < 3:
                    lane.link(ins)
                else:
                    ins.then_inc(m.s_raw_used, 1)
                    if j < 3:
                        dve.wait_ge(m.s_raw_used, 4 * v + j + 5)

    def mod_row(st, i):
        n = st.m0 + i
        dve.wait_ge(m.s_mod_summed, n + 2)
        dve.wait_ge(m.s_brow_landed, 16 * n + 16)
        dve.tensor_tensor(m.acc[0:1, :], m.u[0:1, 0, :], m.brow[:], ALU.add).then_inc(m.s_mod_row, 1)

    def product_done(st, i, k):
        dve.wait_ge(m.s_w_used, 4 * (st.g0 + 2 * i + k) + 8)

    def gemm(name, take=None, next_too=True, late=0, aside=None):
        st = PLAN[name]

        def by(u):
            return aside and (lambda j: aside(4 * u + j))

        def after(i, k):
            if take:
                take(st, i, k)

        def turn(i):
            low_unit(name, i, 1, aside=by(2 * i))
            if st.mods:
                mod_piece(st, i)
            after(i, 0)
            low_unit(name, i, 2, aside=by(2 * i + 1))
            after(i, 1)
            if st.mods:
                mod_row(st, i)

        def tail(i):
            low_unit(name, i, 1, aside=by(2 * i))
            if late:
                after(i, 0)
            if st.mods:
                mod_piece(st, i)
            if not late:
                after(i, 0)
            if next_too:
                low_unit(st.next, 0, 0, range(min(3, 4 - late)), by(2 * i + 1))
            after(i, 1)
            if st.mods:
                mod_row(st, i)
            if next_too and not late:
                low_unit(st.next, 0, 0, [3], by(2 * i + 1))

        gemm_turns(lane, st, {"step": 12} if st.mods else {}, turn, tail, aside)

    def low_columns(k0, uses):
        for q in range(uses):
            n = lane.n["T"]
            dve.wait_ge(m.s_x_high_ready, lane.n["xh"] + 1)
            k = slice(k0 + 2 * q, k0 + 2 * q + 2)
            dve.tensor_tensor(m.xl[:, k, :], m.t[:, n % 2, :].rearrange("p (k t) -> p k t", k=2), m.xh[:, k, :].bitcast(F32), ALU.subtract)\
               .then_inc(m.s_t_free[n % 2], 1)
            lane.n["T"] += 1
            lane.n["xh"] += 1

    def products_kept(name):
        st = PLAN[name]
        used = st.s0 + (4 if st.units == 1 else st.units)
        for b in range(2):
            dve.wait_ge(m.s_g_free[b], used // 2 + 1)

    def rope(x, heads, half, rates, rb, tmp, out=None):
        out = x if out is None else out
        view = [m.cs[:, c, rb, rates:rates + half].unsqueeze(1).unsqueeze(1).broadcast_to((P, heads, 2, half)) for c in range(2)]
        halves = x.rearrange("p h (a e) -> p h a e", a=2)
        by = [tmp[:, c, 0:heads * 2 * half].rearrange("p (h a e) -> p h a e", h=heads, a=2) for c in range(2)]
        for c in range(2):
            lane.did(dve.tensor_tensor(by[c], halves, view[c], ALU.mult))
        lane.sync()
        lane.did(dve.tensor_tensor(out[:, :, 0:half], by[0][:, :, 0, :], by[1][:, :, 1, :], ALU.subtract))
        lane.link(dve.tensor_tensor(out[:, :, half:2 * half], by[1][:, :, 0, :], by[0][:, :, 1, :], ALU.add))

    def inverse_std(n, columns=RB):
        dve.wait_ge(m.s_std_ready, n)
        lane.link(dve.reciprocal(m.rstd[:, 0:columns], m.rstd[:, 0:columns]))

    def spread(n_chunks):
        for rb in range(RB):
            lane.did(dve.bn_aggr(m.mv[:, rb, :], m.st[:, rb, 0:n_chunks, :]))
        lane.sync()

    def mean_square():
        mean, var = m.mv[:, 0:RB, 0], m.mv[:, 0:RB, 1]
        lane.link(dve.tensor_tensor(m.msq[:, 0:RB], mean, mean, ALU.mult))
        stt(m.msq[:, 0:RB], m.msq[:, 0:RB], RMS_EPS, var, ALU.add, ALU.add).then_inc(m.s_var_ready, 1)

    def chunk(c):
        return slice(512 * c, 512 * c + 512)

    lane.n["T"] = 1
    for c in range(4):
        low_columns(4 * c, 2)
        low_unit("a_idx", 0, 0, [c])
    dve.wait_ge(m.s_pos_landed, 48)
    lane.link(dve.tensor_copy(m.posf[:], m.posi[:]))
    na = ROT_A + ROT_I
    for rb in range(RB):
        lane.did(dve.tensor_scalar(m.ang[:, rb, 0:na], m.rot[:, 0:na], m.posf[:, rb:rb + 1], None, ALU.mult))
        lane.did(dve.tensor_scalar(m.ang[:, rb, na:], m.rot[:, na:], m.posf[:, RB + rb:RB + rb + 1], None, ALU.mult))
    lane.sync()
    lane.link(dve.tensor_scalar(m.turns[:], m.ang[:], 0.15915494309189535, ROUND, ALU.mult, ALU.add))
    lane.link(dve.tensor_scalar(m.turns[:], m.turns[:], ROUND, None, ALU.subtract))
    for part in (TWO_PI_HI, TWO_PI_MID, TWO_PI_LO):
        lane.link(stt(m.ang[:], m.turns[:], -part, m.ang[:], ALU.mult, ALU.add))
    lane.link(dve.tensor_scalar(m.ang[:], m.ang[:], -3.1415925, 3.1415925, ALU.max, ALU.min))
    lane.link(stt(m.turns[:], m.ang[:], -1.0, m.ang[:], ALU.mult, ALU.max))
    dve.tensor_scalar(m.turns[:], m.turns[:], -1.0, 1.5707963267948966, ALU.mult, ALU.add).then_inc(m.s_angles_ready, 1)
    gemm("a_idx")

    products_kept("a_idx")
    dve.wait_ge(m.s_sin_ready, 2)
    for rb in range(RB):
        rope(m.pa[:, rb, 5120:5120 + (IDX_H + 1) * IDX_D].rearrange("p (h e) -> p h e", e=IDX_D)[:, :, 0:2 * ROT_I], IDX_H + 1, ROT_I, ROT_A, rb, m.a_rope)
    dve.memset(m.a_bias0[:, P:T], 0.0)
    dve.tensor_copy(m.a_bias0[:, 0:P], m.tri)
    lane.link(dve.tensor_copy(m.a_bias0[:, T:384], m.tri))
    dve.tensor_copy(m.a_score[:], m.a_bias0[:]).then_inc(m.s_a_ready, 1)
    dve.wait_ge(m.s_a_ready, 1)
    blocks = (slice(0, P), slice(P, 384))

    def index_aside(b):
        t, k = b - DOTS_AT, (b - DOTS_AT) % 2
        if 0 <= t < IDX_PAIRS:
            dve.wait_ge(m.s_a_relu, 2 * t + 2)
            for hh in range(2):
                for rb in range(RB):
                    s = m.a_score[:, blocks[rb]]
                    ins = stt(s, m.a_rl[:, k, hh, blocks[rb]], m.a_iws[:, k, rb, hh:hh + 1], s, ALU.mult, ALU.add)
                    if (hh, rb) != (1, 1):
                        lane.did(ins)
                if hh == 0:
                    lane.sync()
            ins.then_inc(m.s_a_idx_done, 1)
            dve.wait_ge(m.s_a_idx_done, t + 3)
        if BEST_AT <= b < BEST_AT + ROUNDS:
            for rb in range(RB):
                lane.did(dve.max(m.a_top[:, rb, :], m.a_score[:, blocks[rb]]))
            lane.sync()
            for rb in range(RB):
                lane.did(dve.match_replace(m.a_score[:, blocks[rb]], m.a_top[:, rb, :], m.a_score[:, blocks[rb]], TAKEN))
            lane.sync()
        if b == BEST_AT + ROUNDS:
            lane.link(dve.tensor_scalar(m.a_bias[:], m.a_score[:], -2e38, NEG, ALU.is_gt, ALU.mult))
            lane.link(dve.tensor_tensor(m.a_bias[:], m.a_bias[:], m.a_bias0[:], ALU.add))

    gemm("a_qkv", aside=index_aside)
    products_kept("a_qkv")
    for rb in range(RB):
        rope(m.pa[:, rb, 0:(NH + NKV) * HD].rearrange("p (h e) -> p h e", e=HD)[:, :, 0:2 * ROT_A], NH + NKV, ROT_A, 0, rb, m.a_rope)
    dve.memset(m.a_nm[:], 0.0).then_inc(m.s_a_roped, 1)
    dve.wait_ge(m.s_a_roped, 1)
    gemm("a_gate", late=4)
    products_kept("a_gate")

    def head_low(bank, h):
        xl, xh = (x[:, bass.ds(h, 1), :].rearrange("p k t -> p (k t)") for x in (m.xl, m.xh))
        return dve.tensor_tensor(xl, m.t[:, bank, T:2 * T], xh.bitcast(F32), ALU.subtract)

    def group_low(c, high_ready, done):
        dve.wait_ge(high_ready, c + 1)
        xl, xh = (x[:, GROUP * c:GROUP * c + GROUP, :].rearrange("p (a k) t -> p a (k t)", a=2) for x in (m.xl, m.xh))
        dve.tensor_tensor(xl, m.pairs[c % 2][:], xh.bitcast(F32), ALU.subtract).then_inc(done, 1)

    def biased(c):
        w = GROUP * HD
        lg0, lg1 = logits(m, c)
        for out, z, b in ((lg0, m.pa[:, 0, w * c:w * c + w], 0), (lg1[:, :, 0], m.pa[:, 1, w * c:w * c + w], P),
                          (lg1[:, :, 1], m.a_z11[:, w * c:w * c + w], T)):
            lane.did(dve.tensor_tensor(out, z.rearrange("p (h t) -> p h t", h=GROUP),
                                       m.a_bias[:, b:b + P].unsqueeze(1).broadcast_to((P, GROUP, P)), ALU.add))
        lane.sync()
        lane.did(dve.tensor_reduce(m.a_nm[:, c, 0], lg0, AXX, ALU.max, negate=True))
        dve.tensor_reduce(m.a_nm[:, c, 1], lg1.rearrange("p h b t -> p h (b t)"), AXX, ALU.max, negate=True).then_inc(m.s_a_nmax, 1)

    def a_gated(c):
        dve.wait_ge(m.s_a_p, 2 * GROUP * (c + 1))
        lane.link(dve.reciprocal(m.a_rs[:, c], m.a_sum[:, c]))
        dve.wait_ge(m.s_a_o, c + 1)
        for hh in range(GROUP):
            h, g = slice(HD * hh, HD * hh + HD), 3072 + HD * (GROUP * c + hh)
            for rb in range(RB):
                ins = stt(m.a_og[:, c % 2, rb, h], m.pairs[c % 2][:, rb, h], m.a_rs[:, c, rb, hh:hh + 1], m.pa[:, rb, g:g + HD], ALU.mult, ALU.mult)
                if (hh, rb) != (GROUP - 1, RB - 1):
                    lane.did(ins)
        ins.then_inc(m.s_a_ogr, 1)

    dve.wait_ge(m.s_a_zc, 4 * PAIRS)
    biased(0)
    biased(1)
    biased(2)
    biased(3)
    a_gated(0)
    a_gated(1)
    group_low(0, m.s_a_xh, m.s_a_done)
    a_gated(2)
    group_low(1, m.s_a_xh, m.s_a_done)
    low_unit("a_out", 0, 0, [0])
    a_gated(3)
    group_low(2, m.s_a_xh, m.s_a_done)
    group_low(3, m.s_a_xh, m.s_a_done)
    low_unit("a_out", 0, 0, [1, 2, 3])

    def norm_and_embed(name_out, name_ple, layer):
        dve.wait_ge(m.s_x_landed, 32)

        def add(st, i, k):
            u, s = 2 * i + k, st.s0 // 2 + i
            product_done(st, i, k)
            stt(m.res[:, :, chunk(u)], m.res[:, :, chunk(u)], ALPHA, m.g[:, 2 * k:2 * k + 2, :], ALU.mult, ALU.add).then_inc(m.s_g_free[k], 1)
            dve.wait_ge(m.s_g_free[k], s + 2)
            for rb in range(RB):
                lane.did(dve.bn_stats(m.st[:, rb, u, :], m.res[:, rb, chunk(u)]))

        gemm(name_out, add, late=4)
        lane.sync()
        spread(4)
        dve.tensor_scalar(m.msq[:, 0:RB], m.mv[:, 0:RB, 1], LN_EPS, None, ALU.add).then_inc(m.s_var_ready, 1)
        lane.n["T"] += 1
        low_unit(name_ple, 0, 0, [0])
        dve.wait_ge(m.s_rows_landed, 32 * (layer + 1))
        inverse_std(layer + 1)
        for c in range(4):
            x = [m.res[:, rb, chunk(c)] for rb in range(RB)]
            for rb in range(RB):
                lane.did(stt(x[rb], x[rb], m.mv[:, rb, 0:1], m.row_g[:, chunk(c)], ALU.subtract, ALU.mult))
            lane.sync()
            for rb in range(RB):
                stt(x[rb], x[rb], m.rstd[:, rb:rb + 1], m.row_b[:, chunk(c)], ALU.mult, ALU.add).then_inc(m.s_y_ready, 1)
                lane.n["y"] += 1
            if c < 3:
                low_unit(name_ple, 0, 0, [c + 1])
            low_columns(4 * c, 2)
        dve.wait_ge(m.s_y_ready, lane.n["y"])

        def embed(st, i, k):
            u, s = 2 * i + k, st.s0 // 2 + i
            product_done(st, i, k)
            x = m.res[:, :, chunk(u)]
            if (layer, u) == (1, 2):
                dve.wait_ge(m.s_rows2_landed, 48)
                lane.did(stt(m.c_g1[:], m.c_sc[:], 1.0, m.c_g1[:], ALU.add, ALU.mult))
            dve.wait_ge(m.s_g_free[k], s + 2)
            dve.wait_ge(m.s_ple_full, 4 * layer + u + 1)
            dve.tensor_tensor(m.ple_s[:, k], m.ple_s[:, k], m.u[:], ALU.mult).then_inc(m.s_ple_free, 1)
            dve.wait_ge(m.s_ple_free, 4 * layer + u + 2)
            ins = dve.tensor_tensor(x, x, m.ple_s[:, k], ALU.add)
            if layer == 0:
                ins.then_inc(m.s_y_ready, 1)
                lane.n["y"] += 1
            else:
                ins.then_inc(m.s_x4_ready, 1)
                dve.wait_ge(m.s_x4_ready, u + 1)
                for rb in range(RB):
                    lane.did(dve.bn_stats(m.st[:, rb, u, :], m.res[:, rb, chunk(u)]))

        gemm(name_ple, embed, late=layer)

    norm_and_embed("a_out", "ple0", 0)
    low_columns(0, 8)
    gemm("b_kvq")
    gemm("b_gate", late=4)

    products_kept("b_gate")

    def masked_diagonal(x):
        x = x[:, 0:3:2, :].rearrange("p b (h t) -> p b h t", h=GROUP)
        return dve.tensor_tensor(x, x, m.lt.unsqueeze(1).unsqueeze(1).broadcast_to((P, 2, GROUP, P)), ALU.mult)

    def softplus(c):
        dve.wait_ge(m.s_b_l, c + 1)
        z, e = scores(m, c), (m.b_e[:, c, 0:2], m.b_e[:, c, 2])
        for n, sp in enumerate((m.b_sp[:, c, 0:2], m.b_sp[:, c, 2])):
            lane.did(stt(sp, z[n], 0.0, e[n], ALU.max, ALU.add))
        lane.sync()
        masked_diagonal(m.b_sp[:, c]).then_inc(m.s_b_spr, 1)
        for n in range(2):
            lane.did(stt(e[n], z[n], 0.0, e[n], ALU.min, ALU.subtract))

    def less_later(c):
        dve.wait_ge(m.s_b_sfx, c + 1)
        lane.sync()
        dve.tensor_tensor(m.b_e[:, c], m.b_e[:, c], m.g[:, 0:3, :], ALU.subtract).then_inc(m.s_b_a1, 1)

    def weights(c):
        dve.wait_ge(m.s_b_ex, c + 1)
        masked_diagonal(m.b_e[:, c]).then_inc(m.s_b_w, 1)

    def gate_group(c):
        dve.wait_ge(m.s_b_o, c + 1)
        g = 3072 + GROUP * HD * c
        dve.tensor_tensor(m.b_og[:, c % 2], m.pairs[c % 2][:], m.pb[:, :, g:g + GROUP * HD], ALU.mult).then_inc(m.s_b_ogr, 1)

    dve.wait_ge(m.s_b_zc, 4 * PAIRS)
    for c in range(NKV):
        for e, z in zip((m.b_e[:, c, 0:2], m.b_e[:, c, 2]), scores(m, c)):
            stt(e, z, -1.0, z, ALU.mult, ALU.min).then_inc(m.s_b_abs, 1)
    softplus(0)
    softplus(1)
    less_later(0)
    weights(0)
    less_later(1)
    softplus(2)
    gate_group(0)
    weights(1)
    less_later(2)
    softplus(3)
    group_low(0, m.s_b_xh, m.s_b_done)
    gate_group(1)
    weights(2)
    less_later(3)
    group_low(1, m.s_b_xh, m.s_b_done)
    gate_group(2)
    weights(3)
    low_unit("b_out", 0, 0, [0])
    group_low(2, m.s_b_xh, m.s_b_done)
    gate_group(3)
    low_unit("b_out", 0, 0, [1])
    group_low(3, m.s_b_xh, m.s_b_done)
    low_unit("b_out", 0, 0, [2, 3])
    norm_and_embed("b_out", "ple1", 1)

    def normed(x, gain, shift, out, following, left):
        for c in range(4):
            for rb in range(RB):
                lane.did(stt(out[:, rb, chunk(c)], x[:, rb, chunk(c)], m.rstd[:, rb:rb + 1], gain[:, chunk(c)], ALU.mult, ALU.mult))
            lane.sync()
            o = out[:, :, chunk(c)]
            dve.tensor_tensor(o, o, shift[:, chunk(c)].unsqueeze(1).broadcast_to((P, RB, 512)), ALU.add).then_inc(m.s_y_ready, 1)
            lane.n["y"] += 1
            if c < len(left):
                low_unit(following, 0, 0, [left[c]])
            low_columns(4 * c, 2)

    lane.sync()
    spread(4)
    mean_square()
    inverse_std(3)
    normed(m.res, m.c_g1, m.c_sh, m.c_h, "c_hq", [3])
    def forget_gates(dr):
        products_kept("c_f")
        dve.wait_ge(m.s_h_rows, 64)
        bound = m.h_l0[:, dr, 0]
        dve.tensor_tensor(bound, bound, m.h_l0[:, dr, 1], ALU.subtract).then_inc(m.s_h_lb, 1)
        f = m.pc[:, :, 1024 * (dr + 1):1024 * (dr + 2)]
        lane.link(dve.tensor_scalar(m.h_t[:], f, -1.0, 1.0, ALU.mult, ALU.add))
        dve.wait_ge(m.s_h_lbs, dr + 1)
        lane.link(dve.tensor_tensor(m.h_t[:], m.h_t[:], bound.unsqueeze(1).broadcast_to((P, RB, 1024)), ALU.mult))
        dve.tensor_tensor(f, f, m.h_t[:], ALU.add).then_inc(m.s_h_fr, 1)
        dve.wait_ge(m.s_h_fr, dr + 1)

    gemm("c_hq")
    gemm("c_f")
    gemm("c_hi")
    forget_gates(0)
    gemm("c_hg")
    forget_gates(1)
    gemm("c_mla", late=4)

    products_kept("c_mla")
    parts = ((slice(0, QRANK), 0), (slice(QRANK, QRANK + KVRANK), RB))
    for s, n in parts:
        for rb in range(RB):
            lane.did(dve.bn_stats(m.st[:, rb, n // RB, :], m.pm[:, rb, s]))
    lane.sync()
    for s, n in parts:
        for rb in range(RB):
            lane.did(dve.bn_aggr(m.mv[:, n + rb, :], m.st[:, rb, n // RB:n // RB + 1, :]))
    lane.sync()
    lane.link(dve.tensor_tensor(m.msq[:], m.mv[:, :, 0], m.mv[:, :, 0], ALU.mult))
    stt(m.msq[:], m.msq[:], RMS_EPS, m.mv[:, :, 1], ALU.add, ALU.add).then_inc(m.s_var_ready, 1)
    low_unit("uq", 0, 0, [0])
    dve.wait_ge(m.s_rows2_landed, 80)
    inverse_std(4, 2 * RB)
    for s, n in parts:
        for rb in range(RB):
            ins = stt(m.pm[:, rb, s], m.pm[:, rb, s], m.rstd[:, n + rb:n + rb + 1], m.m_rg[:, s], ALU.mult, ALU.mult)
            if n + rb < 2 * RB - 1:
                lane.did(ins)
    ins.then_inc(m.s_y_ready, 1)
    lane.n["y"] += 1
    dve.wait_ge(m.s_mod_stored, 16 * (PLAN["c_mla"].m0 + 1) + 16)
    lane.link(dve.memset(m.m_krd[:], 0.0))
    for rb in range(RB):
        rope(m.pm[:, rb:rb + 1, QRANK + KVRANK:], 1, ROT_M, na, rb, m.m_rope, m.m_krd[:, rb:rb + 1, 0:ROPE])
    low_columns(8, 3)
    low_unit("uq", 0, 0, [1, 2, 3])
    ukv = PLAN["ukv"]
    low(ukv, ukv.v0, ukv.g0)
    products_kept("uq")
    dve.wait_ge(m.s_raw_used, 4 * ukv.v0 + 8)
    for rb in range(RB):
        rope(m.mq[:, rb, :].rearrange("p (h e) -> p h e", e=NOPE + ROPE)[:, :, NOPE:], MH, ROT_M, na, rb, m.m_rope2)
    products_kept("ukv")
    dve.memset(m.m_nm[:], 0.0).then_inc(m.s_m_ready, 1)
    dve.wait_ge(m.s_m_ready, 1)
    mscale = (NOPE + ROPE) ** -0.5

    def m_turn(nxt, cur, prev):
        if prev:
            dve.wait_ge(m.s_m_xh, prev[0] + 1)
            head_low(prev[1], prev[0]).then_inc(m.s_m_done, 1)
        if nxt:
            n, k, _ = nxt
            dve.wait_ge(m.s_m_s, n + 1)
            lane.link(dve.tensor_reduce(m.m_nm[:, k], m.g[:, 2 + k, :].rearrange("p (r s) -> p r s", r=RB), AXX, ALU.max, negate=True))
            dve.tensor_scalar(m.m_nm[:, k], m.m_nm[:, k], mscale, None, ALU.mult).then_inc(m.s_m_nmax, 1)
        if cur:
            t, kc, _ = cur
            dve.wait_ge(m.s_m_p, 2 * t + 2)
            lane.link(dve.reciprocal(m.m_rs[:, kc], m.m_sum[:, kc]))
            dve.wait_ge(m.s_m_o, t + 1)
            for rb in range(RB):
                ins = dve.tensor_scalar(m.m_og[:, rb], m.t[:, kc, P * rb:P * rb + P], m.m_rs[:, kc, rb:rb + 1], None, ALU.mult)
                if rb == 0:
                    lane.did(ins)
            ins.then_inc(m.s_m_ogr, 1)

    heads_three_deep(lane, {"step": 6}, m_turn, MH, 2)
    dve.wait_ge(m.s_h_consts, 48)

    def decayed(k, group):
        for l in range(4):
            half = P >> (4 * group + l)

            def side(ap, s):
                return ap.rearrange("p (b s h) -> p b s h", s=2, h=half)[:, :, s, :]

            e = [m.h_e[:, group, dr, l] for dr in range(2)]
            for s in range(2):
                lane.did(dve.tensor_tensor(side(m.h_kq[:, group, 0, l], s), side(m.h_kt[:, k, s], s), side(e[s], s), ALU.mult))
                ins = dve.tensor_tensor(side(m.h_kq[:, group, 1, l], s), side(m.h_qt[:, k], s), side(e[1 - s], s), ALU.mult)
                if (l, s) != (3, 1):
                    lane.did(ins)
        ins.then_inc(m.s_h_mul, 1)

    def masked(levels, n0):
        n = len(levels)
        return dve.tensor_tensor(m.h_tm[:, :, n0:n0 + n, :], m.t[:, :, 0:P * n].rearrange("p b (l t) -> p b l t", l=n),
                                 m.h_mask[:, n0:n0 + n, :].unsqueeze(1).broadcast_to((P, RB, n, P)), ALU.mult)

    def h_turn(nxt, cur, prev):
        if nxt:
            n, k, _ = nxt
            dve.wait_ge(m.s_h_k1, n + 1)
            dve.tensor_tensor(m.h_ks[:, k], m.h_kt[:, k, 0], m.h_kt[:, k, 1], ALU.add).then_inc(m.s_h_kc, 1)
        if cur:
            t = cur[0]
            dve.wait_ge(m.s_h_am, 3 * t + 1)
            masked(range(3), 0).then_inc(m.s_h_msk, 1)
        if nxt:
            dve.wait_ge(m.s_h_qc, n + 1)
            dve.wait_ge(m.s_h_ex, 8 * n + 4)
            decayed(k, 0)
        if cur:
            dve.wait_ge(m.s_h_am, 3 * t + 3)
            dve.tensor_tensor(m.h_tm[:, :, 7, :], m.g[:, 1, 0:T].rearrange("p (b t) -> p b t", b=RB),
                              m.h_mask[:, 7:8, :].broadcast_to((P, RB, P)), ALU.mult).then_inc(m.s_h_dg, 1)
            lane.link(masked(range(4), 3))
            dve.wait_ge(m.s_h_dg, t + 1)
            if prev:
                dve.wait_ge(m.s_h_o, prev[0] + 1)
            lane.did(dve.tensor_reduce(m.h_at[:, 0], m.h_tm[:, 0].rearrange("p l t -> p t l"), AXX, ALU.add))
            dve.tensor_reduce(m.h_at[:, 3], m.h_tm[:, 1].rearrange("p l t -> p t l"), AXX, ALU.add).then_inc(m.s_h_red, 1)
        if nxt:
            dve.wait_ge(m.s_h_ex, 8 * n + 8)
            decayed(k, 1)

    heads_three_deep(lane, {"step": 64}, h_turn, HH, 2)
    dve.wait_ge(m.s_h_ms, 1)
    o = m.pc[:, :, 0:1024]
    dve.tensor_scalar(m.h_ms[:], m.h_ms[:], 1.0 / HD, RMS_EPS, ALU.mult, ALU.add).then_inc(m.s_h_ms1, 1)
    low_unit("c_out", 0, 0, [0])
    dve.wait_ge(m.s_h_std, 1)
    lane.link(dve.reciprocal(m.h_r[:], m.h_r[:]))
    for rb in range(RB):
        heads = o[:, rb].rearrange("p (h e) -> p h e", h=HH)
        lane.did(dve.tensor_tensor(heads, heads, m.h_r[:, rb].unsqueeze(2).broadcast_to((P, HH, HD)), ALU.mult))
    lane.sync()
    dve.wait_ge(m.s_h_gain, RB)
    dve.tensor_tensor(o, o, m.pc[:, :, 4096:5120], ALU.mult).then_inc(m.s_y_ready, 1)
    lane.n["y"] += 1
    low_unit("c_out", 0, 0, [1])
    low_columns(8, 4)

    low_unit("c_out", 0, 0, [2, 3])

    def keep_mix(st, i, k):
        u, s = 2 * i + k, st.s0 // 2 + i
        product_done(st, i, k)
        dve.tensor_copy(m.mix[:, :, chunk(u)], m.g[:, 2 * k:2 * k + 2, :]).then_inc(m.s_g_free[k], 1)
        dve.wait_ge(m.s_g_free[k], s + 2)
        for rb in range(RB):
            lane.did(dve.bn_stats(m.st[:, rb, u, :], m.mix[:, rb, chunk(u)]))

    def into_residual(y, gain, done):
        for c in range(4):
            for rb in range(RB):
                lane.did(stt(y[:, rb, chunk(c)], y[:, rb, chunk(c)], m.rstd[:, rb:rb + 1], gain[:, chunk(c)], ALU.mult, ALU.mult))
            lane.sync()
            ins = dve.tensor_tensor(m.res[:, :, chunk(c)], m.res[:, :, chunk(c)], y[:, :, chunk(c)], ALU.add)
            ins.then_inc(done, 1)

    gemm("c_out", keep_mix, late=4)
    lane.sync()
    spread(4)
    mean_square()
    dve.wait_ge(m.s_res2_landed, 16)
    inverse_std(5)
    dve.wait_ge(m.s_x_gains, 1)
    into_residual(m.mix, m.x_pg, m.s_x_added)
    low_unit("mlp", 0, 0, [0])
    dve.wait_ge(m.s_x_sq, 2 * 4)
    lane.link(dve.tensor_reduce(m.msq[:, 0:RB], m.x_sq[:], AXX, ALU.add))
    dve.tensor_scalar(m.msq[:, 0:RB], m.msq[:, 0:RB], 1.0 / D, RMS_EPS, ALU.mult, ALU.add).then_inc(m.s_var_ready, 1)
    inverse_std(6)
    dve.wait_ge(m.s_x_gains, 2)
    dve.wait_ge(m.s_rows2_landed, 96)
    normed(m.res, m.x_g1, m.x_sh, m.mix, "mlp", [1, 2, 3])

    lane.link(dve.memset(m.y[:], 0.0))
    mlp = PLAN["mlp"]
    t0, x0 = lane.n["T"], lane.n["xh"]

    def hidden_low(q, k):
        for half in range(2):
            b = (t0 + half) % 2
            dve.wait_ge(m.s_x_high_ready, x0 + 8 * q + 2 * k + half + 1)
            s = slice(4 * k + 2 * half, 4 * k + 2 * half + 2)
            dve.tensor_tensor(m.ul[:, s, :], m.t[:, b, :].rearrange("p (k t) -> p k t", k=2), m.uh[:, s, :].bitcast(F32), ALU.subtract)\
               .then_inc(m.s_t_free[b], 1)

    def hidden_quarter(q, last):
        for k in range(8):
            if k == 4:
                low(mlp, mlp.v0 + 8 * q + 5, mlp.g0 + 8 * q + 5, (0, 1))
                hidden_low(q, 3)
                low(mlp, mlp.v0 + 8 * q + 5, mlp.g0 + 8 * q + 5, (2, 3))
            elif k < 7 or not last:
                low(mlp, mlp.v0 + 8 * q + k + 1, mlp.g0 + 8 * q + k + 1)
            if 1 <= k <= 3:
                hidden_low(q, k - 1)
            if k >= 4:
                if last and k == 7:
                    dve.wait_ge(m.s_rows2_landed, 128)
                    lane.link(dve.tensor_tensor(m.z_pg[:], m.z_pg[:], m.z_gm[:], ALU.mult))
                    for c in range(3):
                        gain_chunk(c)
                dve.wait_ge(m.s_w_used, 4 * (mlp.g0 + 8 * q + k) + 8)
                y = m.y[:, :, chunk(k - 4)]
                dve.tensor_tensor(y, y, m.g[:, 2 * (k % 2):2 * (k % 2) + 2, :], ALU.add).then_inc(m.s_g_free[k % 2], 1)
                if last:
                    dve.wait_ge(m.s_g_free[k % 2], mlp.s0 // 2 + 4 * q + k // 2 + 2)
                    for rb in range(RB):
                        lane.did(dve.bn_stats(m.st[:, rb, k - 4, :], m.y[:, rb, chunk(k - 4)]))
    def gain_chunk(c):
        y = m.y[:, :, chunk(c)]
        lane.did(dve.tensor_tensor(y, y, m.z_pg[:, chunk(c)].unsqueeze(1).broadcast_to((P, RB, 512)), ALU.mult))

    lane.loop(3, {}, lambda q: hidden_quarter(q, False))
    hidden_quarter(3, True)
    lane.sync()
    spread(4)
    mean_square()
    gain_chunk(3)
    inverse_std(7)
    for c in range(4):
        for rb in range(RB):
            x = m.res[:, rb, chunk(c)]
            stt(x, m.y[:, rb, chunk(c)], m.rstd[:, rb:rb + 1], x, ALU.mult, ALU.add).then_inc(m.s_mlp_done, 1)


def tensor_program(nc, pe, m, d):
    lane = Lane(pe, m.s_pe_step)

    def quarter(st, v, g, j, pair, x0, first, last, xh=m.xh, xl=m.xl):
        pe.wait_ge(m.s_raw_used, 4 * v + j + 5)
        for kk in range(st.kq):
            for rb in range(RB):
                a, w = slice(P * rb, P * rb + P), (j, kk, slice(0, st.width))
                bank = m.g[:, 2 * pair + rb, 0:st.width]
                parts = ((xh, m.hi), (xh, m.lo), (xl, m.hi))
                for n, (x, wt) in enumerate(parts):
                    ins = pe.matmul(bank, x[:, x0 + kk, a], wt[(slice(None),) + w],
                                    start=first and kk == 0 and n == 0, stop=last and kk == st.kq - 1 and n == 2)
        ins.then_inc(m.s_w_used, 1)

    def unit(st, v, g, half_s, pair, xh=m.xh, xl=m.xl, aside=None):
        pe.wait_ge(m.s_g_free[pair], half_s + 1)
        for j in range(4):
            quarter(st, v, g, j, pair, 4 * j, j == 0, j == 3, xh, xl)
            if aside:
                aside(j)

    def gemm(name, after=None, first=None, aside=None):
        st = PLAN[name]

        def pair(i, first=None):
            for k in range(2):
                if first and k == 0:
                    first(st)
                else:
                    unit(st, v_of(st, i, k), st.g0 + 2 * i + k, st.s0 // 2 + i, k, aside=aside and (lambda j: aside(4 * (2 * i + k) + j)))
                if after:
                    after(2 * i + k)
            if st.mods:
                pe.wait_ge(m.s_raw_used, 4 * v_mod(st, i) + 8)
                pe.matmul(m.u[0:1, 0, :], m.ones[:, 0:1], m.acc[:], start=True, stop=True).then_inc(m.s_mod_summed, 1)

        if aside:
            for i in range(st.units // 2):
                pair(i)
        elif first:
            pair(0, first)
            lane.loop(st.units // 2 - 1, {}, pair, 1)
        else:
            lane.loop(st.units // 2, {}, pair)

    def bank_for_columns():
        n = lane.n["T"]
        pe.wait_ge(m.s_t_free[n % 2], n // 2 + 1)
        lane.n["T"] += 1
        return n % 2

    def blocks(b, src):
        for kt in range(2):
            for rb in range(RB):
                ins = pe.transpose(m.t[:, b, T * kt + P * rb:T * kt + P * rb + P], src(kt, rb), m.ident)
        ins.then_inc(m.s_t_full[b], 1)

    def columns(x, uses, y_total=0, per_chunk=0):
        base = lane.n["y"]
        for q in range(uses):
            if per_chunk:
                pe.wait_ge(m.s_y_ready, base + per_chunk * (q // 2 + 1))
            b = bank_for_columns()
            blocks(b, lambda kt, rb: x[:, rb, T * q + P * kt:T * q + P * kt + P])
        lane.n["y"] += y_total

    def arriving(x, y_total, per_chunk):
        def go(st):
            n, y = lane.n["T"], lane.n["y"]
            pe.wait_ge(m.s_g_free[0], st.s0 // 2 + 1)

            def product(j):
                for b in range(2):
                    pe.wait_ge(m.s_t_free[b], (n + 2 * j + 2 + 1 - b) // 2 + 1)
                quarter(st, st.v0, st.g0, j, 0, 4 * j, j == 0, j == 3)

            for c in range(4):
                if per_chunk:
                    pe.wait_ge(m.s_y_ready, y + per_chunk * (c + 1))
                for q in (2 * c, 2 * c + 1):
                    blocks(bank_for_columns(), lambda kt, rb: x[:, rb, T * q + P * kt:T * q + P * kt + P])
                if c:
                    product(c - 1)
            product(3)
            lane.n["y"] += y_total
        return go

    def columns_split():
        n = lane.n["T"]
        for b in range(2):
            pe.wait_ge(m.s_t_free[b], (n + 1 - b) // 2 + 1)

    def pieces(dst, src, n, sem):
        for a in range(n):
            ins = pe.transpose(dst(a), src(a), m.ident)
        ins.then_inc(sem, 1)

    pe.wait_ge(m.s_const_landed, 32)
    b = bank_for_columns()
    pe.transpose(m.t[:, b, 0:KT], m.crow[:], m.const[0:KT, C_IDENT:C_IDENT + KT]).then_inc(m.s_t_full[b], 1)
    pe.wait_ge(m.s_x_landed, 16)
    gemm("a_idx", None, arriving(m.res, 0, 0))

    def keys(src, col0, banks):
        for kv in range(NKV):
            for rb in range(RB):
                c = T * (kv % 2) + P * rb
                ins = pe.transpose(banks[:, kv // 2, c:c + P], src[:, rb, col0 + HD * kv:col0 + HD * kv + HD], m.ident)
        return ins

    def index_aside(b):
        if b == KEYS_AT:
            pe.wait_ge(m.s_a_ready, 1)
            pe.wait_ge(m.s_a_k_t, 2)
            pieces(lambda rb: m.u[:, 1, P * rb:P * rb + P], lambda rb: m.a_ikd[:, rb].rearrange("p a e -> p (a e)"), RB, m.s_a_ktp)
        t = b - DOTS_AT
        if 0 <= t < IDX_PAIRS:
            pe.wait_ge(m.s_a_iqc, t + 1)
            if t:
                pe.wait_ge(m.s_a_relu, 2 * t)
            for hh, bank in enumerate((m.t[:, 1], m.u[:, 1])):
                e = slice(IDX_D * hh, IDX_D * hh + IDX_D)
                pe.matmul(bank[:, 0:P], m.a_iqt[e, t % 2, 0:P], m.a_ikt[e, 0:P], start=True, stop=True)
                ins = pe.matmul(bank[:, P:384], m.a_iqt[e, t % 2, P:T], m.a_ikt[e, :], start=True, stop=True)
            ins.then_inc(m.s_a_dots, 1)
        t = b - DOTS_AT + 1
        if 0 <= t < IDX_PAIRS:
            pe.wait_ge(m.s_a_iq, 2 * t + 2)
            if t == 0:
                pe.wait_ge(m.s_a_k_copied, 1)
            pieces(lambda rb: m.t[:, 0, P * rb:P * rb + P], lambda rb: m.a_iqs[:, t % 2, rb], RB, m.s_a_iqt)

    gemm("a_qkv", aside=index_aside)

    def a_scores_aside(b):
        if b == KEYS_AT:
            pe.wait_ge(m.s_a_relu, 2 * IDX_PAIRS)
            pe.wait_ge(m.s_a_roped, 1)
            keys(m.pa, 2048, m.t).then_inc(m.s_a_ktp, 1)
        t = b - DOTS_AT
        if 0 <= t < PAIRS:
            pe.wait_ge(m.s_a_qtc, t + 1)
            if t:
                pe.wait_ge(m.s_a_zc, 4 * t)
            for hh, bank in enumerate((m.t[:, 1], m.u[:, 1])):
                kv, q = (2 * t + hh) // GROUP, m.a_qt[:, t % 2, T * hh:T * hh + T]
                pe.matmul(bank[:, 0:P], q[:, 0:P], m.a_kt[:, kv, 0:P], start=True, stop=True)
                ins = pe.matmul(bank[:, P:384], q[:, P:T], m.a_kt[:, kv, :], start=True, stop=True)
            ins.then_inc(m.s_a_z, 1)
        t = b - DOTS_AT + 1
        if 0 <= t < PAIRS:
            if t == 0:
                pe.wait_ge(m.s_a_k_copied, 2)
            query_pieces(m.pa, 0, t, m.s_a_qtp)

    def query_pieces(proj, q0, t, transposed):
        def src(a):
            q = q0 + HD * (2 * t + a // 2)
            return proj[:, a % 2, q:q + HD]

        pieces(lambda a: m.t[:, 0, P * a:P * a + P], src, 4, transposed)

    gemm("a_gate", aside=a_scores_aside)
    gate = PLAN["a_gate"]
    for b in range(2):
        pe.wait_ge(m.s_g_free[b], (gate.s0 + gate.units) // 2 + 1)

    def probs_transposed(c):
        pe.wait_ge(m.s_a_p, 2 * GROUP * (c + 1))
        if c:
            pe.wait_ge(m.s_a_ptc, c)
        lg0, lg1 = logits(m, c)
        blocks_of = [lambda hh: lg0[:, hh], lambda hh: lg1[:, hh, 0], lambda hh: lg1[:, hh, 1]]
        pieces(lambda a: m.g[:, a // GROUP, P * (a % GROUP):P * (a % GROUP) + P],
               lambda a: blocks_of[a // GROUP](a % GROUP), 3 * GROUP, m.s_a_ptp)

    def attend_group(c, probs, v, ready, split, done):
        pe.wait_ge(ready, c + 1)
        if c >= 2:
            pe.wait_ge(split, c - 1)
        banks = m.pairs[c % 2]
        for hh in range(GROUP):
            h = slice(HD * hh, HD * hh + HD)
            pe.matmul(banks[:, 0, h], probs[:, 0, h], v[0], start=True, stop=True)
            pe.matmul(banks[:, 1, h], probs[:, 1, h], v[0], start=True, stop=False)
            ins = pe.matmul(banks[:, 1, h], probs[:, 2, h], v[1], start=False, stop=True)
        ins.then_inc(done, 1)

    def group_columns(c, og, gated, transposed):
        pe.wait_ge(gated, c + 1)
        pieces(lambda a: m.pairs[c % 2][:, a // 4, P * (a % 4):P * (a % 4) + P],
               lambda a: og[:, c % 2, a % 2, HD * (a // 2):HD * (a // 2) + HD], 2 * GROUP, transposed)

    def a_attend(c):
        v = [m.pa[:, s, 2560 + HD * c:2560 + HD * c + HD] for s in range(RB)]
        attend_group(c, m.a_pt[:, c % 2], v, m.s_a_ptc, m.s_a_done, m.s_a_o)

    def a_columns(c):
        group_columns(c, m.a_og, m.s_a_ogr, m.s_a_ogt)

    probs_transposed(0)
    probs_transposed(1)
    a_attend(0)
    probs_transposed(2)
    a_attend(1)
    a_columns(0)
    probs_transposed(3)
    a_attend(2)
    a_columns(1)
    a_attend(3)
    a_columns(2)
    a_columns(3)
    pe.wait_ge(m.s_a_done, NKV)

    def norm_and_embed(name_out, name_ple, layer):
        gemm(name_out)
        pe.wait_ge(m.s_ple_landed, 32 * (layer + 1))
        blocks(bank_for_columns(), lambda kt, rb: m.ple_p[:, rb, P * kt:P * kt + P])

        def embed(u):
            pe.wait_ge(m.s_ple_free, 4 * layer + u + 1)
            for rb in range(RB):
                for k in range(2):
                    ins = pe.matmul(m.u[:, rb, :], m.ple_pt[:, k, P * rb:P * rb + P], m.ple_w[:, k, bass.ds(512 * u, 512)],
                                    start=k == 0, stop=k == 1)
            ins.then_inc(m.s_ple_full, 1)

        gemm(name_ple, embed, arriving(m.res, 8, 2))

    norm_and_embed("a_out", "ple0", 0)
    gemm("b_kvq", None, arriving(m.res, 4, 1))

    kvq = PLAN["b_kvq"]

    def scores_aside(b):
        if b == KEYS_AT:
            for k in range(2):
                pe.wait_ge(m.s_g_free[k], (kvq.s0 + kvq.units) // 2 + 1)
            columns_split()
            keys(m.pb, 0, m.t).then_inc(m.s_b_k_t, 1)
        t = b - DOTS_AT
        if 0 <= t < PAIRS:
            pe.wait_ge(m.s_b_qtc, t + 1)
            if t:
                pe.wait_ge(m.s_b_zc, 4 * t)
            for hh, bank in enumerate((m.t[:, 1], m.u[:, 1])):
                kv, q = (2 * t + hh) // GROUP, m.b_qt[:, t % 2, T * hh:T * hh + T]
                pe.matmul(bank[:, 0:T], m.b_kt[:, kv, 0:P], q, start=True, stop=True)
                ins = pe.matmul(bank[:, T:384], m.b_kt[:, kv, P:T], q[:, P:T], start=True, stop=True)
            ins.then_inc(m.s_b_z, 1)
        t = b - DOTS_AT + 1
        if 0 <= t < PAIRS:
            if t == 0:
                pe.wait_ge(m.s_b_k_copied, 1)
            query_pieces(m.pb, 1024, t, m.s_b_qtp)

    gemm("b_gate", aside=scores_aside)
    gate = PLAN["b_gate"]
    for k in range(2):
        pe.wait_ge(m.s_g_free[k], (gate.s0 + gate.units) // 2 + 1)

    def later_sums(c):
        pe.wait_ge(m.s_b_spr, c + 1)
        if c:
            pe.wait_ge(m.s_b_a1, c)
        for n in (0, 2):
            pe.matmul(m.g[:, n], m.gt, m.b_sp[:, c, n], start=True, stop=True)
        pe.matmul(m.g[:, 1], m.gt, m.b_sp[:, c, 1], start=True, stop=False)
        pe.matmul(m.g[:, 1], m.ones, m.b_sp[:, c, 2], start=False, stop=True).then_inc(m.s_b_sfx, 1)

    def b_attend(c):
        v = [m.pb[:, s, 512 + HD * c:512 + HD * c + HD] for s in range(RB)]
        attend_group(c, m.b_e[:, c], v, m.s_b_w, m.s_b_done, m.s_b_o)

    def b_columns(c):
        group_columns(c, m.b_og, m.s_b_ogr, m.s_b_ogt)

    later_sums(0)
    later_sums(1)
    b_attend(0)
    later_sums(2)
    b_attend(1)
    b_columns(0)
    later_sums(3)
    b_attend(2)
    b_columns(1)
    b_attend(3)
    b_columns(2)
    b_columns(3)
    pe.wait_ge(m.s_b_done, NKV)
    norm_and_embed("b_out", "ple1", 1)
    gemm("c_hq", None, arriving(m.c_h, 4, 1))
    for name in ("c_f", "c_hi", "c_hg", "c_mla"):
        gemm(name)
    pe.wait_ge(m.s_y_ready, lane.n["y"] + 1)
    columns(m.pm, 3, 1)
    columns_split()
    for name, x0 in (("uq", 8), ("ukv", 12)):
        st = PLAN[name]
        for j in range(4):
            pe.wait_ge(m.s_g_free[j % 2], (st.s0 + j) // 2 + 1)
            quarter(st, st.v0, st.g0, j, j % 2, x0, True, True)
    pe.wait_ge(m.s_m_ready, 1)
    pieces(lambda rb: m.t[:, 0, P * rb:P * rb + P], lambda rb: m.m_krd[:, rb], RB, m.s_m_krt_t)
    pe.wait_ge(m.s_m_krt_c, 1)
    for h in range(MH):
        for rb in range(RB):
            c = T * (h % 2) + P * rb
            ins = pe.transpose(m.g[:, h // 2, c:c + P], m.mkv[:, rb, (NOPE + VD) * h:(NOPE + VD) * h + NOPE], m.ident)
        if h % 2:
            ins.then_inc(m.s_m_ktp, 1)
    pe.wait_ge(m.s_m_ktc, 4)

    def m_turn(nxt, cur, prev):
        if nxt:
            n, k, _ = nxt
            pe.wait_ge(m.s_m_q, n + 1)
            pieces(lambda a: m.g[:, k, P * a:P * a + P], lambda a: m.m_qs[:, k, a % 2, P * (a // 2):P * (a // 2) + P], 4, m.s_m_qtp)
        if cur:
            t, kc, _ = cur
            pe.wait_ge(m.s_m_p, 2 * t + 2)
            pieces(lambda a: m.u[:, kc, P * a:P * a + P], lambda a: m.m_lg[:, kc, a // 2, P * (a % 2):P * (a % 2) + P], 4, m.s_m_ptp)
        if prev:
            pt, kp, _ = prev
            pe.wait_ge(m.s_m_ogr, pt + 1)
            pe.wait_ge(m.s_m_done, pt + 1)
            pieces(lambda rb: m.t[:, kp, T + P * rb:T + P * rb + P], lambda rb: m.m_og[:, rb], RB, m.s_m_ogt)
        if nxt:
            pe.wait_ge(m.s_m_qtc, n + 1)
            keys_t = m.m_ktt[:, bass.ds(n, 1), :].rearrange("p h t -> p (h t)")
            for rb in range(RB):
                rows_, out = slice(P * rb, P * rb + P), m.g[:, 2 + k, T * rb:T * rb + T]
                pe.matmul(out, m.m_qt[:, k, 0, rows_], keys_t, start=True, stop=False)
                ins = pe.matmul(out, m.m_qt[:, k, 1, rows_], m.m_krt[:], start=False, stop=True)
            ins.then_inc(m.s_m_s, 1)
        if cur:
            pe.wait_ge(m.s_m_ptc, t + 1)
            for rb in range(RB):
                for s in range(RB):
                    ins = pe.matmul(m.t[:, kc, P * rb:P * rb + P], m.m_pt[:, kc, rb, P * s:P * s + P],
                                    m.mkv[:, s, bass.ds((NOPE + VD) * t + NOPE, VD)], start=s == 0, stop=s == 1)
            ins.then_inc(m.s_m_o, 1)

    heads_three_deep(lane, {}, m_turn, MH, 2)
    pe.wait_ge(m.s_m_done, MH + 2)
    pe.wait_ge(m.s_h_consts, 48)

    def spans(k, group):
        for dr in range(2):
            for blk, bank in enumerate(((m.g[:, 2], m.g[:, 3]), (m.u[:, 0], m.u[:, 1]))[dr]):
                lf = m.h_lf[:, k, dr, blk, :]
                if group:
                    ins = pe.matmul(bank, lf, m.h_md[:, dr, 5:9, :].rearrange("p l t -> p (l t)"), start=True, stop=True)
                elif blk == 0:
                    ins = pe.matmul(bank, lf, m.h_md[:, dr, 0:4, :].rearrange("p l t -> p (l t)"), start=True, stop=True)
                else:
                    pe.matmul(bank[:, 0:P], lf, m.h_md[:, dr, 4, :], start=True, stop=True)
                    ins = pe.matmul(bank[:, P:512], lf, m.h_md[:, dr, 1:4, :].rearrange("p l t -> p (l t)"), start=True, stop=True)
        ins.then_inc(m.s_h_d, 1)

    def block_products(group, levels):
        for blk in range(RB):
            b = slice(P * blk, P * blk + P)
            for n, l in enumerate(levels):
                ins = pe.matmul(m.t[:, blk, P * n:P * n + P], m.h_kq[:, group, 0, l, b], m.h_kq[:, group, 1, l, b], start=True, stop=True)
        ins.then_inc(m.s_h_am, 1)

    def h_turn(nxt, cur, prev):
        if nxt:
            n, k, _ = nxt
            pe.wait_ge(m.s_h_q, 5 * n + 3)
            if cur:
                pe.wait_ge(m.s_h_qc, cur[0] + 1)
                pe.wait_ge(m.s_h_kc, cur[0] + 1)
            if prev:
                pe.wait_ge(m.s_h_off, prev[0] + 1)
                pe.wait_ge(m.s_h_dg, prev[0] + 1)
            for rb in range(RB):
                pe.transpose(m.g[:, 0, P * rb:P * rb + P], m.h_qs[:, k, rb], m.ident)
            pieces(lambda a: m.g[:, 1, P * a:P * a + P], lambda a: m.h_fs[:, k, a // 2, a % 2], 4, m.s_h_tr)
            pe.wait_ge(m.s_h_q, 5 * n + 5)
            if cur:
                pe.wait_ge(m.s_h_ex, 8 * cur[0] + 8)
            spans(k, 0)
        if prev:
            pe.wait_ge(m.s_h_red, prev[0] + 1)
            pe.wait_ge(m.s_h_off, prev[0] + 1)
            for blk in range(RB):
                for s in range(RB):
                    ins = pe.matmul(m.t[:, 0, P * blk:P * blk + P], m.h_at[:, 2 * s + blk, :], m.pc[:, s, bass.ds(3072 + HD * prev[0], HD)],
                                    start=s == 0, stop=s == 1)
            ins.then_inc(m.s_h_o, 1)
        if cur:
            t, kc, _ = cur
            pe.wait_ge(m.s_h_mul, 2 * t + 3)
            if nxt:
                pe.wait_ge(m.s_h_qc, n + 1)
            if prev:
                pe.wait_ge(m.s_h_oc, prev[0] + 1)
            pe.matmul(m.g[:, 0, T:T + P], m.h_kq[:, 0, 0, 0, 0:P], m.h_kq[:, 0, 1, 0, P:T], start=True, stop=True)
            pe.matmul(m.g[:, 0, T + P:2 * T], m.h_kq[:, 0, 0, 0, P:T], m.h_kq[:, 0, 1, 0, 0:P], start=True, stop=True)
            block_products(0, range(1, 4))
        if nxt:
            pe.wait_ge(m.s_h_ex, 8 * n + 4)
            spans(k, 1)
        if cur:
            pe.wait_ge(m.s_h_mul, 2 * t + 4)
            pe.wait_ge(m.s_h_msk, t + 1)
            block_products(1, range(4))
            if nxt:
                pe.wait_ge(m.s_h_kc, n + 1)
            for blk in range(RB):
                b = slice(P * blk, P * blk + P)
                ins = pe.matmul(m.g[:, 1, b], m.h_ks[:, kc, b], m.h_qt[:, kc, b], start=True, stop=True)
            ins.then_inc(m.s_h_am, 1)

    heads_three_deep(lane, {}, h_turn, HH, 2)
    pe.wait_ge(m.s_h_oc, HH)

    def mixed(st):
        pe.wait_ge(m.s_g_free[0], st.s0 // 2 + 1)
        quarter(st, st.v0, st.g0, 0, 0, 0, True, False)
        pe.wait_ge(m.s_y_ready, lane.n["y"] + 1)
        columns(m.pc, 4, 1)
        quarter(st, st.v0, st.g0, 1, 0, 4, False, False)
        columns_split()
        for j in (2, 3):
            quarter(st, st.v0, st.g0, j, 0, 4 * j, False, j == 3)

    gemm("c_out", None, mixed)
    mlp = PLAN["mlp"]
    first = arriving(m.mix, 4, 1)
    t0 = lane.n["T"] + 8

    def hidden_columns(q, k):
        pe.wait_ge(m.s_g_free[k % 2], mlp.s0 // 2 + 4 * q + k // 2 + 2)
        for half in range(2):
            b = (t0 + half) % 2
            pe.wait_ge(m.s_t_free[b], (t0 + half) // 2 + 4 * q + k + 1)
            blocks(b, lambda kt, rb: m.ur[:, k % 2, rb, T * half + P * kt:T * half + P * kt + P])

    def hidden_quarter(q, first=None):
        for k in range(8):
            xs = (m.xh, m.xl) if k < 4 else (m.uh, m.ul)
            if first and k == 0:
                first(mlp)
            elif k == 4:
                pe.wait_ge(m.s_g_free[0], mlp.s0 // 2 + 4 * q + 3)
                for j in range(4):
                    if j == 2:
                        hidden_columns(q, 3)
                    for half in range(2):
                        pe.wait_ge(m.s_t_free[(t0 + half) % 2], (t0 + half) // 2 + 4 * q + j + 2)
                    quarter(mlp, mlp.v0 + 8 * q + 4, mlp.g0 + 8 * q + 4, j, 0, 4 * j, j == 0, j == 3, m.uh, m.ul)
            else:
                unit(mlp, mlp.v0 + 8 * q + k, mlp.g0 + 8 * q + k, mlp.s0 // 2 + 4 * q + k // 2, k % 2, *xs)
            if 1 <= k <= 3:
                hidden_columns(q, k - 1)

    hidden_quarter(0, first)
    lane.loop(3, {}, hidden_quarter, 1)


def shape_constants():
    import numpy as np

    i = np.arange(P)
    s, t = i[:, None], i[None, :]
    const = np.concatenate([np.eye(P), np.ones((P, P)), np.where(t <= s, 0.0, NEG), s < t, s > t], axis=1)

    def inverse(base, half):
        return 1.0 / np.float32(base) ** (np.arange(half, dtype=np.float32) / np.float32(half))

    rates = np.tile(np.concatenate([inverse(500000.0, ROT_A), inverse(500000.0, ROT_I), inverse(10000.0, ROT_M)]), (P, 1))
    tau, spans = s, np.zeros((P, 2, 9, P))

    def span(mid, right):
        fwd = np.where(right, (mid <= tau) & (tau <= t), (t < tau) & (tau < mid))
        bwd = np.where(right, (mid <= tau) & (tau < t), (t <= tau) & (tau < mid))
        return fwd, bwd

    def level(l):
        half = P >> l
        return span(t // (2 * half) * (2 * half) + half, t % (2 * half) >= half)

    order = [span(P, np.zeros((1, P), bool))] + [level(l) for l in range(1, 4)]
    order += [span(0, np.ones((1, P), bool))] + [level(l) for l in range(4, LEVELS)]
    for n, pair in enumerate(order):
        for dr in range(2):
            spans[:, dr, n] = pair[dr]
    masks = [(s // (P >> l) // 2 == t // (P >> l) // 2) & (s // (P >> l) != t // (P >> l)) for l in range(1, LEVELS)]
    masks = np.stack(masks + [s == t], axis=1)
    out = {"consts": const, "rates": rates, "spans": spans.reshape(P, -1), "level_masks": masks.reshape(P, -1)}
    return {k: np.ascontiguousarray(v, dtype=np.float32) for k, v in out.items()}


def program(nc, arrays):
    import numpy as np

    a = {}
    for name, x in arrays.items():
        a[name] = nc.dram_tensor(f"in_{name}", x.shape, mybir.dt.from_np(np.dtype(x.dtype)), kind="ExternalInput").ap()
    out = nc.dram_tensor("out", (1, T, D), F32, kind="ExternalOutput").ap()
    d = Names()
    d.x = a["x"][0]
    d.p = a["p"][:, 0]
    d.positions = a["positions"]
    d.positions_2 = a["positions_2"]
    d.w_in_a = a["w_in_a"][0]
    d.w_o_a = a["w_o_a"][0]
    d.w_kv_b = a["w_kv_b"]
    d.w_in_b = a["w_in_b"][0]
    d.w_o_b = a["w_o_b"][0]
    d.ln_g = a["ln_g"]
    d.ln_b = a["ln_b"]
    d.w_ple = a["w_ple"]
    d.w_g0 = a["w_ple_gate"][0]
    d.w_g1 = a["w_ple_gate"][1]
    d.c = a["c_2"]
    d.w_mod = a["w_mod_2"][0]
    d.b_mod = a["b_mod_2"][0]
    d.pre_mix_g = a["pre_mix_g_2"][0]
    d.post_mix_g = a["post_mix_g_2"][0]
    d.pre_mlp_g = a["pre_mlp_g_2"][0]
    d.post_mlp_g = a["post_mlp_g_2"][0]
    d.w_in_c = a["w_in_2"][0]
    d.q_norm_g = a["q_norm_g_2"][0]
    d.kv_norm_g = a["kv_norm_g_2"][0]
    d.w_uq = a["w_uq_2"][0]
    d.w_ukv = a["w_ukv_2"][0]
    d.hgrn_g = a["hgrn_norm_g_2"][0]
    d.lb_f = a["hgrn_lb_logits_fwd_2"]
    d.lb_b = a["hgrn_lb_logits_bwd_2"]
    d.w_out = a["w_out_2"][0]
    d.w_up = a["w_up_2"][0]
    d.w_down = a["w_down_2"][0]
    d.consts = a["consts"]
    d.rates = a["rates"]
    d.spans = a["spans"]
    d.level_masks = a["level_masks"]
    build(nc, d, out[0])


def kernel(**inputs):
    import concourse.bacc as bacc
    import numpy as np
    from concourse.bass_utils import run_bass_kernel_spmd

    arrays = {k: np.ascontiguousarray(v) for k, v in inputs.items()}
    arrays.update(shape_constants())
    nc = bacc.Bacc("TRN2", target_bir_lowering=False, num_devices=1)
    program(nc, arrays)
    r = run_bass_kernel_spmd(nc, [{f"in_{k}": v for k, v in arrays.items()}], core_ids=[0])
    return r.results[0]["out"]
```
